# Optimizing a Trainium2 kernel written in Bass

```python
import jax
import jax.numpy as jnp
from jax import lax
import numpy as np
import jax, jax.numpy as jnp

D_MODEL = 1024
BATCH = 1
SEQ = 256
DEPTH = 1

D_MIX = D_MODEL
GLA_HEADS = 4
GLA_DV = (D_MIX // 2) // GLA_HEADS
GLA_DK = GLA_DV // 2
GLA_LOWRANK = 16
GLA_TAU = 16.0
GLA_CHUNK = 16
ATT_HEADS = 8
ATT_HD = (D_MIX - GLA_HEADS * GLA_DV) // ATT_HEADS
DILATIONS = ((128, 1), (512, 4), (2048, 16))
ATT_BLOCK = 128
N_GROUPS = 4
EXPERTS_PER_GROUP = 8
N_EXPERTS = N_GROUPS * EXPERTS_PER_GROUP
TOP_K = 2
D_FF_EXPERT = 512
MOE_BLOCK = 128
EPS = 1e-6

GLA_QK = GLA_HEADS * GLA_DK
GLA_V = GLA_HEADS * GLA_DV
ATT_W = ATT_HEADS * ATT_HD
IN_SIZES = (GLA_QK, GLA_QK, GLA_V, GLA_V, GLA_LOWRANK, ATT_W, ATT_W, ATT_W)
IN_SPLITS = tuple(sum(IN_SIZES[:i + 1]) for i in range(len(IN_SIZES) - 1))
IN_COLS = sum(IN_SIZES)


def rmsnorm(x, g):
    xf = x.astype(jnp.float32)
    y = xf * lax.rsqrt(jnp.mean(xf * xf, axis=-1, keepdims=True) + EPS)
    return (y * g.astype(jnp.float32)).astype(x.dtype)

def gla_chunked(q, k, v, log_a):
    B, T, H, DK = q.shape
    DV = v.shape[-1]
    C = GLA_CHUNK
    N = T // C

    def chunks(t):
        return t.astype(jnp.float32).reshape(B, N, C, H, t.shape[-1]).transpose(0, 3, 1, 2, 4)

    q = chunks(q) * (DK ** -0.5)
    k, v, la = chunks(k), chunks(v), chunks(log_a)
    G = jnp.cumsum(la, axis=3)
    causal = jnp.tril(jnp.ones((C, C), dtype=bool))[:, :, None]
    diff = G[:, :, :, :, None, :] - G[:, :, :, None, :, :]
    decay = jnp.where(causal, jnp.exp(jnp.where(causal, diff, 0.0)), 0.0)
    A = jnp.einsum('bhnid,bhnjd,bhnijd->bhnij', q, k, decay)
    o_intra = jnp.einsum('bhnij,bhnjv->bhniv', A, v)
    G_last = G[:, :, :, -1:, :]
    U = jnp.einsum('bhncd,bhncv->bhndv', k * jnp.exp(G_last - G), v)
    a_chunk = jnp.exp(G_last[:, :, :, 0, :])

    def step(S, inp):
        a, u = inp
        return a[..., None] * S + u, S

    S0 = jnp.zeros((B, H, DK, DV), jnp.float32)
    _, S_prev = lax.scan(step, S0, (jnp.moveaxis(a_chunk, 2, 0), jnp.moveaxis(U, 2, 0)))
    S_prev = jnp.moveaxis(S_prev, 0, 2)
    o_inter = jnp.einsum('bhncd,bhndv->bhncv', q * jnp.exp(G), S_prev)
    o = o_intra + o_inter
    return o.transpose(0, 2, 3, 1, 4).reshape(B, T, H, DV)

def dilated_branch(q, k, v, window, dilation):
    B, H, T, D = q.shape
    d = dilation
    L = T // d
    n_back = window // d
    P = ATT_BLOCK
    nb = -(-L // P)
    Lp = nb * P

    def phase(t):
        t = t.reshape(B, H, L, d, D).transpose(0, 1, 3, 2, 4)
        t = jnp.pad(t, ((0, 0), (0, 0), (0, 0), (0, Lp - L), (0, 0)))
        return t.reshape(B, H, d, nb, P, D)

    def with_prev(t):
        prev = jnp.concatenate([jnp.zeros_like(t[:, :, :, :1]), t[:, :, :, :-1]], axis=3)
        return jnp.concatenate([prev, t], axis=4)

    qb = phase(q)
    kb, vb = with_prev(phase(k)), with_prev(phase(v))
    s = jnp.einsum('bhrnqd,bhrnkd->bhrnqk', qb, kb) * (D ** -0.5)
    blk = jnp.arange(nb)[:, None, None]
    qpos = jnp.arange(P)[None, :, None] + P
    kpos = jnp.arange(2 * P)[None, None, :]
    dist = qpos - kpos
    valid = (dist >= 0) & (dist <= n_back) & (blk * P + kpos - P >= 0)
    s = jnp.where(valid, s, -jnp.inf)
    m = jnp.max(s, axis=-1)
    p = jnp.exp(s - m[..., None])
    den = jnp.sum(p, axis=-1)
    o = jnp.einsum('bhrnqk,bhrnkd->bhrnqd', p, vb) / den[..., None]

    def unphase(t):
        rest = t.shape[5:]
        t = t.reshape((B, H, d, Lp) + rest)[:, :, :, :L]
        t = jnp.moveaxis(t, 2, 3)
        return t.reshape((B, H, T) + rest)

    return unphase(o), unphase(m), unphase(den)

def hybrid_mixer(n, w_in, gla_gate_w2, gla_gate_b, gla_norm_g, w_out):
    B, T, _ = n.shape
    proj = n @ w_in
    gq, gk, gv, gr, glr, aq, ak, av = jnp.split(proj, IN_SPLITS, axis=-1)
    log_a = jax.nn.log_sigmoid((glr @ gla_gate_w2 + gla_gate_b).astype(jnp.float32)) / GLA_TAU
    heads = lambda t: t.reshape(B, T, GLA_HEADS, -1)
    o_gla = gla_chunked(heads(gq), heads(gk), heads(gv), heads(log_a))
    o_gla = o_gla * lax.rsqrt(jnp.mean(o_gla * o_gla, axis=-1, keepdims=True) + EPS) * gla_norm_g.astype(jnp.float32)
    o_gla = o_gla.reshape(B, T, GLA_V) * jax.nn.silu(gr.astype(jnp.float32))
    to_bhtd = lambda t: t.astype(jnp.float32).reshape(B, T, ATT_HEADS, ATT_HD).transpose(0, 2, 1, 3)
    q, k, v = to_bhtd(aq), to_bhtd(ak), to_bhtd(av)
    branches = [dilated_branch(q, k, v, w, d) for (w, d) in DILATIONS]
    o_all = jnp.stack([br[0] for br in branches])
    m_all = jnp.stack([br[1] for br in branches])
    den_all = jnp.stack([br[2] for br in branches])
    wts = den_all * jnp.exp(m_all - jnp.max(m_all, axis=0, keepdims=True))
    o_att = jnp.sum(wts[..., None] * o_all, axis=0) / jnp.sum(wts, axis=0)[..., None]
    o_att = o_att.transpose(0, 2, 1, 3).reshape(B, T, ATT_W)
    o = jnp.concatenate([o_gla, o_att], axis=-1).astype(n.dtype)
    return o @ w_out

def hier_moe(n, w_grp, b_grp, w_exp, b_exp, w1, w3, w2):
    B, T, D = n.shape
    M = B * T
    x = n.reshape(M, D)
    g_logits = (x @ w_grp).astype(jnp.float32) + b_grp.astype(jnp.float32)
    g_idx = jnp.argmax(g_logits, axis=-1).astype(jnp.int32)
    g_prob = jnp.take_along_axis(jax.nn.softmax(g_logits, axis=-1), g_idx[:, None], axis=-1)
    e_logits = ((x @ w_exp).astype(jnp.float32) + b_exp.astype(jnp.float32)).reshape(M, N_GROUPS, EXPERTS_PER_GROUP)
    e_logits = jnp.take_along_axis(e_logits, g_idx[:, None, None], axis=1)[:, 0]
    top_v, top_i = lax.top_k(e_logits, TOP_K)
    gate = jax.nn.softmax(top_v, axis=-1) * g_prob
    expert_id = g_idx[:, None] * EXPERTS_PER_GROUP + top_i.astype(jnp.int32)
    A = M * TOP_K
    e_flat = expert_id.reshape(A)
    tok_flat = jnp.repeat(jnp.arange(M, dtype=jnp.int32), TOP_K)
    order = jnp.argsort(e_flat)
    e_s, tok_s, w_s = e_flat[order], tok_flat[order], gate.reshape(A)[order]
    counts = jnp.bincount(e_flat, length=N_EXPERTS)
    start = jnp.cumsum(counts) - counts
    padded = (counts + MOE_BLOCK - 1) // MOE_BLOCK * MOE_BLOCK
    p_end = jnp.cumsum(padded)
    dest = (p_end - padded)[e_s] + jnp.arange(A) - start[e_s]
    R = (-(-A // MOE_BLOCK) + N_EXPERTS) * MOE_BLOCK
    n_blk = R // MOE_BLOCK
    row_tok = jnp.zeros((R,), jnp.int32).at[dest].set(tok_s)
    row_w = jnp.zeros((R,), jnp.float32).at[dest].set(w_s)
    blk_exp = jnp.minimum(jnp.searchsorted(p_end, jnp.arange(n_blk) * MOE_BLOCK, side='right'), N_EXPERTS - 1)

    def expert_block(args):
        toks, e = args
        xb = x[toks]
        hb = jax.nn.silu(xb @ w1[e]) * (xb @ w3[e])
        return hb @ w2[e]

    y = lax.map(expert_block, (row_tok.reshape(n_blk, MOE_BLOCK), blk_exp))
    y = y.reshape(R, D).astype(jnp.float32) * row_w[:, None]
    out = jnp.zeros((M, D), jnp.float32).at[row_tok].add(y)
    return out.astype(n.dtype).reshape(B, T, D)

def first_inputs(seed: int = 0) -> dict:
    key = jax.random.key(seed)
    ks = jax.random.split(key, 17)
    nrm = jax.random.normal
    f = jnp.float32
    return {
        'x': nrm(ks[0], (BATCH, SEQ, D_MODEL), f),
        'norm1_g': 1.0 + 0.02 * nrm(ks[1], (DEPTH, D_MODEL), f),
        'w_in': nrm(ks[2], (DEPTH, D_MODEL, IN_COLS), f) * D_MODEL ** -0.5,
        'gla_gate_w2': nrm(ks[3], (DEPTH, GLA_LOWRANK, GLA_QK), f) * GLA_LOWRANK ** -0.5,
        'gla_gate_b': 0.1 * nrm(ks[4], (DEPTH, GLA_QK), f),
        'gla_norm_g': 1.0 + 0.02 * nrm(ks[5], (DEPTH, GLA_DV), f),
        'w_out': nrm(ks[6], (DEPTH, D_MIX, D_MODEL), f) * D_MIX ** -0.5,
        'norm2_g': 1.0 + 0.02 * nrm(ks[7], (DEPTH, D_MODEL), f),
        'router_group_w': nrm(ks[8], (DEPTH, D_MODEL, N_GROUPS), f) * D_MODEL ** -0.5,
        'router_group_b': 0.01 * nrm(ks[9], (DEPTH, N_GROUPS), f),
        'router_expert_w': nrm(ks[10], (DEPTH, D_MODEL, N_EXPERTS), f) * D_MODEL ** -0.5,
        'router_expert_b': 0.01 * nrm(ks[11], (DEPTH, N_EXPERTS), f),
        'expert_w1': nrm(ks[12], (DEPTH, N_EXPERTS, D_MODEL, D_FF_EXPERT), f) * D_MODEL ** -0.5,
        'expert_w3': nrm(ks[13], (DEPTH, N_EXPERTS, D_MODEL, D_FF_EXPERT), f) * D_MODEL ** -0.5,
        'expert_w2': nrm(ks[14], (DEPTH, N_EXPERTS, D_FF_EXPERT, D_MODEL), f) * D_FF_EXPERT ** -0.5,
        'final_norm_g': 1.0 + 0.02 * nrm(ks[15], (D_MODEL,), f),
    }

def first_block(x, norm1_g, w_in, gla_gate_w2, gla_gate_b, gla_norm_g, w_out, norm2_g,
              router_group_w, router_group_b, router_expert_w, router_expert_b,
              expert_w1, expert_w3, expert_w2, final_norm_g):
    h = x
    for l in range(DEPTH):
        h = h + hybrid_mixer(rmsnorm(h, norm1_g[l]), w_in[l], gla_gate_w2[l], gla_gate_b[l],
                             gla_norm_g[l], w_out[l])
        h = h + hier_moe(rmsnorm(h, norm2_g[l]), router_group_w[l], router_group_b[l],
                         router_expert_w[l], router_expert_b[l],
                         expert_w1[l], expert_w3[l], expert_w2[l])
    return rmsnorm(h, final_norm_g)


DEPTH_2 = 2

CHUNK = 64
N_MEM = 256
D_MIX_2 = D_MODEL
D_A = D_MIX_2 // 2
D_B = D_MIX_2 - D_A
HGRN_KDIM = 128
HGRN_HEADS = D_A // HGRN_KDIM
HGRN_VDIM = D_A // HGRN_HEADS
POOL_WINDOWS = (2, 4, 8, 16)
POOL_GROUPS = len(POOL_WINDOWS)
POOL_CH = D_B // POOL_GROUPS
D_IN = 4 * D_A + D_B
D_FF = ((8 * D_MODEL // 3) + 127) // 128 * 128
XA_HEADS = 4
XA_HEAD_DIM = D_MODEL // XA_HEADS


def rmsnorm_2(x, g):
    xf = x.astype(jnp.float32)
    y = xf * lax.rsqrt(jnp.mean(xf * xf, axis=-1, keepdims=True) + EPS)
    return (y * g.astype(jnp.float32)).astype(x.dtype)

def swiglu(h, w1, w3, w2):
    return (jax.nn.silu(h @ w1) * (h @ w3)) @ w2

def hgrn2_chunkwise(q, k, v, log_f):
    B, T, H, K = q.shape
    V = v.shape[-1]
    nc = T // CHUNK

    def to_chunks(a):
        return a.reshape(B, nc, CHUNK, H, a.shape[-1]).transpose(1, 0, 3, 2, 4)

    causal = jnp.tril(jnp.ones((CHUNK, CHUNK), dtype=bool))[:, :, None]

    def step(S, inp):
        qc, kc, vc, gc = inp
        b = jnp.cumsum(gc, axis=2)
        o_inter = jnp.einsum('bhtk,bhkv->bhtv', qc * jnp.exp(b), S)
        rel = b[:, :, :, None, :] - b[:, :, None, :, :]
        decay = jnp.exp(jnp.where(causal, rel, -jnp.inf))
        A = jnp.einsum('bhtk,bhsk,bhtsk->bhts', qc, kc, decay)
        o = o_inter + jnp.einsum('bhts,bhsv->bhtv', A, vc)
        b_last = b[:, :, -1:, :]
        S = jnp.exp(b_last[:, :, 0, :, None]) * S + jnp.einsum(
            'bhsk,bhsv->bhkv', kc * jnp.exp(b_last - b), vc)
        return S, o

    S0 = jnp.zeros((B, H, K, V), jnp.float32)
    _, o = lax.scan(step, S0, (to_chunks(q), to_chunks(k), to_chunks(v), to_chunks(log_f)))
    return o.transpose(1, 0, 3, 2, 4).reshape(B, T, H, V)

def hgrn2_mixer(q_in, f_in, i_in, g_in, lb, norm_g):
    B, T, _ = q_in.shape
    shp = (B, T, HGRN_HEADS, HGRN_KDIM)
    q = q_in.astype(jnp.float32).reshape(shp)
    z = f_in.astype(jnp.float32).reshape(shp)
    lbh = lb.reshape(HGRN_HEADS, HGRN_KDIM)
    log_f = jnp.logaddexp(jnp.log(lbh), jnp.log1p(-lbh) + jax.nn.log_sigmoid(z))
    k = (1.0 - lbh) * jax.nn.sigmoid(-z)
    v = i_in.astype(jnp.float32).reshape(B, T, HGRN_HEADS, HGRN_VDIM)
    o = hgrn2_chunkwise(q, k, v, log_f)
    o = o * lax.rsqrt(jnp.mean(o * o, axis=-1, keepdims=True) + EPS)
    o = o * norm_g.astype(jnp.float32).reshape(HGRN_HEADS, HGRN_VDIM)
    o = o.reshape(B, T, D_A) * jax.nn.silu(g_in.astype(jnp.float32))
    return o.astype(q_in.dtype)

def multiscale_pool(u, pool_w, pool_scale):
    B, T, _ = u.shape
    uf = u.astype(jnp.float32).reshape(B, T, POOL_GROUPS, POOL_CH)
    cs = jnp.cumsum(uf, axis=1)
    t_count = jnp.arange(1, T + 1, dtype=jnp.float32)
    outs = []
    for j, w in enumerate(POOL_WINDOWS):
        csj = cs[:, :, j]
        prev = jnp.pad(csj, ((0, 0), (w, 0), (0, 0)))[:, :T]
        mean = (csj - prev) / jnp.minimum(t_count, w)[None, :, None]
        outs.append(mean - uf[:, :, j])
    p = jnp.stack(outs, axis=2)
    y = jnp.einsum('btgc,gcd->btgd', p, pool_w.astype(jnp.float32)).reshape(B, T, D_B)
    return (y * pool_scale.astype(jnp.float32)).astype(u.dtype)

def mem_cross_attention(h, mem_n, wq, wkv, wo):
    B, T, _ = h.shape
    M = mem_n.shape[1]
    q = (h @ wq).reshape(B, T, XA_HEADS, XA_HEAD_DIM)
    kv = (mem_n @ wkv).reshape(B, M, 2, XA_HEADS, XA_HEAD_DIM)
    k, v = kv[:, :, 0], kv[:, :, 1]
    s = jnp.einsum('bthd,bmhd->bhtm', q, k).astype(jnp.float32) * (XA_HEAD_DIM ** -0.5)
    p = jax.nn.softmax(s, axis=-1).astype(h.dtype)
    o = jnp.einsum('bhtm,bmhd->bthd', p, v).reshape(B, T, D_MODEL)
    return o @ wo

def second_inputs(seed: int = 0) -> dict:
    key = jax.random.key(seed)
    ks = jax.random.split(key, 24)
    f32 = jnp.float32

    def nrm(k, shape, scale):
        return jax.random.normal(k, shape, f32) * scale

    def gain(k, shape):
        return 1.0 + 0.1 * jax.random.normal(k, shape, f32)

    L, D, F = DEPTH_2, D_MODEL, D_FF
    return {
        'x': nrm(ks[0], (BATCH, SEQ, D), 1.0),
        'mem': nrm(ks[1], (BATCH, N_MEM, D), 1.0),
        'ffn1_norm': gain(ks[2], (L, D)),
        'ffn1_w1': nrm(ks[3], (L, D, F), D ** -0.5),
        'ffn1_w3': nrm(ks[4], (L, D, F), D ** -0.5),
        'ffn1_w2': nrm(ks[5], (L, F, D), F ** -0.5),
        'mix_norm': gain(ks[6], (L, D)),
        'w_in': nrm(ks[7], (L, D, D_IN), D ** -0.5),
        'lb_logits': nrm(ks[8], (L, D_A), 1.0),
        'hgrn_norm': gain(ks[9], (L, D_A)),
        'pool_w': nrm(ks[10], (L, POOL_GROUPS, POOL_CH, POOL_CH), POOL_CH ** -0.5),
        'pool_scale': gain(ks[11], (L, D_B)),
        'w_out': nrm(ks[12], (L, D_MIX_2, D), D_MIX_2 ** -0.5),
        'xa_norm': gain(ks[13], (L, D)),
        'mem_norm': gain(ks[14], (L, D)),
        'xa_wq': nrm(ks[15], (L, D, D), D ** -0.5),
        'xa_wkv': nrm(ks[16], (L, D, 2 * D), D ** -0.5),
        'xa_wo': nrm(ks[17], (L, D, D), D ** -0.5),
        'ffn2_norm': gain(ks[18], (L, D)),
        'ffn2_w1': nrm(ks[19], (L, D, F), D ** -0.5),
        'ffn2_w3': nrm(ks[20], (L, D, F), D ** -0.5),
        'ffn2_w2': nrm(ks[21], (L, F, D), F ** -0.5),
        'final_norm': gain(ks[22], (D,)),
    }

def second_block(x, mem, ffn1_norm, ffn1_w1, ffn1_w3, ffn1_w2, mix_norm, w_in, lb_logits,
              hgrn_norm, pool_w, pool_scale, w_out, xa_norm, mem_norm, xa_wq, xa_wkv,
              xa_wo, ffn2_norm, ffn2_w1, ffn2_w3, ffn2_w2, final_norm):
    lb_all = jnp.cumsum(jax.nn.softmax(lb_logits.astype(jnp.float32), axis=0), axis=0)
    lb_all = lb_all - lb_all[0:1]
    splits = [D_A, 2 * D_A, 3 * D_A, 4 * D_A]
    for l in range(DEPTH_2):
        x = x + 0.5 * swiglu(rmsnorm_2(x, ffn1_norm[l]), ffn1_w1[l], ffn1_w3[l], ffn1_w2[l])
        h = rmsnorm_2(x, mix_norm[l])
        proj = h @ w_in[l]
        q_a, f_a, i_a, g_a, u_b = jnp.split(proj, splits, axis=-1)
        o_a = hgrn2_mixer(q_a, f_a, i_a, g_a, lb_all[l], hgrn_norm[l])
        o_b = multiscale_pool(u_b, pool_w[l], pool_scale[l])
        x = x + jnp.concatenate([o_a, o_b], axis=-1) @ w_out[l]
        x = x + mem_cross_attention(rmsnorm_2(x, xa_norm[l]), rmsnorm_2(mem, mem_norm[l]),
                                    xa_wq[l], xa_wkv[l], xa_wo[l])
        x = x + 0.5 * swiglu(rmsnorm_2(x, ffn2_norm[l]), ffn2_w1[l], ffn2_w3[l], ffn2_w2[l])
    return rmsnorm_2(x, final_norm)


def setup_inputs(seed=0):
    out = dict(first_inputs(seed))
    for name, value in second_inputs(seed + 1).items():
        if name != "x":
            out[name + "_2"] = value
    return out


def reference(
    x, norm1_g, w_in, gla_gate_w2, gla_gate_b, gla_norm_g, w_out, norm2_g, router_group_w,
    router_group_b, router_expert_w, router_expert_b, expert_w1, expert_w3, expert_w2,
    final_norm_g, mem_2, ffn1_norm_2, ffn1_w1_2, ffn1_w3_2, ffn1_w2_2, mix_norm_2, w_in_2,
    lb_logits_2, hgrn_norm_2, pool_w_2, pool_scale_2, w_out_2, xa_norm_2, mem_norm_2, xa_wq_2,
    xa_wkv_2, xa_wo_2, ffn2_norm_2, ffn2_w1_2, ffn2_w3_2, ffn2_w2_2, final_norm_2,
):
    x = first_block(
        x, norm1_g, w_in, gla_gate_w2, gla_gate_b, gla_norm_g, w_out, norm2_g, router_group_w,
        router_group_b, router_expert_w, router_expert_b, expert_w1, expert_w3, expert_w2,
        final_norm_g,
    )
    return second_block(
        x, mem_2, ffn1_norm_2, ffn1_w1_2, ffn1_w3_2, ffn1_w2_2, mix_norm_2, w_in_2, lb_logits_2,
        hgrn_norm_2, pool_w_2, pool_scale_2, w_out_2, xa_norm_2, mem_norm_2, xa_wq_2, xa_wkv_2,
        xa_wo_2, ffn2_norm_2, ffn2_w1_2, ffn2_w3_2, ffn2_w2_2, final_norm_2,
    )


_drawn_inputs = setup_inputs


def setup_inputs(seed=0):
    import zlib

    import numpy as np

    out = dict(_drawn_inputs(seed))
    spreads = {}
    factors = {'router_group_b': 4.086, 'xa_norm_2': 4.474, 'mem_norm_2': 3.061}
    for name, (base, spread) in spreads.items():
        noise = np.random.default_rng([zlib.crc32(name.encode()), seed]).standard_normal(out[name].shape)
        drawn = base * np.exp(spread * noise) if base else spread * noise
        out[name] = jnp.asarray(drawn.astype(out[name].dtype))
    for name, factor in factors.items():
        out[name] = (out[name] * factor).astype(out[name].dtype)
    return out
```

```python
from contextlib import ExitStack

import numpy as np

import concourse.bass as bass
from concourse import mybir

F32 = mybir.dt.float32
U32 = mybir.dt.uint32
ALU = mybir.AluOpType
ACT = mybir.ActivationFunctionType
AX = mybir.AxisListType

P = 128
T = 256
TT = T // P
D = 1024
DT = D // P
EPS = 1e-6

GLA_DK = 64
GLA_TAU = 16.0
LOWRANK = 16
ATT_HEADS = 8
ATT_HD = 64
DILATIONS = ((128, 1), (512, 4), (2048, 16))
N_GROUPS = 4
PER_GROUP = 8
N_EXPERTS = N_GROUPS * PER_GROUP
N_LOGITS = N_GROUPS + N_EXPERTS
D_EXPERT = 512

LAYERS = 2
LIN_HEADS = 4
LIN_DV = 128
HGRN_DK = 128
D_FF = 2816
N_MEM = 256
XA_HEADS = 4
XA_HD = 256
POOL_WINDOWS = (2, 4, 8, 16)

SEG = 64
LEVELS = 7
PAD = 16

UNIT = 4096
RING = 5

GLR_AT = 1536

VECTORS = [("norm1_g", 1), ("norm2_g", 1), ("gla_norm_g", 1), ("gla_gate_b", 1), ("ffn1_norm_2", 2),
           ("mix_norm_2", 2), ("xa_norm_2", 2), ("mem_norm_2", 2), ("ffn2_norm_2", 2), ("hgrn_norm_2", 2),
           ("pool_scale_2", 2), ("lb_logits_2", 2)]
VECTOR_SIZE = {"gla_norm_g": 128, "gla_gate_b": 256, "hgrn_norm_2": 512, "pool_scale_2": 512, "lb_logits_2": 512}
ROWS = [("final_norm_g", D), ("final_norm_2", D), ("router_group_b", N_GROUPS), ("router_expert_b", N_EXPERTS)]


def vector_columns():
    at, start = 0, {}
    for name, layers in VECTORS:
        start[name] = at
        at += layers * VECTOR_SIZE.get(name, D) // P
    return start, at


def row_columns():
    at, start = 0, {}
    for name, size in ROWS:
        start[name] = at
        at += size
    return start, at


def shape_constants():
    row, col = np.arange(P)[:, None], np.arange(P)[None, :]
    parts = {}
    levels = [(row == col)]
    for level in range(1, LEVELS + 1):
        block, half = 1 << level, 1 << (level - 1)
        levels.append((row // block == col // block) & (row % block < half) & (col % block >= half))
    parts["levels"] = np.concatenate([m.astype(np.float32) for m in levels], axis=1)
    i = (np.arange(TT)[:, None, None] * P + np.arange(P)[None, :, None])
    j = np.arange(T)[None, None, :]
    back = i - j
    count = np.zeros(back.shape, np.int64)
    for window, dilation in DILATIONS:
        count += (back >= 0) & (back % dilation == 0) & (back <= window)
    log_count = np.where(count > 0, np.log(np.maximum(count, 1)), -1e30).astype(np.float32)
    parts["log_count"] = log_count.transpose(1, 0, 2).reshape(P, TT * T)
    token = np.arange(T)
    keep = np.tile((token % SEG != 0).astype(np.float32), 4)
    parts["keep"] = np.broadcast_to(keep, (P, 4 * T))
    share = np.concatenate([1.0 / np.minimum(token + 1, w) for w in POOL_WINDOWS]).astype(np.float32)
    parts["share"] = np.broadcast_to(share, (P, 4 * T))
    parts["index"] = np.broadcast_to(np.arange(PER_GROUP, dtype=np.float32), (P, PER_GROUP))
    at, start = 0, {}
    for name, a in parts.items():
        start[name] = (at, a.shape[1])
        at += a.shape[1]
    return start, np.concatenate(list(parts.values()), axis=1).astype(np.float32)


class Engine:

    def __init__(self, semaphore, one_by_one=True):
        self.semaphore = semaphore
        self.one_by_one = one_by_one
        self.count = 0
        self.steps = []
        self.waited = {}

    def wait(self, *done):
        for semaphore, value in done:
            if self.waited.get(semaphore.name, 0) < value:
                self.waited[semaphore.name] = value
                self.steps.append(lambda e, s=semaphore, v=value: e.wait_ge(s, v))

    def quiet(self, make, *done):
        self.wait(*done)
        self.steps.append(make)

    def __call__(self, make, *done):
        self.wait(*done)
        if self.one_by_one and self.count:
            self.wait(self.last)
        self.count += 1
        self.steps.append(lambda e: make(e).then_inc(self.semaphore, 1))
        return (self.semaphore, self.count)

    @property
    def last(self):
        return (self.semaphore, self.count)

    def emit(self, e):
        for step in self.steps:
            step(e)


class Bank:

    def __init__(self, ap):
        self.ap = ap
        self.free = ()


class Stream:

    def __init__(self, slots, semaphores):
        self.slots = slots
        self.semaphores = semaphores
        self.sources = []
        self.released = []

    def take(self, source):
        n = len(self.sources)
        self.sources.append(source)
        self.released.append(None)
        return n, self.slots[n % RING], (self.semaphores[n % RING], 16 * (n // RING + 1))

    def plan(self, dma):
        for n, source in enumerate(self.sources):
            if n >= RING:
                dma.wait(self.released[n - RING])
            slot = self.slots[n % RING]
            shape = source.shape
            target = slot[:, 0:shape[1] * shape[2]].rearrange("p (a b) -> p a b", a=shape[1])
            semaphore = self.semaphores[n % RING]
            dma.steps.append(lambda e, t=target, s=source, m=semaphore: e.dma_start(t, s).then_inc(m, 16))


def build(nc, a, out, limit=None):
    with ExitStack() as ctx:
        def sb(name, *shape):
            return ctx.enter_context(nc.sbuf_tensor(name, list(shape), F32))

        def sem(name):
            return ctx.enter_context(nc.semaphore(name))

        const_at, _ = a["constants_at"], None
        vec_at, n_vec = vector_columns()
        row_at, n_row = row_columns()

        ring = [sb(f"weights_{i}", P, UNIT) for i in range(RING)]
        constants = sb("constants", P, a["constants"].shape[1])
        vectors = sb("vectors", P, n_vec)
        rows = sb("rows", P, n_row)
        resid = sb("resid", P, TT, D)
        normed = sb("normed_T", P, DT, T)
        mem_T = sb("mem_T", P, DT, T)
        mix_T = sb("mix_T", P, DT, T)
        q_T = sb("q_T", P, DT, T)
        k_T = sb("k_T", P, DT, T)
        v_tok = sb("v_tok", P, TT, D)
        work = sb("work", P, TT, D)
        scratch = [sb(f"scratch_{i}", P, 4 * (PAD + T)) for i in range(4)]
        gate_tok = sb("gate_tok", P, TT, 512)
        attn = sb("attn", P, 3, 512)
        w_router = sb("w_router", P, DT, N_LOGITS)
        w_lowrank = sb("w_lowrank", P, DT, LOWRANK)
        gate_w2 = sb("gate_w2", LOWRANK, 2 * P)
        pool_w = sb("pool_w", P, 4, P)
        lowrank_T = sb("lowrank_T", LOWRANK, T)
        gates = sb("gates", P, TT, N_EXPERTS)
        gates_T = sb("gates_T", N_EXPERTS, T)
        stats = sb("stats", P, 64)
        route = sb("route", P, 256)
        lb = sb("lb", P, 32)
        picks = ctx.enter_context(nc.sbuf_tensor("picks", [P, 16], U32))

        banks = [Bank(ctx.enter_context(nc.psum_tensor(f"bank_{i}", [P, 512], F32))) for i in range(8)]
        y_banks, loose = banks[0:4], banks[4:8]

        act, dve, pool, sp = (Engine(sem(f"{n}_done")) for n in ("act", "dve", "pool", "sp"))
        pe = Engine(sem("pe_done"), one_by_one=False)
        slot_loaded = [sem(f"slot_loaded_{i}") for i in range(RING)]
        small_loaded = sem("small_loaded")
        x_loaded = sem("x_loaded")
        mem_loaded = [sem(f"mem_loaded_{i}") for i in range(LAYERS)]
        pool_w_loaded = [sem(f"pool_w_loaded_{i}") for i in range(LAYERS)]
        stored = sem("stored")
        stream = Stream(ring, slot_loaded)

        def const(name):
            at, size = const_at[name]
            return constants[:, at:at + size]

        ident = const("levels")[:, 0:P]

        def vector(name, layer=0):
            size = VECTOR_SIZE.get(name, D) // P
            at = vec_at[name] + layer * size
            return vectors[:, at:at + size]

        def row(name):
            return rows[:, row_at[name]:row_at[name] + dict(ROWS)[name]]

        turn = [0]

        def next_bank():
            turn[0] += 1
            return loose[turn[0] % 4]

        def tiles(ap):
            return ap.rearrange("p (a b) -> p a b", b=T)

        small = [(constants[:, :], a["constants"]), (vectors[:, :], a["vectors"]), (rows[:, :], a["rows"]),
                 (w_router[:, :, 0:N_GROUPS], a["router_group_w"][0].rearrange("(t p) n -> p t n", p=P)),
                 (w_router[:, :, N_GROUPS:], a["router_expert_w"][0].rearrange("(t p) n -> p t n", p=P)),
                 (w_lowrank[:, :, :],
                  a["w_in"][0, :, GLR_AT:GLR_AT + LOWRANK].rearrange("(t p) n -> p t n", p=P)),
                 (gate_w2[:, :], a["gla_gate_w2"][0])]
        act.steps.append(lambda e: e.dma_start(resid[:, :, :], a["x"][0].rearrange("(t p) n -> p t n", p=P))
                         .then_inc(x_loaded, 16))
        for target, source in small:
            act.steps.append(lambda e, t=target, s=source: e.dma_start(t, s).then_inc(small_loaded, 16))
        have_x = (x_loaded, 16)
        have_small = (small_loaded, 16 * len(small))


        def inverse_rms(src, at, ready, size=D):
            for t in range(TT):
                squares = act(lambda e, t=t: e.activation(scratch[3][:, 0:size], src[:, t, :], ACT.Square,
                                                          accum_out=stats[:, at + t:at + t + 1]), *ready)
            s = stats[:, at:at + TT]
            mean = dve(lambda e: e.tensor_scalar(s, s, 1.0 / size, EPS, ALU.mult, ALU.add), squares)
            inverse = dve(lambda e: e.reciprocal(s, s), mean)
            return act(lambda e: e.activation(s, s, ACT.Sqrt), inverse)

        def to_features(src, dst, gain, ready, n_tiles=DT, src_at=0, dst_at=0):
            done = []
            for k in range(0, n_tiles, 2):
                bank = next_bank()
                pe.wait(*ready, have_small, *bank.free)
                for j in range(2):
                    for t in range(TT):
                        at = (src_at + k + j) * P
                        turned = pe(lambda e, t=t, at=at, j=j, b=bank: e.transpose(
                            b.ap[:, j * T + t * P:j * T + (t + 1) * P], src[:, t, at:at + P], ident))
                if k % 4 == 0:
                    for j in range(2):
                        last = act(lambda e, k=k, j=j, b=bank: e.activation(
                            dst[:, dst_at + k + j, :], b.ap[:, j * T:(j + 1) * T], ACT.Copy,
                            scale=gain[:, k + j:k + j + 1]), turned)
                else:
                    for j in range(2):
                        last = dve(lambda e, k=k, j=j, b=bank: e.tensor_scalar(
                            dst[:, dst_at + k + j, :], b.ap[:, j * T:(j + 1) * T], gain[:, k + j:k + j + 1],
                            None, ALU.mult), turned)
                bank.free = (last,)
                done.append(last)
            return done[-2:]

        def norm_to_features(src, dst, gain, ready, at=0):
            rms = inverse_rms(src, at, ready)
            for t in range(TT):
                scaled = dve(lambda e, t=t: e.tensor_scalar(work[:, t, :], src[:, t, :], stats[:, at + t:at + t + 1],
                                                            None, ALU.mult), rms)
            return to_features(work, dst, gain, (scaled,))

        def columns(w, start):
            return w[:, start:start + 512].rearrange("(t p) n -> p t n", p=P)

        def features_out(source, src, ready, evacuate):
            n, slot, arrived = stream.take(source)
            w = slot[:, :].rearrange("p (t n) -> p t n", t=DT)
            for pair in range(2):
                bank = next_bank()
                pe.wait(*ready, arrived, *bank.free)
                for j in range(2):
                    at = (2 * pair + j) * P
                    for k in range(DT):
                        make = lambda e, k=k, at=at, j=j, b=bank: e.matmul(
                            b.ap[:, j * T:(j + 1) * T], w[:, k, at:at + P], src[:, k, :],
                            start=(k == 0), stop=(k == DT - 1))
                        if k < DT - 1:
                            pe.quiet(make)
                        else:
                            done = pe(make)
                bank.free = (evacuate(pair, bank.ap, done),)
            stream.released[n] = done
            return bank.free[0]

        def tokens_out(source, src, ready, evacuate):
            n, slot, arrived = stream.take(source)
            w = slot[:, :].rearrange("p (t n) -> p t n", t=DT)
            freed = []
            for t in range(TT):
                bank = next_bank()
                pe.wait(*ready, arrived, *bank.free)
                for k in range(DT):
                    make = lambda e, k=k, t=t, b=bank: e.matmul(
                        b.ap[:, :], src[:, k, t * P:(t + 1) * P], w[:, k, :], start=(k == 0), stop=(k == DT - 1))
                    if k < DT - 1:
                        pe.quiet(make)
                    else:
                        done = pe(make)
                bank.free = (evacuate(t, bank.ap, done),)
                freed.append(bank.free[0])
            stream.released[n] = done
            return freed

        def act_copy(dst, scale=1.0, func=ACT.Copy):
            return lambda i, bank, done: act(lambda e: e.activation(dst(i), bank[:, :], func, scale=scale), done)

        def dve_copy(dst):
            return lambda i, bank, done: dve(lambda e: e.tensor_copy(dst(i), bank[:, :]), done)

        def pair_of(dst, at=0):
            return lambda pair: dst[:, at + 2 * pair:at + 2 * pair + 2, :].rearrange("p a b -> p (a b)")

        def add_projection(w, src, ready):
            done = []
            for half in range(2):
                def add(t, bank, made, half=half):
                    r = resid[:, t, half * 512:(half + 1) * 512]
                    return dve(lambda e: e.tensor_tensor(r, bank[:, :], r, ALU.add), made)
                done += tokens_out(columns(w, half * 512), src, ready, add)
            return done[-1:]

        def swiglu(w13, w2_units, n_tiles, src, ready, gate_of=None):
            hidden, silus = scratch[0], scratch[1]
            pending = []
            units = {}

            def second(f, ready_h, w2, last):
                unit, slot, arrived = w2
                pe.wait(ready_h, arrived)
                if f == 0:
                    for b in y_banks:
                        pe.wait(*b.free)
                at = (f % 4) * D
                for t in range(TT):
                    for half in range(2):
                        make = lambda e, t=t, half=half: e.matmul(
                            y_banks[2 * t + half].ap[:, :],
                            hidden[:, (f % 4) * T + t * P:(f % 4) * T + (t + 1) * P],
                            slot[:, at + half * 512:at + (half + 1) * 512],
                            start=(f == 0), stop=(f == n_tiles - 1))
                        if t == TT - 1 and half == 1:
                            done = pe(make)
                        else:
                            pe.quiet(make)
                read_h[f % 4] = (done,)
                if last:
                    stream.released[unit] = done
                return done

            read_h = {i: () for i in range(4)}
            gate_bc = None
            for f in range(n_tiles):
                group, within = f // 4, f % 4
                last_of_group = within == 3 or f == n_tiles - 1
                if within == 0:
                    w1, w3 = (stream.take(s) for s in w13(group))
                    w2 = stream.take(w2_units(group))
                    if gate_of:
                        gate_bc = gate_of(group)
                bank = next_bank()
                pe.wait(*ready, *bank.free)
                for j, (unit, slot, arrived) in enumerate((w1, w3)):
                    width = w13(group)[0].shape[2]
                    w = slot[:, 0:DT * width].rearrange("p (t n) -> p t n", t=DT)
                    pe.wait(arrived)
                    for k in range(DT):
                        make = lambda e, k=k, j=j, b=bank, w=w, within=within: e.matmul(
                            b.ap[:, j * T:(j + 1) * T], w[:, k, within * P:(within + 1) * P], src[:, k, :],
                            start=(k == 0), stop=(k == DT - 1))
                        if k < DT - 1:
                            pe.quiet(make)
                        else:
                            both = pe(make)
                    if last_of_group:
                        stream.released[unit] = both
                s = silus[:, (f % 4) * T:(f % 4 + 1) * T]
                h = hidden[:, (f % 4) * T:(f % 4 + 1) * T]
                silu = act(lambda e, b=bank, s=s: e.activation(s, b.ap[:, 0:T], ACT.Silu), both,
                           *read_h[f % 4])
                product = dve(lambda e, b=bank, s=s, h=h: e.tensor_tensor(
                    h, s, b.ap[:, T:2 * T], ALU.mult), silu)
                bank.free = (product,)
                if gate_bc:
                    product = dve(lambda e, h=h, g=gate_bc[0]: e.tensor_tensor(h, h, g, ALU.mult),
                                  product, gate_bc[1])
                pending.append((f, product, w2, last_of_group))
                if len(pending) > 1:
                    second(*pending.pop(0))
            return second(*pending.pop(0))

        def add_y(done, scale):
            for t in range(TT):
                for half in range(2):
                    r = resid[:, t, half * 512:(half + 1) * 512]
                    b = y_banks[2 * t + half]
                    added = dve(lambda e, r=r, b=b: e.scalar_tensor_tensor(r, b.ap[:, :], scale, r, ALU.mult,
                                                                           ALU.add), done)
                    b.free = (added,)
            return (added,)

        def softmax_rows(score_bank, scored, at, scale, log_count=None):
            p = probs[at % 2]
            top = stats[:, 8 + 4 * (at % 2):10 + 4 * (at % 2)]
            den = stats[:, 10 + 4 * (at % 2):12 + 4 * (at % 2)]
            if log_count is not None:
                s = dve(lambda e, scale=scale: e.scalar_tensor_tensor(p, score_bank.ap[:, :], scale, log_count, ALU.mult,
                                                         ALU.add), scored, *prob_free[at % 2])
                source, scale = p, 1.0
                score_bank.free = (s,)
            else:
                s, source = scored, score_bank.ap[:, :]
            largest = dve(lambda e: e.tensor_reduce(top, tiles(source), AX.X, ALU.max, negate=True), s,
                          *prob_free[at % 2])
            if scale != 1.0:
                largest = dve(lambda e: e.tensor_scalar(top, top, scale, None, ALU.mult), largest)
            for t in range(TT):
                ex = act(lambda e, t=t: e.activation(p[:, t * T:(t + 1) * T], source[:, t * T:(t + 1) * T],
                                                     ACT.Exp, bias=top[:, t:t + 1], scale=scale,
                                                     accum_out=den[:, t:t + 1]), largest)
            if log_count is None:
                score_bank.free = (ex,)
            inv = dve(lambda e: e.reciprocal(den, den), ex)
            return dve(lambda e: e.tensor_tensor(tiles(p), tiles(p), den.unsqueeze(2).broadcast_to([P, TT, T]),
                                                 ALU.mult), inv)

        probs = [scratch[2][:, 0:512], scratch[2][:, 512:1024]]
        prob_free = [(), ()]
        probs_T = [scratch[1][:, 0:512], scratch[1][:, 512:1024]]
        probs_T_free = [(), ()]

        def turn_probs(p_ready, at):
            bank = next_bank()
            pe.wait(p_ready, *bank.free)
            for kt in range(TT):
                for t in range(TT):
                    turned = pe(lambda e, kt=kt, t=t, b=bank: e.transpose(
                        b.ap[:, kt * T + t * P:kt * T + (t + 1) * P],
                        probs[at % 2][:, t * T + kt * P:t * T + (kt + 1) * P], ident))
            prob_free[at % 2] = (turned,)
            copied = act(lambda e, b=bank: e.activation(probs_T[at % 2], b.ap[:, :], ACT.Copy), turned,
                         *probs_T_free[at % 2])
            bank.free = (copied,)
            return copied

        def linear_attention(dk, n_q, q_ready, v_ready, gate_ready, norm_gain, q_at=0, v_at=0):
            n = n_q * T
            b = scratch[0][:, 0:n]
            arg, xq, xk = scratch[1][:, 0:n], scratch[2][:, 0:n], scratch[3][:, 0:n]
            q = q_T[:, q_at:q_at + n_q, :].rearrange("p a b -> p (a b)")
            k = k_T[:, q_at:q_at + n_q, :].rearrange("p a b -> p (a b)")
            cleared = dve(lambda e: e.memset(xq, 0.0), *q_ready)
            cleared = dve(lambda e: e.memset(xk, 0.0))
            xq_free, arg_free = (), ()
            evacuated = None

            def scores(xq, xk, ready, level):
                blocks = [(0, 0, 0), (1, 1, 1)] if level <= LEVELS else [(2, 0, 1)]
                for target, jt, it in blocks:
                    bank = next_bank()
                    pe.wait(*ready, *bank.free)
                    for n_h, h in enumerate(sorted(range(LIN_HEADS), key=lambda h: h * dk % P)):
                        tile, part = h * dk // P, h * dk % P
                        if part and n_h == LIN_HEADS // 2:
                            pe.wait(pe.last)
                        done = pe(lambda e, h=h, tile=tile, part=part, jt=jt, it=it, bk=bank: e.matmul(
                            bk.ap[:, h * P:(h + 1) * P],
                            xk[part:part + dk, tile * T + jt * P:tile * T + (jt + 1) * P],
                            xq[part:part + dk, tile * T + it * P:tile * T + (it + 1) * P],
                            start=True, stop=True))
                    dst = attn[:, target, :].rearrange("p (h i) -> p h i", h=LIN_HEADS)
                    src = bank.ap[:, :].rearrange("p (h i) -> p h i", h=LIN_HEADS)
                    if level <= LEVELS:
                        mask = const("levels")[:, level * P:(level + 1) * P].unsqueeze(1)\
                            .broadcast_to([P, LIN_HEADS, P])
                    if level == 0:
                        got = dve(lambda e, d=dst, s=src, m=mask: e.tensor_tensor(d, s, m, ALU.mult), done)
                    elif level <= LEVELS:
                        got = dve(lambda e, d=dst, s=src, m=mask: e.copy_predicated(d, m.bitcast(U32), s),
                                  done, got_by[target])
                    else:
                        got = dve(lambda e, d=dst, s=src: e.tensor_copy(d, s), done)
                    got_by[target] = got
                    bank.free = (got,)
                return done

            got_by = {}
            scores(q, k, q_ready, 0)
            def level_factors(level, arg_free, xq_free):
                half = 1 << (level - 1)
                if level <= LEVELS - 1:
                    split = lambda x: x.rearrange("p (m s) -> p m s", s=2 * half)
                    first = lambda x: split(x)[:, :, 0:half]
                    later = lambda x: split(x)[:, :, half:2 * half]
                    mid = split(b)[:, :, half - 1:half].broadcast_to([P, n // (2 * half), half])
                    a1 = dve(lambda e, f=first, m=mid: e.tensor_tensor(f(arg), m, f(b), ALU.subtract),
                             *q_ready, *arg_free)
                    a2 = dve(lambda e, l=later, m=mid: e.tensor_tensor(l(arg), l(b), m, ALU.subtract))
                elif level == LEVELS:
                    split = lambda x: x.rearrange("p (m s) -> p m s", s=2 * SEG)
                    first = lambda x: split(x)[:, :, 0:SEG]
                    later = lambda x: split(x)[:, :, SEG:2 * SEG]
                    end = first(b)[:, :, SEG - 1:SEG].broadcast_to([P, n // (2 * SEG), SEG])
                    a1 = dve(lambda e: e.tensor_tensor(first(arg), end, first(b), ALU.subtract), *arg_free)
                    a2 = dve(lambda e: e.tensor_copy(later(arg), later(b)))
                else:
                    seg = lambda x: x.rearrange("p (m c s) -> p m c s", c=4, s=SEG)
                    split = lambda x: x.rearrange("p (m s) -> p m s", s=T)
                    first = lambda x: split(x)[:, :, 0:P]
                    later = lambda x: split(x)[:, :, P:T]
                    total = lambda c: seg(b)[:, :, c, SEG - 1:SEG].broadcast_to([P, n_q, SEG])
                    t0 = dve(lambda e: e.tensor_tensor(seg(arg)[:, :, 0, :], total(0), seg(b)[:, :, 0, :],
                                                       ALU.subtract), *arg_free)
                    dve(lambda e: e.tensor_tensor(seg(arg)[:, :, 0, :], seg(arg)[:, :, 0, :], total(1), ALU.add),
                        t0)
                    dve(lambda e: e.tensor_tensor(seg(arg)[:, :, 1, :], total(1), seg(b)[:, :, 1, :],
                                                  ALU.subtract))
                    dve(lambda e: e.tensor_copy(seg(arg)[:, :, 2, :], seg(b)[:, :, 2, :]))
                    a2 = dve(lambda e: e.tensor_tensor(seg(arg)[:, :, 3, :], seg(b)[:, :, 3, :], total(2),
                                                       ALU.add))
                ex = act(lambda e: e.activation(arg, arg, ACT.Exp), a2)
                r1 = dve(lambda e, l=later: e.tensor_tensor(l(xq), l(q), l(arg), ALU.mult), ex, *xq_free)
                r2 = pool(lambda e, f=first: e.tensor_tensor(f(xk), f(k), f(arg), ALU.mult), ex, cleared,
                          *xq_free)
                return (r1, r2), (scores(xq, xk, (r1, r2), level),)

            for level in range(1, LEVELS + 2):
                arg_free, xq_free = level_factors(level, arg_free, xq_free)

            v = v_tok
            outs = []
            for t in range(TT):
                bank = next_bank()
                pe.wait(*got_by.values(), *v_ready, *bank.free)
                for h in range(LIN_HEADS):
                    pieces = [(0, 0)] if t == 0 else [(2, 0), (1, 1)]
                    for i, (block, jt) in enumerate(pieces):
                        done = pe(lambda e, h=h, block=block, jt=jt, i=i, last=len(pieces) - 1, bk=bank: e.matmul(
                            bk.ap[:, h * P:(h + 1) * P], attn[:, block, h * P:(h + 1) * P],
                            v[:, jt, v_at + h * LIN_DV:v_at + (h + 1) * LIN_DV], start=(i == 0),
                            stop=(i == last)))
                outs.append((bank, done))
            s = stats[:, 16:16 + TT * LIN_HEADS]
            for t, (bank, done) in enumerate(outs):
                square = act(lambda e, t=t, bk=bank: e.activation(work[:, t, 0:512], bk.ap[:, :], ACT.Square), done)
                gated = dve(lambda e, t=t, bk=bank: e.tensor_tensor(work[:, t, 512:D], bk.ap[:, :],
                                                                    gate_tok[:, t, :], ALU.mult),
                            square, *gate_ready)
                bank.free = (gated,)
                summed = dve(lambda e, t=t: e.tensor_reduce(
                    s[:, t * LIN_HEADS:(t + 1) * LIN_HEADS],
                    work[:, t, 0:512].rearrange("p (h v) -> p h v", h=LIN_HEADS), AX.X, ALU.add), square)
            mean = dve(lambda e: e.tensor_scalar(s, s, 1.0 / LIN_DV, EPS, ALU.mult, ALU.add), summed)
            inverse = dve(lambda e: e.reciprocal(s, s), mean)
            rms = act(lambda e: e.activation(s, s, ACT.Sqrt), inverse)
            for t in range(TT):
                o = work[:, t, 512:D].rearrange("p (h v) -> p h v", h=LIN_HEADS)
                r = s[:, t * LIN_HEADS:(t + 1) * LIN_HEADS].unsqueeze(2).broadcast_to([P, LIN_HEADS, LIN_DV])
                scaled = dve(lambda e, o=o, r=r: e.tensor_tensor(o, o, r, ALU.mult), rms)
            return to_features(work, mix_T, norm_gain, (scaled,), n_tiles=4, src_at=4, dst_at=0)

        def log_sigmoid(z, tmp, ready):
            t1 = act(lambda e: e.activation(tmp, z, ACT.Abs), *ready)
            t2 = act(lambda e: e.activation(tmp, tmp, ACT.Exp, scale=-1.0), t1)
            t3 = act(lambda e: e.activation(tmp, tmp, ACT.Ln, bias=1.0), t2)
            return t3, lambda dst: dve(lambda e: e.scalar_tensor_tensor(dst, z, 0.0, tmp, ALU.min, ALU.subtract),
                                       t3)

        def running_sum(values, dst, n, ready):
            return dve(lambda e: e.tensor_tensor_scan(dst, const("keep")[:, 0:n], values, 0.0, ALU.mult, ALU.add),
                       ready)

        stages = []

        def gla_and_attention():
            n_T = norm_to_features(resid, normed, vector("norm1_g"), (have_x, have_small))
            w = a["w_in"][0]
            bank = next_bank()
            pe.wait(*n_T, *bank.free)
            for k in range(DT):
                low = pe(lambda e, k=k, b=bank: e.matmul(b.ap[0:LOWRANK, 0:T], w_lowrank[:, k, :],
                                                         normed[:, k, :], start=(k == 0), stop=(k == DT - 1)))
            low = act(lambda e, b=bank: e.activation(lowrank_T[:, :], b.ap[0:LOWRANK, 0:T], ACT.Copy), low)
            bank.free = (low,)
            bank = next_bank()
            pe.wait(low, *bank.free)
            for j in range(2):
                made = pe(lambda e, j=j, b=bank: e.matmul(b.ap[:, j * T:(j + 1) * T],
                                                          gate_w2[:, j * P:(j + 1) * P], lowrank_T[:, :],
                                                          start=True, stop=True))
            z = scratch[1][:, 0:2 * T]
            for j in range(2):
                zed = dve(lambda e, j=j, b=bank: e.tensor_scalar(
                    z[:, j * T:(j + 1) * T], b.ap[:, j * T:(j + 1) * T], vector("gla_gate_b")[:, j:j + 1], None,
                    ALU.add), made)
            bank.free = (zed,)
            _, finish = log_sigmoid(z, scratch[2][:, 0:2 * T], (zed,))
            la = finish(scratch[1][:, 0:2 * T])
            la = dve(lambda e: e.tensor_scalar(z, z, 1.0 / GLA_TAU, None, ALU.mult), la)
            b_ready = running_sum(z, scratch[0][:, 0:2 * T], 2 * T, la)

            def q_and_k(pair, bank, done):
                dst = (q_T if pair == 0 else k_T)[:, 4:6, :].rearrange("p a b -> p (a b)")
                return act(lambda e: e.activation(dst, bank[:, :], ACT.Copy,
                                                  scale=GLA_DK ** -0.5 if pair == 0 else 1.0), done)
            qk = features_out(columns(w, 0), normed, n_T, q_and_k)
            v = tokens_out(columns(w, 512), normed, n_T, act_copy(lambda t: v_tok[:, t, 0:512]))
            gate = tokens_out(columns(w, 1024), normed, n_T, act_copy(lambda t: gate_tok[:, t, :], func=ACT.Silu))
            at = GLR_AT + LOWRANK
            aq = features_out(columns(w, at), normed, n_T, act_copy(pair_of(q_T)))
            ak = features_out(columns(w, at + 512), normed, n_T, dve_copy(pair_of(k_T)))
            av = tokens_out(columns(w, at + 1024), normed, n_T, act_copy(lambda t: v_tok[:, t, 512:D]))
            gla = linear_attention(GLA_DK, 2, (qk, b_ready), v, gate,
                                   vector("gla_norm_g").broadcast_to([P, 4]), q_at=4)
            log_count = const("log_count")
            for i in range(2):
                prob_free[i] = (pe.last, dve.last, pool.last)
                probs_T_free[i] = (pe.last, dve.last, pool.last)
            out_bank = None
            for h in range(ATT_HEADS):
                tile, part = h // 2, (h % 2) * ATT_HD
                bank = next_bank()
                pe.wait(aq, ak, *bank.free)
                for t in range(TT):
                    scored = pe(lambda e, t=t, tile=tile, part=part, b=bank: e.matmul(
                        b.ap[:, t * T:(t + 1) * T], q_T[part:part + ATT_HD, tile, t * P:(t + 1) * P],
                        k_T[part:part + ATT_HD, tile, :], start=True, stop=True))
                p_ready = softmax_rows(bank, scored, h, ATT_HD ** -0.5, log_count)
                p_T = turn_probs(p_ready, h)
                if h % 2 == 0:
                    out_bank = next_bank()
                    pe.wait(*out_bank.free)
                pe.wait(p_T, *av)
                pt = tiles(probs_T[h % 2])
                dst = out_bank.ap[part:part + ATT_HD, 0:T]
                for jt in range(TT):
                    done = pe(lambda e, jt=jt, h=h, pt=pt, dst=dst: e.matmul(
                        dst, v_tok[:, jt, 512 + h * ATT_HD:512 + (h + 1) * ATT_HD], pt[:, jt, :],
                        start=(jt == 0), stop=(jt == TT - 1)))
                probs_T_free[h % 2] = (done,)
                if h % 2:
                    put = dve(lambda e, b=out_bank, h=h: e.tensor_copy(mix_T[:, 4 + h // 2, :], b.ap[:, 0:T]), done)
                    out_bank.free = (put,)
            return add_projection(a["w_out"][0], mix_T, (*gla, put))

        def route_tokens(n_T):
            for t in range(TT):
                bank = next_bank()
                pe.wait(*n_T, have_small, *bank.free)
                for k in range(DT):
                    done = pe(lambda e, k=k, t=t, b=bank: e.matmul(
                        b.ap[:, 0:N_LOGITS], normed[:, k, t * P:(t + 1) * P], w_router[:, k, :],
                        start=(k == 0), stop=(k == DT - 1)))
                r = route[:, t * 128:(t + 1) * 128]
                logits, group8, top8, hot = r[:, 0:36], r[:, 36:44], r[:, 44:52], r[:, 52:56]
                spread, top2, pick1, pick2, one = r[:, 56:88], r[:, 88:96], r[:, 96:104], r[:, 104:112], r[:, 112:128]
                bias = rows[:, row_at["router_group_b"]:row_at["router_group_b"] + N_LOGITS]
                g = gates[:, t, :].rearrange("p (g e) -> p g e", g=N_GROUPS)
                experts = logits[:, N_GROUPS:].rearrange("p (g e) -> p g e", g=N_GROUPS)
                sp3 = spread.rearrange("p (g e) -> p g e", g=N_GROUPS)
                index = const("index")
                pk = picks[:, t * 8:(t + 1) * 8]

                def step(make, *more):
                    return dve(make, dve.last, *more)

                read = dve(lambda e, b=bank, l=logits, bi=bias: e.tensor_tensor(l, b.ap[:, 0:N_LOGITS], bi,
                                                                               ALU.add), done)
                bank.free = (read,)
                step(lambda e, x=group8: e.memset(x, -3.0e38))
                step(lambda e, x=group8, l=logits: e.tensor_copy(x[:, 0:N_GROUPS], l[:, 0:N_GROUPS]))
                step(lambda e, o=top8, x=group8: e.max(o, x))
                step(lambda e, o=pk, m=top8, x=group8: e.max_index(o, m, x))
                step(lambda e, o=one, x=pk: e.tensor_copy(o[:, 0:8], x))
                step(lambda e, o=hot, x=one, i=index: e.tensor_scalar(o, i[:, 0:N_GROUPS], x[:, 0:1], None,
                                                                      ALU.is_equal))
                neg = step(lambda e, o=one, m=top8: e.tensor_scalar(o[:, 8:9], m[:, 0:1], -1.0, None, ALU.mult))
                ex = act(lambda e, o=one, l=logits, s=spread: e.activation(
                    s[:, 0:N_GROUPS], l[:, 0:N_GROUPS], ACT.Exp, bias=o[:, 8:9], accum_out=o[:, 9:10]), neg)
                step(lambda e, o=one: e.reciprocal(o[:, 10:11], o[:, 9:10]), ex)
                step(lambda e, o=sp3, x=experts, hh=hot: e.tensor_tensor(
                    o, x, hh.unsqueeze(2).broadcast_to([P, N_GROUPS, PER_GROUP]), ALU.mult))
                step(lambda e, o=group8, s=sp3: e.tensor_reduce(o, s.rearrange("p g e -> p e g"), AX.X, ALU.add))
                step(lambda e, o=top2, x=group8: e.max(o, x))
                step(lambda e, o=pk, m=top2, x=group8: e.max_index(o, m, x))
                step(lambda e, o=one, x=pk: e.tensor_copy(o[:, 0:8], x))
                diff = step(lambda e, o=one, m=top2: e.tensor_tensor(o[:, 11:12], m[:, 1:2], m[:, 0:1],
                                                                     ALU.subtract))
                ex = act(lambda e, o=one: e.activation(o[:, 12:13], o[:, 11:12], ACT.Exp), diff)
                step(lambda e, o=one: e.tensor_scalar(o[:, 13:14], o[:, 12:13], 1.0, None, ALU.add), ex)
                step(lambda e, o=one: e.reciprocal(o[:, 14:15], o[:, 13:14]))
                step(lambda e, o=one: e.tensor_tensor(o[:, 14:15], o[:, 14:15], o[:, 10:11], ALU.mult))
                step(lambda e, o=one: e.tensor_tensor(o[:, 15:16], o[:, 14:15], o[:, 12:13], ALU.mult))
                step(lambda e, o=pick1, x=one, i=index: e.tensor_scalar(o, i, x[:, 0:1], x[:, 14:15],
                                                                        ALU.is_equal, ALU.mult))
                step(lambda e, o=pick2, x=one, i=index: e.tensor_scalar(o, i, x[:, 1:2], x[:, 15:16],
                                                                        ALU.is_equal, ALU.mult))
                step(lambda e, o=pick1, x=pick2: e.tensor_tensor(o, o, x, ALU.add))
                last = step(lambda e, o=g, x=pick1, hh=hot: e.tensor_tensor(
                    o, x.unsqueeze(1).broadcast_to([P, N_GROUPS, PER_GROUP]),
                    hh.unsqueeze(2).broadcast_to([P, N_GROUPS, PER_GROUP]), ALU.mult))
            bank = next_bank()
            pe.wait(last, *bank.free)
            for t in range(TT):
                turned = pe(lambda e, t=t, b=bank: e.transpose(b.ap[0:N_EXPERTS, t * P:(t + 1) * P],
                                                               gates[:, t, :], ident))
            got = dve(lambda e, b=bank: e.tensor_copy(gates_T[:, :], b.ap[0:N_EXPERTS, 0:T]), turned)
            bank.free = (got,)
            return got

        def experts(before):
            n_T = norm_to_features(resid, normed, vector("norm2_g"), before)
            routed = route_tokens(n_T)
            expert_gate = [mix_T[:, 0, :], mix_T[:, 1, :]]

            def gate_of(expert):
                bank = next_bank()
                made = pe(lambda e, b=bank: e.matmul(
                    b.ap[:, 0:T], ident[0:N_EXPERTS, expert:expert + 1].broadcast_to([N_EXPERTS, P]), gates_T[:, :],
                    start=True, stop=True), routed, *bank.free)
                dst = expert_gate[expert % 2]
                got = act(lambda e, b=bank, d=dst: e.activation(d, b.ap[:, 0:T], ACT.Copy), made, dve.last)
                bank.free = (got,)
                return dst, got

            w1, w3, w2 = a["expert_w1"][0], a["expert_w3"][0], a["expert_w2"][0]
            y = swiglu(lambda e: (w1[e].rearrange("(t p) n -> p t n", p=P),
                                  w3[e].rearrange("(t p) n -> p t n", p=P)),
                       lambda e: w2[e].rearrange("(t p) n -> p t n", p=P),
                       4 * N_EXPERTS, normed, n_T, gate_of)
            return add_y(y, 1.0)

        def norm_tokens(gain, before, dst):
            rms = inverse_rms(resid, 0, before)
            for t in range(TT):
                done = dve(lambda e, t=t: e.scalar_tensor_tensor(dst[:, t, :], resid[:, t, :], stats[:, t:t + 1],
                                                                 gain, ALU.mult, ALU.mult), rms)
            return (done,)

        def ffn(which, layer, before):
            n_T = norm_to_features(resid, normed, vector(f"{which}_norm_2", layer), before)
            w1, w3, w2 = (a[f"{which}_{m}_2"][layer] for m in ("w1", "w3", "w2"))

            def cut(w, g):
                return w[:, g * 512:min(D_FF, (g + 1) * 512)].rearrange("(t p) n -> p t n", p=P)
            y = swiglu(lambda g: (cut(w1, g), cut(w3, g)),
                       lambda g: w2[g * 512:min(D_FF, (g + 1) * 512), :].rearrange("(t p) n -> p t n", p=P),
                       D_FF // P, normed, n_T)
            return add_y(y, 0.5)

        def lower_bounds():
            l0, l1 = vector("lb_logits_2", 0), vector("lb_logits_2", 1)
            top, e0, e1, d0, d1 = (lb[:, 4 * i:4 * i + 4] for i in range(2, 7))
            m = dve(lambda e: e.tensor_tensor(top, l0, l1, ALU.max), have_small)
            dve(lambda e: e.tensor_tensor(d0, l0, top, ALU.subtract), m)
            d = dve(lambda e: e.tensor_tensor(d1, l1, top, ALU.subtract))
            act(lambda e: e.activation(e0, d0, ACT.Exp), d)
            x = act(lambda e: e.activation(e1, d1, ACT.Exp))
            s = dve(lambda e: e.tensor_tensor(e0, e0, e1, ALU.add), x)
            ln = act(lambda e: e.activation(e0, e0, ACT.Ln), s)
            dve(lambda e: e.tensor_tensor(lb[:, 0:4], d1, e0, ALU.subtract), ln)
            return dve(lambda e: e.tensor_tensor(lb[:, 4:8], d0, e0, ALU.subtract))

        def hgrn_and_pool(layer, before):
            n_T = norm_to_features(resid, normed, vector("mix_norm_2", layer), before)
            w = a["w_in_2"][layer]
            loaded = (pool_w_loaded[layer], 16)
            sp_wait = dve.last
            act.wait(pe.last)
            act.steps.append(lambda e: e.dma_start(pool_w[:, :, :], a["pool_w_2"][layer].rearrange("g c d -> c g d"))
                             .then_inc(pool_w_loaded[layer], 16))
            q = features_out(columns(w, 0), normed, n_T, act_copy(pair_of(q_T)))
            z4 = scratch[1][:, 0:4 * T]
            zed = features_out(columns(w, 512), normed, n_T, dve_copy(
                lambda pair: z4[:, pair * 512:(pair + 1) * 512]))
            v = tokens_out(columns(w, 1024), normed, n_T, act_copy(lambda t: v_tok[:, t, 0:512]))
            gate = tokens_out(columns(w, 1536), normed, n_T, act_copy(lambda t: gate_tok[:, t, :], func=ACT.Silu))
            u, wa, wb = (x[:, :].rearrange("p (g t) -> p g t", g=4) for x in (scratch[0], scratch[2], scratch[3]))
            pads = [dve(lambda e, x=x: e.memset(x[:, :, 0:PAD], 0.0)) for x in (u, wa, wb)]
            up = features_out(columns(w, 2048), normed, n_T, lambda pair, bank, done: dve(
                lambda e: e.tensor_copy(u[:, 2 * pair:2 * pair + 2, PAD:], bank[:, :].rearrange(
                    "p (a b) -> p a b", b=T)), done))

            def shifted(dst, src, g0, by, ready):
                return dve(lambda e: e.tensor_tensor(dst[:, g0:, PAD:], src[:, g0:, PAD:],
                                                     src[:, g0:, PAD - by:PAD + T - by], ALU.add), ready)
            last = shifted(wa, u, 0, 1, up)
            last = shifted(wb, wa, 1, 2, last)
            last = shifted(wa, wb, 2, 4, last)
            last = shifted(wb, wa, 3, 8, last)
            share = const("share").rearrange("p (g t) -> p g t", g=4)
            pooled = k_T[:, 4:8, :]
            for g in range(4):
                s = (wa, wb, wa, wb)[g]
                mean = dve(lambda e, g=g, s=s: e.tensor_tensor(pooled[:, g, :], s[:, g, PAD:], share[:, g, :],
                                                               ALU.mult), last)
            less = dve(lambda e: e.tensor_tensor(pooled, pooled, u[:, :, PAD:], ALU.subtract), mean)
            for pair in range(2):
                bank = next_bank()
                pe.wait(less, loaded, *bank.free)
                for j in range(2):
                    g = 2 * pair + j
                    made = pe(lambda e, g=g, j=j, b=bank: e.matmul(b.ap[:, j * T:(j + 1) * T], pool_w[:, g, :],
                                                                   pooled[:, g, :], start=True, stop=True))
                for j in range(2):
                    g = 2 * pair + j
                    put = dve(lambda e, g=g, j=j, b=bank: e.tensor_scalar(
                        mix_T[:, 4 + g, :], b.ap[:, j * T:(j + 1) * T],
                        vector("pool_scale_2", layer)[:, g:g + 1], None, ALU.mult), made)
                bank.free = (put,)
            tmp, logf = scratch[2][:, 0:4 * T], scratch[3][:, 0:4 * T]
            _, finish = log_sigmoid(z4, tmp, (zed, less))
            lsz = finish(logf)
            km = dve(lambda e: e.tensor_tensor(tmp, logf, z4, ALU.subtract), lsz)
            k4 = k_T[:, 0:4, :].rearrange("p a b -> p (a b)")
            if layer == 0:
                keys = act(lambda e: e.activation(k4, tmp, ACT.Exp), km)
                b_ready = running_sum(logf, scratch[0][:, 0:4 * T], 4 * T, lsz)
            else:
                for j in range(4):
                    keys = act(lambda e, j=j: e.activation(k4[:, j * T:(j + 1) * T], tmp[:, j * T:(j + 1) * T],
                                                           ACT.Exp, bias=lb[:, 4 + j:5 + j]), km)
                larger = scratch[0][:, 0:4 * T]
                for j in range(4):
                    c = slice(j * T, (j + 1) * T)
                    x1 = dve(lambda e, j=j, c=c: e.tensor_scalar(logf[:, c], logf[:, c], lb[:, 4 + j:5 + j], None,
                                                                 ALU.add), km)
                    dve(lambda e, j=j, c=c: e.tensor_scalar(larger[:, c], logf[:, c], lb[:, j:j + 1], None,
                                                            ALU.max), x1)
                    x2 = dve(lambda e, j=j, c=c: e.tensor_scalar(logf[:, c], logf[:, c], lb[:, j:j + 1], None,
                                                                 ALU.subtract))
                act(lambda e: e.activation(logf, logf, ACT.Abs), x2)
                act(lambda e: e.activation(logf, logf, ACT.Exp, scale=-1.0), act.last)
                ln = act(lambda e: e.activation(logf, logf, ACT.Ln, bias=1.0), act.last)
                whole = dve(lambda e: e.tensor_tensor(logf, logf, larger, ALU.add), ln)
                b_ready = running_sum(logf, scratch[0][:, 0:4 * T], 4 * T, whole)
            heads = linear_attention(HGRN_DK, 4, (q, keys, b_ready), v, gate, vector("hgrn_norm_2", layer))
            return add_projection(a["w_out_2"][layer], mix_T, (*heads, put))

        def cross_attention(layer, before):
            act.wait(*before)
            act.steps.append(lambda e: e.dma_start(v_tok[:, :, :], a["mem_2"][0].rearrange("(t p) n -> p t n", p=P))
                             .then_inc(mem_loaded[layer], 16))
            m_T = norm_to_features(v_tok, mem_T, vector("mem_norm_2", layer), ((mem_loaded[layer], 16),), at=2)
            n_T = norm_to_features(resid, normed, vector("xa_norm_2", layer), (*before, *m_T))
            wq, wkv = a["xa_wq_2"][layer], a["xa_wkv_2"][layer]
            for i in range(2):
                k_ready = features_out(columns(wkv, 512 * i), mem_T, m_T, dve_copy(pair_of(k_T, 4 * i)))
            for i in range(2):
                v_ready = tokens_out(columns(wkv, D + 512 * i), mem_T, m_T,
                                     act_copy(lambda t, i=i: v_tok[:, t, 512 * i:512 * (i + 1)]))
            for i in range(2):
                q_ready = features_out(columns(wq, 512 * i), normed, n_T, act_copy(pair_of(q_T, 4 * i)))
            for i in range(2):
                prob_free[i] = (pe.last, dve.last, act.last)
                probs_T_free[i] = (pe.last, dve.last, act.last)
            for h in range(XA_HEADS):
                bank = next_bank()
                pe.wait(q_ready, k_ready, *bank.free)
                for t in range(TT):
                    for j in range(2):
                        scored = pe(lambda e, t=t, j=j, h=h, b=bank: e.matmul(
                            b.ap[:, t * T:(t + 1) * T], q_T[:, 2 * h + j, t * P:(t + 1) * P], k_T[:, 2 * h + j, :],
                            start=(j == 0), stop=(j == 1)))
                p_ready = softmax_rows(bank, scored, h, XA_HD ** -0.5)
                p_T = turn_probs(p_ready, h)
                bank = next_bank()
                pe.wait(p_T, *v_ready, *bank.free)
                pt = tiles(probs_T[h % 2])
                for j in range(2):
                    for mt in range(TT):
                        done = pe(lambda e, j=j, mt=mt, h=h, pt=pt, b=bank: e.matmul(
                            b.ap[:, j * T:(j + 1) * T],
                            v_tok[:, mt, h * XA_HD + j * P:h * XA_HD + (j + 1) * P], pt[:, mt, :],
                            start=(mt == 0), stop=(mt == TT - 1)))
                probs_T_free[h % 2] = (done,)
                put = dve(lambda e, h=h, b=bank: e.tensor_copy(
                    mix_T[:, 2 * h:2 * h + 2, :].rearrange("p a b -> p (a b)"), b.ap[:, :]), done)
                bank.free = (put,)
            return add_projection(a["xa_wo_2"][layer], mix_T, (put,))

        done = (have_x,)
        steps = [lambda d: gla_and_attention(), experts,
                 lambda d: norm_tokens(row("final_norm_g"), (*d, lower_bounds()), resid)]
        for layer in range(LAYERS):
            steps += [lambda d, l=layer: ffn("ffn1", l, d), lambda d, l=layer: hgrn_and_pool(l, d),
                      lambda d, l=layer: cross_attention(l, d), lambda d, l=layer: ffn("ffn2", l, d)]
        if limit is not None:
            steps = steps[:limit]
        for step in steps:
            done = step(done)
        result = resid
        if limit is None:
            done = norm_tokens(row("final_norm_2"), done, work)
            result = work
        stream.plan(sp)
        sp.wait(*done)
        sp.steps.append(lambda e: e.dma_start(out[0].rearrange("(t p) n -> p t n", p=P), result[:, :, :])
                        .then_inc(stored, 16))
        sp.wait((stored, 16))

        block = ctx.enter_context(nc.Block())
        block.sync(sp.emit)
        block.scalar(act.emit)
        block.tensor(pe.emit)
        block.vector(dve.emit)
        block.gpsimd(pool.emit)


DIRECT = ["x", "w_in", "gla_gate_w2", "w_out", "router_group_w", "router_expert_w", "expert_w1", "expert_w3",
          "expert_w2", "mem_2", "ffn1_w1_2", "ffn1_w3_2", "ffn1_w2_2", "w_in_2", "pool_w_2", "w_out_2", "xa_wq_2",
          "xa_wkv_2", "xa_wo_2", "ffn2_w1_2", "ffn2_w3_2", "ffn2_w2_2"]


def kernel(**inputs):
    import concourse.bacc as bacc
    from concourse.bass_utils import run_bass_kernel_spmd

    nc = bacc.Bacc("TRN2", target_bir_lowering=False, num_devices=1)
    arrays = {name: np.ascontiguousarray(inputs[name]) for name in DIRECT}
    arrays["vectors"] = np.ascontiguousarray(
        np.concatenate([np.asarray(inputs[name]).reshape(-1, P) for name, _ in VECTORS]).T)
    row = np.concatenate([np.asarray(inputs[name]).reshape(-1) for name, _ in ROWS])
    arrays["rows"] = np.ascontiguousarray(np.broadcast_to(row, (P, row.size)))
    start, arrays["constants"] = shape_constants()
    a = {name: nc.dram_tensor(f"in_{name}", v.shape, mybir.dt.from_np(v.dtype), kind="ExternalInput").ap()
         for name, v in arrays.items()}
    a["constants_at"] = start
    out = nc.dram_tensor("out_0", (1, T, D), F32, kind="ExternalOutput").ap()
    build(nc, a, out)
    result = run_bass_kernel_spmd(nc, [{f"in_{name}": v for name, v in arrays.items()}], core_ids=[0])
    return result.results[0]["out_0"]
```

```python
from contextlib import ExitStack

import numpy as np

import concourse.bass as bass
from concourse import mybir

F32 = mybir.dt.float32
U32 = mybir.dt.uint32
I32 = mybir.dt.int32
ALU = mybir.AluOpType
ACT = mybir.ActivationFunctionType
AX = mybir.AxisListType

P = 128
T = 256
TT = T // P
D = 1024
DT = D // P
EPS = 1e-6

GLA_DK = 64
GLA_TAU = 16.0
LOWRANK = 16
ATT_HEADS = 8
ATT_HD = 64
DILATIONS = ((128, 1), (512, 4), (2048, 16))
N_GROUPS = 4
PER_GROUP = 8
N_EXPERTS = N_GROUPS * PER_GROUP
N_LOGITS = N_GROUPS + N_EXPERTS
D_EXPERT = 512
TOP_K = 2
SLOTS = 64
EXTRA = (TOP_K * T - 1) // (SLOTS + 1)
BLOCKS = N_EXPERTS + EXTRA

LAYERS = 2
LIN_HEADS = 4
LIN_DV = 128
HGRN_DK = 128
D_FF = 2816
N_MEM = 256
XA_HEADS = 4
XA_HD = 256
POOL_WINDOWS = (2, 4, 8, 16)

SEG = 64
LEVELS = 7
PAD = 16

UNIT = 4096
RING = 5

GLR_AT = 1536

VECTORS = [("norm1_g", 1), ("norm2_g", 1), ("gla_norm_g", 1), ("gla_gate_b", 1), ("ffn1_norm_2", 2),
           ("mix_norm_2", 2), ("xa_norm_2", 2), ("mem_norm_2", 2), ("ffn2_norm_2", 2), ("hgrn_norm_2", 2),
           ("pool_scale_2", 2), ("lb_logits_2", 2)]
VECTOR_SIZE = {"gla_norm_g": 128, "gla_gate_b": 256, "hgrn_norm_2": 512, "pool_scale_2": 512, "lb_logits_2": 512}
ROWS = [("final_norm_g", D), ("final_norm_2", D), ("router_group_b", N_GROUPS), ("router_expert_b", N_EXPERTS)]


def vector_columns():
    at, start = 0, {}
    for name, layers in VECTORS:
        start[name] = at
        at += layers * VECTOR_SIZE.get(name, D) // P
    return start, at


def row_columns():
    at, start = 0, {}
    for name, size in ROWS:
        start[name] = at
        at += size
    return start, at


def shape_constants():
    row, col = np.arange(P)[:, None], np.arange(P)[None, :]
    parts = {}
    levels = [(row == col)]
    for level in range(1, LEVELS + 1):
        block, half = 1 << level, 1 << (level - 1)
        levels.append((row // block == col // block) & (row % block < half) & (col % block >= half))
    parts["levels"] = np.concatenate([m.astype(np.float32) for m in levels], axis=1)
    i = (np.arange(TT)[:, None, None] * P + np.arange(P)[None, :, None])
    j = np.arange(T)[None, None, :]
    back = i - j
    count = np.zeros(back.shape, np.int64)
    for window, dilation in DILATIONS:
        count += (back >= 0) & (back % dilation == 0) & (back <= window)
    log_count = np.where(count > 0, np.log(np.maximum(count, 1)), -1e30).astype(np.float32)
    parts["log_count"] = log_count.transpose(1, 0, 2).reshape(P, TT * T)
    token = np.arange(T)
    keep = np.tile((token % SEG != 0).astype(np.float32), 4)
    parts["keep"] = np.broadcast_to(keep, (P, 4 * T))
    share = np.concatenate([1.0 / np.minimum(token + 1, w) for w in POOL_WINDOWS]).astype(np.float32)
    parts["share"] = np.broadcast_to(share, (P, 4 * T))
    parts["index"] = np.broadcast_to(np.arange(SLOTS), (P, SLOTS))
    parts["before"] = row < col
    parts["partition"] = row.astype(np.float32)
    at, start = 0, {}
    for name, a in parts.items():
        start[name] = (at, a.shape[1])
        at += a.shape[1]
    return start, np.concatenate(list(parts.values()), axis=1).astype(np.float32)


class Engine:

    def __init__(self, semaphore, one_by_one=True):
        self.semaphore = semaphore
        self.one_by_one = one_by_one
        self.count = 0
        self.steps = []
        self.waited = {}

    def wait(self, *done):
        for semaphore, value in done:
            if self.waited.get(semaphore.name, 0) < value:
                self.waited[semaphore.name] = value
                self.steps.append(lambda e, s=semaphore, v=value: e.wait_ge(s, v))

    def quiet(self, make, *done):
        self.wait(*done)
        self.steps.append(make)

    def __call__(self, make, *done):
        self.wait(*done)
        if self.one_by_one and self.count:
            self.wait(self.last)
        self.count += 1
        self.steps.append(lambda e: make(e).then_inc(self.semaphore, 1))
        return (self.semaphore, self.count)

    def begin_branch(self):
        self.outside = (self.steps, self.count, dict(self.waited))
        self.steps = []

    def end_branch(self, number):
        body, after = self.steps, self.count
        self.steps, before, self.waited = self.outside

        def step(e):
            value = e.value_load(number, min_val=0, max_val=EXTRA)
            with e.If(value > 0):
                for inner in body:
                    inner(e)
            if after > before:
                with e.Else():
                    e.wait_ge(self.semaphore, before)
                    e.sem_inc(self.semaphore, after - before)
        self.steps.append(step)

    @property
    def last(self):
        return (self.semaphore, self.count)

    def emit(self, e):
        for step in self.steps:
            step(e)


class Bank:

    def __init__(self, ap):
        self.ap = ap
        self.free = ()


class Stream:

    def __init__(self, slots, semaphores, branch_semaphores):
        self.slots = slots
        self.semaphores = {False: semaphores, True: branch_semaphores}
        self.sources = []
        self.in_branch = []
        self.released = []
        self.branch = False

    def arrival(self, n):
        earlier = sum(self.in_branch[m] == self.in_branch[n] for m in range(n % RING, n, RING))
        return self.semaphores[self.in_branch[n]][n % RING], 16 * (earlier + 1)

    def take(self, source):
        n = len(self.sources)
        self.sources.append(source)
        self.in_branch.append(self.branch)
        self.released.append(None)
        return n, self.slots[n % RING], self.arrival(n)

    def load(self, dma, n, expert_number):
        source, slot = self.sources[n], self.slots[n % RING]
        semaphore = self.arrival(n)[0]
        if isinstance(source, tuple):
            w, j = source
            target = slot[:, :].rearrange("p (o a b) -> p o a b", o=1, a=w.shape[1] // P)
            dma.steps.append(lambda e: e.dma_start(
                target, w[bass.ds(expert_number(e, j), 1)].rearrange("o (t p) n -> p o t n", p=P))
                .then_inc(semaphore, 16))
        else:
            target = slot[:, 0:source.shape[1] * source.shape[2]].rearrange("p (a b) -> p a b", a=source.shape[1])
            dma.steps.append(lambda e: e.dma_start(target, source).then_inc(semaphore, 16))

    def plan(self, dma, planned=None, extra_expert=None):
        picked = {}

        def expert_number(e, j):
            if j not in picked:
                picked[j] = e.value_load(extra_expert[0:1, j:j + 1], min_val=0, max_val=N_EXPERTS - 1)
            return picked[j]

        for n in range(len(self.sources)):
            if self.in_branch[n] and not self.in_branch[n - 1]:
                dma.wait(planned)
                dma.begin_branch()
            m = n - RING
            while not self.in_branch[n] and m >= 0 and self.in_branch[m]:
                m -= RING
            if m >= 0:
                dma.wait(self.released[m])
            self.load(dma, n, expert_number)
            if self.in_branch[n] and not (n + 1 < len(self.sources) and self.in_branch[n + 1]):
                dma.wait(*(self.released[m] for m in range(n - RING + 1, n + 1)))
                dma.end_branch(extra_expert[0:1, EXTRA:EXTRA + 1])


def build(nc, a, out, limit=None):
    with ExitStack() as ctx:
        def sb(name, *shape):
            return ctx.enter_context(nc.sbuf_tensor(name, list(shape), F32))

        def sem(name):
            return ctx.enter_context(nc.semaphore(name))

        const_at, _ = a["constants_at"], None
        vec_at, n_vec = vector_columns()
        row_at, n_row = row_columns()

        ring = [sb(f"weights_{i}", P, UNIT) for i in range(RING)]
        constants = sb("constants", P, a["constants"].shape[1])
        vectors = sb("vectors", P, n_vec)
        rows = sb("rows", P, n_row)
        resid = sb("resid", P, TT, D)
        normed = sb("normed_T", P, DT, T)
        mix_T = sb("mix_T", P, DT, T)
        mem_T = mix_T
        q_T = sb("q_T", P, DT, T)
        k_T = sb("k_T", P, DT, T)
        v_tok = sb("v_tok", P, TT, D)
        work = sb("work", P, TT, D)
        scratch = [sb(f"scratch_{i}", P, 4 * (PAD + T)) for i in range(4)]
        gate_tok = sb("gate_tok", P, TT, 512)
        attn = sb("attn", P, 3, 512)
        w_router = sb("w_router", P, DT, N_LOGITS)
        w_lowrank = sb("w_lowrank", P, DT, LOWRANK)
        gate_w2 = sb("gate_w2", LOWRANK, 2 * P)
        pool_w = sb("pool_w", P, 4, P)
        lowrank_T = sb("lowrank_T", LOWRANK, T)
        gates = sb("gates", P, TT, N_EXPERTS)
        chosen = sb("chosen", P, TT, N_EXPERTS)
        ones = sb("ones", P, P)[:, :]
        plan = sb("plan", P, 160)
        slot_of = sb("slot_of", P, TT, BLOCKS)
        gate_of_block = sb("gate_of_block", P, TT, BLOCKS)
        extra_expert = ctx.enter_context(nc.sbuf_tensor("extra_expert", [1, EXTRA + 1], I32))
        work_T = scratch[0]
        stats = sb("stats", P, 64)
        route = sb("route", P, 256)
        lb = sb("lb", P, 32)
        picks = ctx.enter_context(nc.sbuf_tensor("picks", [P, 16], U32))

        banks = [Bank(ctx.enter_context(nc.psum_tensor(f"bank_{i}", [P, 512], F32))) for i in range(8)]
        y_banks, loose = banks[0:4], banks[4:8]

        act, dve, pool, sp = (Engine(sem(f"{n}_done")) for n in ("act", "dve", "pool", "sp"))
        pe = Engine(sem("pe_done"), one_by_one=False)
        slot_loaded = [sem(f"slot_loaded_{i}") for i in range(RING)]
        branch_loaded = [sem(f"branch_loaded_{i}") for i in range(RING)]
        small_loaded = sem("small_loaded")
        x_loaded = sem("x_loaded")
        mem_loaded = [sem(f"mem_loaded_{i}") for i in range(LAYERS)]
        pool_w_loaded = [sem(f"pool_w_loaded_{i}") for i in range(LAYERS)]
        stored = sem("stored")
        stream = Stream(ring, slot_loaded, branch_loaded)

        def const(name):
            at, size = const_at[name]
            return constants[:, at:at + size]

        ident = const("levels")[:, 0:P]

        def vector(name, layer=0):
            size = VECTOR_SIZE.get(name, D) // P
            at = vec_at[name] + layer * size
            return vectors[:, at:at + size]

        def row(name):
            return rows[:, row_at[name]:row_at[name] + dict(ROWS)[name]]

        turn = [0]

        def next_bank():
            turn[0] += 1
            return loose[turn[0] % 4]

        def tiles(ap):
            return ap.rearrange("p (a b) -> p a b", b=T)

        small = [(constants[:, :], a["constants"]), (vectors[:, :], a["vectors"]), (rows[:, :], a["rows"]),
                 (w_router[:, :, 0:N_GROUPS], a["router_group_w"][0].rearrange("(t p) n -> p t n", p=P)),
                 (w_router[:, :, N_GROUPS:], a["router_expert_w"][0].rearrange("(t p) n -> p t n", p=P)),
                 (w_lowrank[:, :, :],
                  a["w_in"][0, :, GLR_AT:GLR_AT + LOWRANK].rearrange("(t p) n -> p t n", p=P)),
                 (gate_w2[:, :], a["gla_gate_w2"][0])]
        act.steps.append(lambda e: e.dma_start(resid[:, :, :], a["x"][0].rearrange("(t p) n -> p t n", p=P))
                         .then_inc(x_loaded, 16))
        for target, source in small:
            act.steps.append(lambda e, t=target, s=source: e.dma_start(t, s).then_inc(small_loaded, 16))
        have_x = (x_loaded, 16)
        have_small = (small_loaded, 16 * len(small))


        def inverse_rms(src, at, ready, size=D):
            for t in range(TT):
                squares = act(lambda e, t=t: e.activation(scratch[3][:, 0:size], src[:, t, :], ACT.Square,
                                                          accum_out=stats[:, at + t:at + t + 1]), *ready)
            s = stats[:, at:at + TT]
            mean = dve(lambda e: e.tensor_scalar(s, s, 1.0 / size, EPS, ALU.mult, ALU.add), squares)
            inverse = dve(lambda e: e.reciprocal(s, s), mean)
            return act(lambda e: e.activation(s, s, ACT.Sqrt), inverse)

        def to_features(src, dst, gain, ready, n_tiles=DT, src_at=0, dst_at=0):
            done = []
            for k in range(0, n_tiles, 2):
                bank = next_bank()
                pe.wait(*ready, have_small, *bank.free)
                for j in range(2):
                    for t in range(TT):
                        at = (src_at + k + j) * P
                        turned = pe(lambda e, t=t, at=at, j=j, b=bank: e.transpose(
                            b.ap[:, j * T + t * P:j * T + (t + 1) * P], src[:, t, at:at + P], ident))
                if k % 4 == 0:
                    for j in range(2):
                        last = act(lambda e, k=k, j=j, b=bank: e.activation(
                            dst[:, dst_at + k + j, :], b.ap[:, j * T:(j + 1) * T], ACT.Copy,
                            scale=gain[:, k + j:k + j + 1]), turned)
                else:
                    for j in range(2):
                        last = dve(lambda e, k=k, j=j, b=bank: e.tensor_scalar(
                            dst[:, dst_at + k + j, :], b.ap[:, j * T:(j + 1) * T], gain[:, k + j:k + j + 1],
                            None, ALU.mult), turned)
                bank.free = (last,)
                done.append(last)
            return done[-2:]

        def norm_to_features(src, dst, gain, ready, at=0):
            rms = inverse_rms(src, at, ready)
            for t in range(TT):
                scaled = dve(lambda e, t=t: e.tensor_scalar(work[:, t, :], src[:, t, :], stats[:, at + t:at + t + 1],
                                                            None, ALU.mult), rms)
            return to_features(work, dst, gain, (scaled,))

        def columns(w, start):
            return w[:, start:start + 512].rearrange("(t p) n -> p t n", p=P)

        def features_out(source, src, ready, evacuate):
            n, slot, arrived = stream.take(source)
            w = slot[:, :].rearrange("p (t n) -> p t n", t=DT)
            for pair in range(2):
                bank = next_bank()
                pe.wait(*ready, arrived, *bank.free)
                for j in range(2):
                    at = (2 * pair + j) * P
                    for k in range(DT):
                        make = lambda e, k=k, at=at, j=j, b=bank: e.matmul(
                            b.ap[:, j * T:(j + 1) * T], w[:, k, at:at + P], src[:, k, :],
                            start=(k == 0), stop=(k == DT - 1))
                        if k < DT - 1:
                            pe.quiet(make)
                        else:
                            done = pe(make)
                bank.free = (evacuate(pair, bank.ap, done),)
            stream.released[n] = done
            return bank.free[0]

        def tokens_out(source, src, ready, evacuate):
            n, slot, arrived = stream.take(source)
            w = slot[:, :].rearrange("p (t n) -> p t n", t=DT)
            freed = []
            for t in range(TT):
                bank = next_bank()
                pe.wait(*ready, arrived, *bank.free)
                for k in range(DT):
                    make = lambda e, k=k, t=t, b=bank: e.matmul(
                        b.ap[:, :], src[:, k, t * P:(t + 1) * P], w[:, k, :], start=(k == 0), stop=(k == DT - 1))
                    if k < DT - 1:
                        pe.quiet(make)
                    else:
                        done = pe(make)
                bank.free = (evacuate(t, bank.ap, done),)
                freed.append(bank.free[0])
            stream.released[n] = done
            return freed

        def act_copy(dst, scale=1.0, func=ACT.Copy):
            return lambda i, bank, done: act(lambda e: e.activation(dst(i), bank[:, :], func, scale=scale), done)

        def dve_copy(dst):
            return lambda i, bank, done: dve(lambda e: e.tensor_copy(dst(i), bank[:, :]), done)

        def pair_of(dst, at=0):
            return lambda pair: dst[:, at + 2 * pair:at + 2 * pair + 2, :].rearrange("p a b -> p (a b)")

        def add_projection(w, src, ready):
            done = []
            for half in range(2):
                def add(t, bank, made, half=half):
                    r = resid[:, t, half * 512:(half + 1) * 512]
                    return dve(lambda e: e.tensor_tensor(r, bank[:, :], r, ALU.add), made)
                done += tokens_out(columns(w, half * 512), src, ready, add)
            return done[-1:]

        def swiglu(w13, w2_units, n_tiles, src, ready):
            hidden, silus = scratch[0], scratch[1]
            pending = []
            units = {}

            def second(f, ready_h, w2, last):
                unit, slot, arrived = w2
                pe.wait(ready_h, arrived)
                if f == 0:
                    for b in y_banks:
                        pe.wait(*b.free)
                at = (f % 4) * D
                for t in range(TT):
                    for half in range(2):
                        make = lambda e, t=t, half=half: e.matmul(
                            y_banks[2 * t + half].ap[:, :],
                            hidden[:, (f % 4) * T + t * P:(f % 4) * T + (t + 1) * P],
                            slot[:, at + half * 512:at + (half + 1) * 512],
                            start=(f == 0), stop=(f == n_tiles - 1))
                        if t == TT - 1 and half == 1:
                            done = pe(make)
                        else:
                            pe.quiet(make)
                read_h[f % 4] = (done,)
                if last:
                    stream.released[unit] = done
                return done

            read_h = {i: () for i in range(4)}
            for f in range(n_tiles):
                group, within = f // 4, f % 4
                last_of_group = within == 3 or f == n_tiles - 1
                if within == 0:
                    w1, w3 = (stream.take(s) for s in w13(group))
                    w2 = stream.take(w2_units(group))
                bank = next_bank()
                pe.wait(*ready, *bank.free)
                for j, (unit, slot, arrived) in enumerate((w1, w3)):
                    width = w13(group)[0].shape[2]
                    w = slot[:, 0:DT * width].rearrange("p (t n) -> p t n", t=DT)
                    pe.wait(arrived)
                    for k in range(DT):
                        make = lambda e, k=k, j=j, b=bank, w=w, within=within: e.matmul(
                            b.ap[:, j * T:(j + 1) * T], w[:, k, within * P:(within + 1) * P], src[:, k, :],
                            start=(k == 0), stop=(k == DT - 1))
                        if k < DT - 1:
                            pe.quiet(make)
                        else:
                            both = pe(make)
                    if last_of_group:
                        stream.released[unit] = both
                s = silus[:, (f % 4) * T:(f % 4 + 1) * T]
                h = hidden[:, (f % 4) * T:(f % 4 + 1) * T]
                silu = act(lambda e, b=bank, s=s: e.activation(s, b.ap[:, 0:T], ACT.Silu), both,
                           *read_h[f % 4])
                product = dve(lambda e, b=bank, s=s, h=h: e.tensor_tensor(
                    h, s, b.ap[:, T:2 * T], ALU.mult), silu)
                bank.free = (product,)
                pending.append((f, product, w2, last_of_group))
                if len(pending) > 1:
                    second(*pending.pop(0))
            return second(*pending.pop(0))

        def add_y(done, scale):
            for t in range(TT):
                for half in range(2):
                    r = resid[:, t, half * 512:(half + 1) * 512]
                    b = y_banks[2 * t + half]
                    added = dve(lambda e, r=r, b=b: e.scalar_tensor_tensor(r, b.ap[:, :], scale, r, ALU.mult,
                                                                           ALU.add), done)
                    b.free = (added,)
            return (added,)

        def softmax_rows(score_bank, scored, at, scale, log_count=None):
            p = probs[at % 2]
            top = stats[:, 8 + 4 * (at % 2):10 + 4 * (at % 2)]
            den = stats[:, 10 + 4 * (at % 2):12 + 4 * (at % 2)]
            if log_count is not None:
                s = dve(lambda e, scale=scale: e.scalar_tensor_tensor(p, score_bank.ap[:, :], scale, log_count, ALU.mult,
                                                         ALU.add), scored, *prob_free[at % 2])
                source, scale = p, 1.0
                score_bank.free = (s,)
            else:
                s, source = scored, score_bank.ap[:, :]
            largest = dve(lambda e: e.tensor_reduce(top, tiles(source), AX.X, ALU.max, negate=True), s,
                          *prob_free[at % 2])
            if scale != 1.0:
                largest = dve(lambda e: e.tensor_scalar(top, top, scale, None, ALU.mult), largest)
            for t in range(TT):
                ex = act(lambda e, t=t: e.activation(p[:, t * T:(t + 1) * T], source[:, t * T:(t + 1) * T],
                                                     ACT.Exp, bias=top[:, t:t + 1], scale=scale,
                                                     accum_out=den[:, t:t + 1]), largest)
            if log_count is None:
                score_bank.free = (ex,)
            inv = dve(lambda e: e.reciprocal(den, den), ex)
            return dve(lambda e: e.tensor_tensor(tiles(p), tiles(p), den.unsqueeze(2).broadcast_to([P, TT, T]),
                                                 ALU.mult), inv)

        probs = [scratch[2][:, 0:512], scratch[2][:, 512:1024]]
        prob_free = [(), ()]
        probs_T = [scratch[1][:, 0:512], scratch[1][:, 512:1024]]
        probs_T_free = [(), ()]

        def turn_probs(p_ready, at):
            bank = next_bank()
            pe.wait(p_ready, *bank.free)
            for kt in range(TT):
                for t in range(TT):
                    turned = pe(lambda e, kt=kt, t=t, b=bank: e.transpose(
                        b.ap[:, kt * T + t * P:kt * T + (t + 1) * P],
                        probs[at % 2][:, t * T + kt * P:t * T + (kt + 1) * P], ident))
            prob_free[at % 2] = (turned,)
            copied = act(lambda e, b=bank: e.activation(probs_T[at % 2], b.ap[:, :], ACT.Copy), turned,
                         *probs_T_free[at % 2])
            bank.free = (copied,)
            return copied

        def linear_attention(dk, n_q, q_ready, v_ready, gate_ready, norm_gain, q_at=0, v_at=0):
            n = n_q * T
            b = scratch[0][:, 0:n]
            arg, xq, xk = scratch[1][:, 0:n], scratch[2][:, 0:n], scratch[3][:, 0:n]
            q = q_T[:, q_at:q_at + n_q, :].rearrange("p a b -> p (a b)")
            k = k_T[:, q_at:q_at + n_q, :].rearrange("p a b -> p (a b)")
            cleared = dve(lambda e: e.memset(xq, 0.0), *q_ready)
            cleared = dve(lambda e: e.memset(xk, 0.0))
            xq_free, arg_free = (), ()
            evacuated = None

            def scores(xq, xk, ready, level):
                blocks = [(0, 0, 0), (1, 1, 1)] if level <= LEVELS else [(2, 0, 1)]
                for target, jt, it in blocks:
                    bank = next_bank()
                    pe.wait(*ready, *bank.free)
                    for n_h, h in enumerate(sorted(range(LIN_HEADS), key=lambda h: h * dk % P)):
                        tile, part = h * dk // P, h * dk % P
                        if part and n_h == LIN_HEADS // 2:
                            pe.wait(pe.last)
                        done = pe(lambda e, h=h, tile=tile, part=part, jt=jt, it=it, bk=bank: e.matmul(
                            bk.ap[:, h * P:(h + 1) * P],
                            xk[part:part + dk, tile * T + jt * P:tile * T + (jt + 1) * P],
                            xq[part:part + dk, tile * T + it * P:tile * T + (it + 1) * P],
                            start=True, stop=True))
                    dst = attn[:, target, :].rearrange("p (h i) -> p h i", h=LIN_HEADS)
                    src = bank.ap[:, :].rearrange("p (h i) -> p h i", h=LIN_HEADS)
                    if level <= LEVELS:
                        mask = const("levels")[:, level * P:(level + 1) * P].unsqueeze(1)\
                            .broadcast_to([P, LIN_HEADS, P])
                    if level == 0:
                        got = dve(lambda e, d=dst, s=src, m=mask: e.tensor_tensor(d, s, m, ALU.mult), done)
                    elif level <= LEVELS:
                        got = dve(lambda e, d=dst, s=src, m=mask: e.copy_predicated(d, m.bitcast(U32), s),
                                  done, got_by[target])
                    else:
                        got = dve(lambda e, d=dst, s=src: e.tensor_copy(d, s), done)
                    got_by[target] = got
                    bank.free = (got,)
                return done

            got_by = {}
            scores(q, k, q_ready, 0)
            def level_factors(level, arg_free, xq_free):
                half = 1 << (level - 1)
                if level <= LEVELS - 1:
                    split = lambda x: x.rearrange("p (m s) -> p m s", s=2 * half)
                    first = lambda x: split(x)[:, :, 0:half]
                    later = lambda x: split(x)[:, :, half:2 * half]
                    mid = split(b)[:, :, half - 1:half].broadcast_to([P, n // (2 * half), half])
                    a1 = dve(lambda e, f=first, m=mid: e.tensor_tensor(f(arg), m, f(b), ALU.subtract),
                             *q_ready, *arg_free)
                    a2 = dve(lambda e, l=later, m=mid: e.tensor_tensor(l(arg), l(b), m, ALU.subtract))
                elif level == LEVELS:
                    split = lambda x: x.rearrange("p (m s) -> p m s", s=2 * SEG)
                    first = lambda x: split(x)[:, :, 0:SEG]
                    later = lambda x: split(x)[:, :, SEG:2 * SEG]
                    end = first(b)[:, :, SEG - 1:SEG].broadcast_to([P, n // (2 * SEG), SEG])
                    a1 = dve(lambda e: e.tensor_tensor(first(arg), end, first(b), ALU.subtract), *arg_free)
                    a2 = dve(lambda e: e.tensor_copy(later(arg), later(b)))
                else:
                    seg = lambda x: x.rearrange("p (m c s) -> p m c s", c=4, s=SEG)
                    split = lambda x: x.rearrange("p (m s) -> p m s", s=T)
                    first = lambda x: split(x)[:, :, 0:P]
                    later = lambda x: split(x)[:, :, P:T]
                    total = lambda c: seg(b)[:, :, c, SEG - 1:SEG].broadcast_to([P, n_q, SEG])
                    t0 = dve(lambda e: e.tensor_tensor(seg(arg)[:, :, 0, :], total(0), seg(b)[:, :, 0, :],
                                                       ALU.subtract), *arg_free)
                    dve(lambda e: e.tensor_tensor(seg(arg)[:, :, 0, :], seg(arg)[:, :, 0, :], total(1), ALU.add),
                        t0)
                    dve(lambda e: e.tensor_tensor(seg(arg)[:, :, 1, :], total(1), seg(b)[:, :, 1, :],
                                                  ALU.subtract))
                    dve(lambda e: e.tensor_copy(seg(arg)[:, :, 2, :], seg(b)[:, :, 2, :]))
                    a2 = dve(lambda e: e.tensor_tensor(seg(arg)[:, :, 3, :], seg(b)[:, :, 3, :], total(2),
                                                       ALU.add))
                ex = act(lambda e: e.activation(arg, arg, ACT.Exp), a2)
                r1 = dve(lambda e, l=later: e.tensor_tensor(l(xq), l(q), l(arg), ALU.mult), ex, *xq_free)
                r2 = pool(lambda e, f=first: e.tensor_tensor(f(xk), f(k), f(arg), ALU.mult), ex, cleared,
                          *xq_free)
                return (r1, r2), (scores(xq, xk, (r1, r2), level),)

            for level in range(1, LEVELS + 2):
                arg_free, xq_free = level_factors(level, arg_free, xq_free)

            v = v_tok
            outs = []
            for t in range(TT):
                bank = next_bank()
                pe.wait(*got_by.values(), *v_ready, *bank.free)
                for h in range(LIN_HEADS):
                    pieces = [(0, 0)] if t == 0 else [(2, 0), (1, 1)]
                    for i, (block, jt) in enumerate(pieces):
                        done = pe(lambda e, h=h, block=block, jt=jt, i=i, last=len(pieces) - 1, bk=bank: e.matmul(
                            bk.ap[:, h * P:(h + 1) * P], attn[:, block, h * P:(h + 1) * P],
                            v[:, jt, v_at + h * LIN_DV:v_at + (h + 1) * LIN_DV], start=(i == 0),
                            stop=(i == last)))
                outs.append((bank, done))
            s = stats[:, 16:16 + TT * LIN_HEADS]
            for t, (bank, done) in enumerate(outs):
                square = act(lambda e, t=t, bk=bank: e.activation(work[:, t, 0:512], bk.ap[:, :], ACT.Square), done)
                gated = dve(lambda e, t=t, bk=bank: e.tensor_tensor(work[:, t, 512:D], bk.ap[:, :],
                                                                    gate_tok[:, t, :], ALU.mult),
                            square, *gate_ready)
                bank.free = (gated,)
                summed = dve(lambda e, t=t: e.tensor_reduce(
                    s[:, t * LIN_HEADS:(t + 1) * LIN_HEADS],
                    work[:, t, 0:512].rearrange("p (h v) -> p h v", h=LIN_HEADS), AX.X, ALU.add), square)
            mean = dve(lambda e: e.tensor_scalar(s, s, 1.0 / LIN_DV, EPS, ALU.mult, ALU.add), summed)
            inverse = dve(lambda e: e.reciprocal(s, s), mean)
            rms = act(lambda e: e.activation(s, s, ACT.Sqrt), inverse)
            for t in range(TT):
                o = work[:, t, 512:D].rearrange("p (h v) -> p h v", h=LIN_HEADS)
                r = s[:, t * LIN_HEADS:(t + 1) * LIN_HEADS].unsqueeze(2).broadcast_to([P, LIN_HEADS, LIN_DV])
                scaled = dve(lambda e, o=o, r=r: e.tensor_tensor(o, o, r, ALU.mult), rms)
            return to_features(work, mix_T, norm_gain, (scaled,), n_tiles=4, src_at=4, dst_at=0)

        def log_sigmoid(z, tmp, ready):
            t1 = act(lambda e: e.activation(tmp, z, ACT.Abs), *ready)
            t2 = act(lambda e: e.activation(tmp, tmp, ACT.Exp, scale=-1.0), t1)
            t3 = act(lambda e: e.activation(tmp, tmp, ACT.Ln, bias=1.0), t2)
            return t3, lambda dst: dve(lambda e: e.scalar_tensor_tensor(dst, z, 0.0, tmp, ALU.min, ALU.subtract),
                                       t3)

        def running_sum(values, dst, n, ready):
            return dve(lambda e: e.tensor_tensor_scan(dst, const("keep")[:, 0:n], values, 0.0, ALU.mult, ALU.add),
                       ready)

        dve(lambda e: e.memset(ones, 1.0))
        plan_ready = []

        def gla_and_attention():
            n_T = norm_to_features(resid, normed, vector("norm1_g"), (have_x, have_small))
            w = a["w_in"][0]
            bank = next_bank()
            pe.wait(*n_T, *bank.free)
            for k in range(DT):
                low = pe(lambda e, k=k, b=bank: e.matmul(b.ap[0:LOWRANK, 0:T], w_lowrank[:, k, :],
                                                         normed[:, k, :], start=(k == 0), stop=(k == DT - 1)))
            low = act(lambda e, b=bank: e.activation(lowrank_T[:, :], b.ap[0:LOWRANK, 0:T], ACT.Copy), low)
            bank.free = (low,)
            bank = next_bank()
            pe.wait(low, *bank.free)
            for j in range(2):
                made = pe(lambda e, j=j, b=bank: e.matmul(b.ap[:, j * T:(j + 1) * T],
                                                          gate_w2[:, j * P:(j + 1) * P], lowrank_T[:, :],
                                                          start=True, stop=True))
            z = scratch[1][:, 0:2 * T]
            for j in range(2):
                zed = dve(lambda e, j=j, b=bank: e.tensor_scalar(
                    z[:, j * T:(j + 1) * T], b.ap[:, j * T:(j + 1) * T], vector("gla_gate_b")[:, j:j + 1], None,
                    ALU.add), made)
            bank.free = (zed,)
            _, finish = log_sigmoid(z, scratch[2][:, 0:2 * T], (zed,))
            la = finish(scratch[1][:, 0:2 * T])
            la = dve(lambda e: e.tensor_scalar(z, z, 1.0 / GLA_TAU, None, ALU.mult), la)
            b_ready = running_sum(z, scratch[0][:, 0:2 * T], 2 * T, la)

            def q_and_k(pair, bank, done):
                dst = (q_T if pair == 0 else k_T)[:, 4:6, :].rearrange("p a b -> p (a b)")
                return act(lambda e: e.activation(dst, bank[:, :], ACT.Copy,
                                                  scale=GLA_DK ** -0.5 if pair == 0 else 1.0), done)
            qk = features_out(columns(w, 0), normed, n_T, q_and_k)
            v = tokens_out(columns(w, 512), normed, n_T, act_copy(lambda t: v_tok[:, t, 0:512]))
            gate = tokens_out(columns(w, 1024), normed, n_T, act_copy(lambda t: gate_tok[:, t, :], func=ACT.Silu))
            at = GLR_AT + LOWRANK
            aq = features_out(columns(w, at), normed, n_T, act_copy(pair_of(q_T)))
            ak = features_out(columns(w, at + 512), normed, n_T, dve_copy(pair_of(k_T)))
            av = tokens_out(columns(w, at + 1024), normed, n_T, act_copy(lambda t: v_tok[:, t, 512:D]))
            gla = linear_attention(GLA_DK, 2, (qk, b_ready), v, gate,
                                   vector("gla_norm_g").broadcast_to([P, 4]), q_at=4)
            log_count = const("log_count")
            for i in range(2):
                prob_free[i] = (pe.last, dve.last, pool.last)
                probs_T_free[i] = (pe.last, dve.last, pool.last)
            out_bank = None
            for h in range(ATT_HEADS):
                tile, part = h // 2, (h % 2) * ATT_HD
                bank = next_bank()
                pe.wait(aq, ak, *bank.free)
                for t in range(TT):
                    scored = pe(lambda e, t=t, tile=tile, part=part, b=bank: e.matmul(
                        b.ap[:, t * T:(t + 1) * T], q_T[part:part + ATT_HD, tile, t * P:(t + 1) * P],
                        k_T[part:part + ATT_HD, tile, :], start=True, stop=True))
                p_ready = softmax_rows(bank, scored, h, ATT_HD ** -0.5, log_count)
                p_T = turn_probs(p_ready, h)
                if h % 2 == 0:
                    out_bank = next_bank()
                    pe.wait(*out_bank.free)
                pe.wait(p_T, *av)
                pt = tiles(probs_T[h % 2])
                dst = out_bank.ap[part:part + ATT_HD, 0:T]
                for jt in range(TT):
                    done = pe(lambda e, jt=jt, h=h, pt=pt, dst=dst: e.matmul(
                        dst, v_tok[:, jt, 512 + h * ATT_HD:512 + (h + 1) * ATT_HD], pt[:, jt, :],
                        start=(jt == 0), stop=(jt == TT - 1)))
                probs_T_free[h % 2] = (done,)
                if h % 2:
                    put = dve(lambda e, b=out_bank, h=h: e.tensor_copy(mix_T[:, 4 + h // 2, :], b.ap[:, 0:T]), done)
                    out_bank.free = (put,)
            return add_projection(a["w_out"][0], mix_T, (*gla, put))

        def route_tokens(n_T):
            for t in range(TT):
                bank = next_bank()
                pe.wait(*n_T, have_small, *bank.free)
                for k in range(DT):
                    done = pe(lambda e, k=k, t=t, b=bank: e.matmul(
                        b.ap[:, 0:N_LOGITS], normed[:, k, t * P:(t + 1) * P], w_router[:, k, :],
                        start=(k == 0), stop=(k == DT - 1)))
                r = route[:, t * 128:(t + 1) * 128]
                logits, group8, top8, hot = r[:, 0:36], r[:, 36:44], r[:, 44:52], r[:, 52:56]
                spread, top2, pick1, pick2, one = r[:, 56:88], r[:, 88:96], r[:, 96:104], r[:, 104:112], r[:, 112:128]
                bias = rows[:, row_at["router_group_b"]:row_at["router_group_b"] + N_LOGITS]
                g = gates[:, t, :].rearrange("p (g e) -> p g e", g=N_GROUPS)
                experts = logits[:, N_GROUPS:].rearrange("p (g e) -> p g e", g=N_GROUPS)
                sp3 = spread.rearrange("p (g e) -> p g e", g=N_GROUPS)
                index = const("index")[:, 0:PER_GROUP]
                pk = picks[:, t * 8:(t + 1) * 8]

                def step(make, *more):
                    return dve(make, dve.last, *more)

                read = dve(lambda e, b=bank, l=logits, bi=bias: e.tensor_tensor(l, b.ap[:, 0:N_LOGITS], bi,
                                                                               ALU.add), done)
                bank.free = (read,)
                step(lambda e, x=group8: e.memset(x, -3.0e38))
                step(lambda e, x=group8, l=logits: e.tensor_copy(x[:, 0:N_GROUPS], l[:, 0:N_GROUPS]))
                step(lambda e, o=top8, x=group8: e.max(o, x))
                step(lambda e, o=pk, m=top8, x=group8: e.max_index(o, m, x))
                step(lambda e, o=one, x=pk: e.tensor_copy(o[:, 0:8], x))
                step(lambda e, o=hot, x=one, i=index: e.tensor_scalar(o, i[:, 0:N_GROUPS], x[:, 0:1], None,
                                                                      ALU.is_equal))
                neg = step(lambda e, o=one, m=top8: e.tensor_scalar(o[:, 8:9], m[:, 0:1], -1.0, None, ALU.mult))
                ex = act(lambda e, o=one, l=logits, s=spread: e.activation(
                    s[:, 0:N_GROUPS], l[:, 0:N_GROUPS], ACT.Exp, bias=o[:, 8:9], accum_out=o[:, 9:10]), neg)
                step(lambda e, o=one: e.reciprocal(o[:, 10:11], o[:, 9:10]), ex)
                step(lambda e, o=sp3, x=experts, hh=hot: e.tensor_tensor(
                    o, x, hh.unsqueeze(2).broadcast_to([P, N_GROUPS, PER_GROUP]), ALU.mult))
                step(lambda e, o=group8, s=sp3: e.tensor_reduce(o, s.rearrange("p g e -> p e g"), AX.X, ALU.add))
                step(lambda e, o=top2, x=group8: e.max(o, x))
                step(lambda e, o=pk, m=top2, x=group8: e.max_index(o, m, x))
                step(lambda e, o=one, x=pk: e.tensor_copy(o[:, 0:8], x))
                diff = step(lambda e, o=one, m=top2: e.tensor_tensor(o[:, 11:12], m[:, 1:2], m[:, 0:1],
                                                                     ALU.subtract))
                ex = act(lambda e, o=one: e.activation(o[:, 12:13], o[:, 11:12], ACT.Exp), diff)
                step(lambda e, o=one: e.tensor_scalar(o[:, 13:14], o[:, 12:13], 1.0, None, ALU.add), ex)
                step(lambda e, o=one: e.reciprocal(o[:, 14:15], o[:, 13:14]))
                step(lambda e, o=one: e.tensor_tensor(o[:, 14:15], o[:, 14:15], o[:, 10:11], ALU.mult))
                step(lambda e, o=one: e.tensor_tensor(o[:, 15:16], o[:, 14:15], o[:, 12:13], ALU.mult))
                step(lambda e, o=pick1, x=one, i=index: e.tensor_scalar(o, i, x[:, 0:1], x[:, 14:15],
                                                                        ALU.is_equal, ALU.mult))
                step(lambda e, o=pick2, x=one, i=index: e.tensor_scalar(o, i, x[:, 1:2], x[:, 15:16],
                                                                        ALU.is_equal, ALU.mult))
                step(lambda e, o=pick1, x=pick2: e.tensor_tensor(o, o, x, ALU.add))
                step(lambda e, o=pick2, x=one, i=index: e.tensor_scalar(o, i, x[:, 0:1], None, ALU.is_equal))
                step(lambda e, o=top2, x=one, i=index: e.tensor_scalar(o, i, x[:, 1:2], None, ALU.is_equal))
                step(lambda e, o=pick2, x=top2: e.tensor_tensor(o, o, x, ALU.add))
                step(lambda e, o=chosen[:, t, :].rearrange("p (g e) -> p g e", g=N_GROUPS), x=pick2, hh=hot:
                     e.tensor_tensor(o, x.unsqueeze(1).broadcast_to([P, N_GROUPS, PER_GROUP]),
                                     hh.unsqueeze(2).broadcast_to([P, N_GROUPS, PER_GROUP]), ALU.mult))
                last = step(lambda e, o=g, x=pick1, hh=hot: e.tensor_tensor(
                    o, x.unsqueeze(1).broadcast_to([P, N_GROUPS, PER_GROUP]),
                    hh.unsqueeze(2).broadcast_to([P, N_GROUPS, PER_GROUP]), ALU.mult))
            return last

        def plan_blocks(routed):
            before_me, index, number = const("before"), const("index"), const("partition")
            rank = next_bank()
            pe.wait(routed, *rank.free)
            for t in range(TT):
                pieces = [(before_me, 0)] if t == 0 else [(ones, 0), (before_me, 1)]
                for i, (which, jt) in enumerate(pieces):
                    ranked = pe(lambda e, t=t, i=i, w=which, jt=jt, n=len(pieces): e.matmul(
                        rank.ap[:, t * N_EXPERTS:(t + 1) * N_EXPERTS], w, chosen[:, jt, :],
                        start=(i == 0), stop=(i == n - 1)))
            for t in range(TT):
                counted = pe(lambda e, t=t: e.matmul(rank.ap[0:N_EXPERTS, 2 * N_EXPERTS:2 * N_EXPERTS + 1],
                                                     chosen[:, t, :], ones[:, 0:1], start=(t == 0),
                                                     stop=(t == TT - 1)))
            place = plan[:, 0:2 * N_EXPERTS].rearrange("p (t e) -> p t e", t=TT)
            by_expert = plan[0:N_EXPERTS, 64:128]
            count, more, tmp, start = (by_expert[:, i:i + 1] for i in range(4))
            placed = dve(lambda e: e.scalar_tensor_tensor(
                place, rank.ap[:, 0:2 * N_EXPERTS].rearrange("p (t e) -> p t e", t=TT), 1.0, chosen[:, :, :],
                ALU.add, ALU.mult), counted)
            dve(lambda e: e.tensor_scalar(slot_of[:, :, 0:N_EXPERTS], place, -1.0, None, ALU.add))
            dve(lambda e: e.tensor_copy(gate_of_block[:, :, 0:N_EXPERTS], gates[:, :, :]))
            read = dve(lambda e: e.tensor_copy(count, rank.ap[0:N_EXPERTS, 2 * N_EXPERTS:2 * N_EXPERTS + 1]))
            rank.free = (read,)
            dve(lambda e: e.tensor_scalar(more, count, float(SLOTS), None, ALU.is_gt))
            for k in range(2, T // SLOTS):
                dve(lambda e, k=k: e.tensor_scalar(tmp, count, float(k * SLOTS), None, ALU.is_gt))
                got = dve(lambda e: e.tensor_tensor(more, more, tmp, ALU.add))
            bank = next_bank()
            begun = pe(lambda e, b=bank: e.matmul(b.ap[0:N_EXPERTS, 0:1], before_me[0:N_EXPERTS, 0:N_EXPERTS], more,
                                                  start=True, stop=True), got, *bank.free)
            owns, shift, tmp7 = (plan[0:N_EXPERTS, 128 + 8 * i:128 + 8 * i + EXTRA] for i in range(3))
            back = dve(lambda e, b=bank: e.tensor_copy(start, b.ap[0:N_EXPERTS, 0:1]), begun)
            bank.free = (back,)
            dve(lambda e: e.tensor_scalar(shift, index[0:N_EXPERTS, 0:EXTRA], start, None, ALU.subtract))
            dve(lambda e: e.tensor_scalar(owns, shift, 0.0, None, ALU.is_ge))
            dve(lambda e: e.tensor_scalar(tmp7, shift, more, None, ALU.is_lt))
            dve(lambda e: e.tensor_tensor(owns, owns, tmp7, ALU.mult))
            dve(lambda e: e.tensor_scalar(shift, shift, 1.0, float(SLOTS), ALU.add, ALU.mult))
            owned = dve(lambda e: e.tensor_tensor(shift, shift, owns, ALU.mult))
            bank = next_bank()
            pe.wait(owned, *bank.free)
            for t in range(TT):
                turned = pe(lambda e, t=t, b=bank: e.transpose(b.ap[0:N_EXPERTS, t * P:(t + 1) * P], place[:, t, :],
                                                               ident))
            for t in range(TT):
                turned = pe(lambda e, t=t, b=bank: e.transpose(b.ap[0:N_EXPERTS, T + t * P:T + (t + 1) * P],
                                                               gates[:, t, :], ident))
            both_T = work_T[0:N_EXPERTS, 0:2 * T]
            got = dve(lambda e, b=bank: e.tensor_copy(both_T, b.ap[0:N_EXPERTS, 0:2 * T]), turned)
            bank.free = (got,)
            bank = next_bank()
            pe.wait(got, *bank.free)
            for i in range(2 * TT):
                pe(lambda e, i=i, b=bank: e.matmul(b.ap[:, i * 8:i * 8 + EXTRA], both_T[:, i * P:(i + 1) * P], owns,
                                                   start=True, stop=True))
            pe(lambda e, b=bank: e.matmul(b.ap[:, 32:32 + EXTRA], ones[0:N_EXPERTS, :], shift, start=True,
                                          stop=True))
            pe(lambda e, b=bank: e.matmul(b.ap[0:1, 40:40 + EXTRA], number[0:N_EXPERTS, :], owns,
                                          start=True, stop=True))
            made = pe(lambda e, b=bank: e.matmul(b.ap[0:1, 40 + EXTRA:41 + EXTRA], ones[0:N_EXPERTS, 0:1], more,
                                                 start=True, stop=True))
            b = bank
            shifts = plan[:, 152:152 + EXTRA]
            dve(lambda e: e.tensor_scalar(shifts, b.ap[:, 32:32 + EXTRA], 1.0, None, ALU.add), made)
            for t in range(TT):
                dve(lambda e, t=t: e.tensor_tensor(slot_of[:, t, N_EXPERTS:], b.ap[:, t * 8:t * 8 + EXTRA], shifts,
                                                   ALU.subtract))
                dve(lambda e, t=t: e.tensor_copy(gate_of_block[:, t, N_EXPERTS:],
                                                 b.ap[:, (TT + t) * 8:(TT + t) * 8 + EXTRA]))
            done = dve(lambda e: e.tensor_copy(extra_expert[:, :], b.ap[0:1, 40:41 + EXTRA]))
            bank.free = (done,)
            return done

        def experts(before):
            n_T = norm_to_features(resid, normed, vector("norm2_g"), before)
            routed = route_tokens(n_T)
            planned = plan_blocks(routed)
            plan_ready.extend((planned, extra_expert))
            gain = vector("norm2_g").unsqueeze(2).broadcast_to([P, DT, SLOTS])
            index = const("index")
            gather_bank, hidden_bank, out_banks = loose[0], loose[1], loose[2:4]
            w1, w3, w2 = a["expert_w1"][0], a["expert_w3"][0], a["expert_w2"][0]
            tokens_of = [q_T[:, 0:2, :], q_T[:, 2:4, :]]
            silu_of = [k_T[:, 0, :], k_T[:, 1, :]]
            hidden_of = [k_T[:, 2, :], k_T[:, 3, :]]
            hot_of = [scratch[2][:, 512 * i:512 * i + 256].rearrange("p (t s) -> p t s", t=TT) for i in range(2)]
            gated_of = [scratch[2][:, 512 * i + 256:512 * i + 512].rearrange("p (t s) -> p t s", t=TT)
                        for i in range(2)]
            back_of = [scratch[3][:, 256 * i:256 * i + 256] for i in range(2)]
            result_of = [v_tok[:, 0, :], v_tok[:, 1, :]]
            start_of = pe.last
            gathered, hot_ready, hidden_ready = {}, {}, {}
            hot_read, back_ready, back_read, result_ready = {}, {}, {}, {}

            def expert_weight(w, b):
                return w[b].rearrange("(t p) n -> p t n", p=P) if b < N_EXPERTS else (w, b - N_EXPERTS)

            def size_of(pair):
                return 2 if 2 * pair + 1 < BLOCKS else 1

            def one_hot(pair):
                waits = [planned, start_of] + ([hot_read[pair - 2]] if pair >= 2 else [])
                for i in range(size_of(pair)):
                    b = 2 * pair + i
                    for t in range(TT):
                        s = slice(i * SLOTS, (i + 1) * SLOTS)
                        pool(lambda e, t=t, s=s, b=b: e.tensor_scalar(
                            hot_of[pair % 2][:, t, s], index[:, :], slot_of[:, t, b:b + 1], None, ALU.is_equal),
                            *waits)
                        hot_ready[pair] = pool(lambda e, t=t, s=s, b=b: e.tensor_scalar(
                            gated_of[pair % 2][:, t, s], hot_of[pair % 2][:, t, s], gate_of_block[:, t, b:b + 1],
                            None, ALU.mult))

            def gather(b):
                pair, s = b // 2, slice(b % 2 * SLOTS, (b % 2 + 1) * SLOTS)
                pe.wait(hot_ready[pair], *gather_bank.free)
                for k in range(DT):
                    for t in range(TT):
                        done = pe(lambda e, k=k, t=t: e.matmul(
                            gather_bank.ap[:, k * SLOTS:(k + 1) * SLOTS], work[:, t, k * P:(k + 1) * P],
                            hot_of[pair % 2][:, t, s], start=(t == 0), stop=(t == TT - 1)))
                dst = tokens_of[b % 2].rearrange("p a b -> p (a b)").rearrange("p (k s) -> p k s", s=SLOTS)
                gathered[b] = dve(lambda e: e.tensor_tensor(
                    dst, gather_bank.ap[:, :].rearrange("p (k s) -> p k s", s=SLOTS), gain, ALU.mult), done)
                gather_bank.free = (gathered[b],)

            def up(b):
                x = tokens_of[b % 2].rearrange("p a b -> p (a b)").rearrange("p (k s) -> p k s", s=SLOTS)
                pe.wait(gathered[b], *hidden_bank.free)
                for i, (unit, slot, arrived) in enumerate([stream.take(expert_weight(w, b)) for w in (w1, w3)]):
                    w = slot[:, :].rearrange("p (t n) -> p t n", t=DT)
                    pe.wait(arrived)
                    for f in range(D_EXPERT // P):
                        for k in range(DT):
                            make = lambda e, i=i, f=f, k=k, w=w: e.matmul(
                                hidden_bank.ap[:, i * 256 + f * SLOTS:i * 256 + (f + 1) * SLOTS],
                                w[:, k, f * P:(f + 1) * P], x[:, k, :], start=(k == 0), stop=(k == DT - 1))
                            if k == DT - 1:
                                done = pe(make)
                            else:
                                pe.quiet(make)
                    stream.released[unit] = done
                s, h = silu_of[b % 2], hidden_of[b % 2]
                silu = act(lambda e: e.activation(s, hidden_bank.ap[:, 0:256], ACT.Silu), done)
                hidden_ready[b] = dve(lambda e: e.tensor_tensor(h, s, hidden_bank.ap[:, 256:512], ALU.mult), silu)
                hidden_bank.free = (hidden_ready[b],)

            def turn(pair):
                n = size_of(pair) * SLOTS
                pe.wait(hot_ready[pair], *gather_bank.free)
                for t in range(TT):
                    done = pe(lambda e, t=t: e.transpose(gather_bank.ap[0:n, t * P:(t + 1) * P],
                                                         gated_of[pair % 2][:, t, 0:n], ident))
                hot_read[pair] = done
                waits = [back_read[pair - 2]] if pair >= 2 else []
                back_ready[pair] = act(lambda e: e.activation(back_of[pair % 2][0:n, :], gather_bank.ap[0:n, 0:T],
                                                              ACT.Copy), done, *waits)
                gather_bank.free = (back_ready[pair],)

            def down(b):
                unit, slot, arrived = stream.take(expert_weight(w2, b))
                pair, at = b // 2, b % 2 * SLOTS
                pe.wait(hidden_ready[b], arrived)
                if b % 2 == 0:
                    pe.wait(*out_banks[0].free, *out_banks[1].free)
                for f in range(D_EXPERT // P):
                    for half in range(2):
                        done = pe(lambda e, f=f, half=half: e.matmul(
                            out_banks[half].ap[at:at + SLOTS, :], hidden_of[b % 2][:, f * SLOTS:(f + 1) * SLOTS],
                            slot[:, f * D + half * 512:f * D + (half + 1) * 512],
                            start=(f == 0), stop=(f == D_EXPERT // P - 1)))
                stream.released[unit] = done
                if b % 2 == 1 or b == BLOCKS - 1:
                    n = at + SLOTS
                    waits = [back_read[pair - 2]] if pair >= 2 else []
                    r = result_of[pair % 2]
                    c0 = act(lambda e: e.activation(r[0:n, 0:512], out_banks[0].ap[0:n, :], ACT.Copy), done, *waits)
                    c1 = dve(lambda e: e.tensor_copy(r[0:n, 512:D], out_banks[1].ap[0:n, :]), done, *waits)
                    out_banks[0].free, out_banks[1].free = (c0,), (c1,)
                    result_ready[pair] = (c0, c1)

            def scatter(pair):
                n = size_of(pair) * SLOTS
                pe.wait(back_ready[pair], *result_ready[pair])
                if pair == 0:
                    for b in y_banks:
                        pe.wait(*b.free)
                for t in range(TT):
                    for half in range(2):
                        done = pe(lambda e, t=t, half=half: e.matmul(
                            y_banks[2 * t + half].ap[:, :], back_of[pair % 2][0:n, t * P:(t + 1) * P],
                            result_of[pair % 2][0:n, half * 512:(half + 1) * 512],
                            start=(pair == 0), stop=(2 * pair + 2 == N_EXPERTS or 2 * pair + 2 > BLOCKS),
                            skip_group_check=True))
                back_read[pair] = done
                return done

            def run(first, last):
                one_hot(first // 2)
                gather(first)
                for b in range(first, last):
                    if b % 2 == 0 and b + 2 < last:
                        one_hot(b // 2 + 1)
                    if b + 1 < last:
                        gather(b + 1)
                    up(b)
                    if b % 2 == 1:
                        turn(b // 2)
                        if b > first + 2:
                            scatter(b // 2 - 1)
                    if b > first:
                        down(b - 1)
                down(last - 1)
                if last % 2:
                    turn(last // 2)
                    scatter(last // 2 - 1)
                return scatter((last - 1) // 2)

            for bank in loose:
                pe.wait(*bank.free)
            run(0, N_EXPERTS)
            engines = (pe, act, dve, pool)
            for engine in engines:
                engine.wait(planned)
                engine.begin_branch()
            stream.branch = True
            y = run(N_EXPERTS, BLOCKS)
            stream.branch = False
            for engine in engines:
                engine.end_branch(extra_expert[0:1, EXTRA:EXTRA + 1])
            return add_y(y, 1.0)

        def norm_tokens(gain, before, dst):
            rms = inverse_rms(resid, 0, before)
            for t in range(TT):
                done = dve(lambda e, t=t: e.scalar_tensor_tensor(dst[:, t, :], resid[:, t, :], stats[:, t:t + 1],
                                                                 gain, ALU.mult, ALU.mult), rms)
            return (done,)

        def ffn(which, layer, before):
            n_T = norm_to_features(resid, normed, vector(f"{which}_norm_2", layer), before)
            w1, w3, w2 = (a[f"{which}_{m}_2"][layer] for m in ("w1", "w3", "w2"))

            def cut(w, g):
                return w[:, g * 512:min(D_FF, (g + 1) * 512)].rearrange("(t p) n -> p t n", p=P)
            y = swiglu(lambda g: (cut(w1, g), cut(w3, g)),
                       lambda g: w2[g * 512:min(D_FF, (g + 1) * 512), :].rearrange("(t p) n -> p t n", p=P),
                       D_FF // P, normed, n_T)
            return add_y(y, 0.5)

        def lower_bounds():
            l0, l1 = vector("lb_logits_2", 0), vector("lb_logits_2", 1)
            top, e0, e1, d0, d1 = (lb[:, 4 * i:4 * i + 4] for i in range(2, 7))
            m = dve(lambda e: e.tensor_tensor(top, l0, l1, ALU.max), have_small)
            dve(lambda e: e.tensor_tensor(d0, l0, top, ALU.subtract), m)
            d = dve(lambda e: e.tensor_tensor(d1, l1, top, ALU.subtract))
            act(lambda e: e.activation(e0, d0, ACT.Exp), d)
            x = act(lambda e: e.activation(e1, d1, ACT.Exp))
            s = dve(lambda e: e.tensor_tensor(e0, e0, e1, ALU.add), x)
            ln = act(lambda e: e.activation(e0, e0, ACT.Ln), s)
            dve(lambda e: e.tensor_tensor(lb[:, 0:4], d1, e0, ALU.subtract), ln)
            return dve(lambda e: e.tensor_tensor(lb[:, 4:8], d0, e0, ALU.subtract))

        def hgrn_and_pool(layer, before):
            n_T = norm_to_features(resid, normed, vector("mix_norm_2", layer), before)
            w = a["w_in_2"][layer]
            loaded = (pool_w_loaded[layer], 16)
            sp_wait = dve.last
            act.wait(pe.last)
            act.steps.append(lambda e: e.dma_start(pool_w[:, :, :], a["pool_w_2"][layer].rearrange("g c d -> c g d"))
                             .then_inc(pool_w_loaded[layer], 16))
            q = features_out(columns(w, 0), normed, n_T, act_copy(pair_of(q_T)))
            z4 = scratch[1][:, 0:4 * T]
            zed = features_out(columns(w, 512), normed, n_T, dve_copy(
                lambda pair: z4[:, pair * 512:(pair + 1) * 512]))
            v = tokens_out(columns(w, 1024), normed, n_T, act_copy(lambda t: v_tok[:, t, 0:512]))
            gate = tokens_out(columns(w, 1536), normed, n_T, act_copy(lambda t: gate_tok[:, t, :], func=ACT.Silu))
            u, wa, wb = (x[:, :].rearrange("p (g t) -> p g t", g=4) for x in (scratch[0], scratch[2], scratch[3]))
            pads = [dve(lambda e, x=x: e.memset(x[:, :, 0:PAD], 0.0)) for x in (u, wa, wb)]
            up = features_out(columns(w, 2048), normed, n_T, lambda pair, bank, done: dve(
                lambda e: e.tensor_copy(u[:, 2 * pair:2 * pair + 2, PAD:], bank[:, :].rearrange(
                    "p (a b) -> p a b", b=T)), done))

            def shifted(dst, src, g0, by, ready):
                return dve(lambda e: e.tensor_tensor(dst[:, g0:, PAD:], src[:, g0:, PAD:],
                                                     src[:, g0:, PAD - by:PAD + T - by], ALU.add), ready)
            last = shifted(wa, u, 0, 1, up)
            last = shifted(wb, wa, 1, 2, last)
            last = shifted(wa, wb, 2, 4, last)
            last = shifted(wb, wa, 3, 8, last)
            share = const("share").rearrange("p (g t) -> p g t", g=4)
            pooled = k_T[:, 4:8, :]
            for g in range(4):
                s = (wa, wb, wa, wb)[g]
                mean = dve(lambda e, g=g, s=s: e.tensor_tensor(pooled[:, g, :], s[:, g, PAD:], share[:, g, :],
                                                               ALU.mult), last)
            less = dve(lambda e: e.tensor_tensor(pooled, pooled, u[:, :, PAD:], ALU.subtract), mean)
            for pair in range(2):
                bank = next_bank()
                pe.wait(less, loaded, *bank.free)
                for j in range(2):
                    g = 2 * pair + j
                    made = pe(lambda e, g=g, j=j, b=bank: e.matmul(b.ap[:, j * T:(j + 1) * T], pool_w[:, g, :],
                                                                   pooled[:, g, :], start=True, stop=True))
                for j in range(2):
                    g = 2 * pair + j
                    put = dve(lambda e, g=g, j=j, b=bank: e.tensor_scalar(
                        mix_T[:, 4 + g, :], b.ap[:, j * T:(j + 1) * T],
                        vector("pool_scale_2", layer)[:, g:g + 1], None, ALU.mult), made)
                bank.free = (put,)
            tmp, logf = scratch[2][:, 0:4 * T], scratch[3][:, 0:4 * T]
            _, finish = log_sigmoid(z4, tmp, (zed, less))
            lsz = finish(logf)
            km = dve(lambda e: e.tensor_tensor(tmp, logf, z4, ALU.subtract), lsz)
            k4 = k_T[:, 0:4, :].rearrange("p a b -> p (a b)")
            if layer == 0:
                keys = act(lambda e: e.activation(k4, tmp, ACT.Exp), km)
                b_ready = running_sum(logf, scratch[0][:, 0:4 * T], 4 * T, lsz)
            else:
                for j in range(4):
                    keys = act(lambda e, j=j: e.activation(k4[:, j * T:(j + 1) * T], tmp[:, j * T:(j + 1) * T],
                                                           ACT.Exp, bias=lb[:, 4 + j:5 + j]), km)
                larger = scratch[0][:, 0:4 * T]
                for j in range(4):
                    c = slice(j * T, (j + 1) * T)
                    x1 = dve(lambda e, j=j, c=c: e.tensor_scalar(logf[:, c], logf[:, c], lb[:, 4 + j:5 + j], None,
                                                                 ALU.add), km)
                    dve(lambda e, j=j, c=c: e.tensor_scalar(larger[:, c], logf[:, c], lb[:, j:j + 1], None,
                                                            ALU.max), x1)
                    x2 = dve(lambda e, j=j, c=c: e.tensor_scalar(logf[:, c], logf[:, c], lb[:, j:j + 1], None,
                                                                 ALU.subtract))
                act(lambda e: e.activation(logf, logf, ACT.Abs), x2)
                act(lambda e: e.activation(logf, logf, ACT.Exp, scale=-1.0), act.last)
                ln = act(lambda e: e.activation(logf, logf, ACT.Ln, bias=1.0), act.last)
                whole = dve(lambda e: e.tensor_tensor(logf, logf, larger, ALU.add), ln)
                b_ready = running_sum(logf, scratch[0][:, 0:4 * T], 4 * T, whole)
            heads = linear_attention(HGRN_DK, 4, (q, keys, b_ready), v, gate, vector("hgrn_norm_2", layer))
            return add_projection(a["w_out_2"][layer], mix_T, (*heads, put))

        def cross_attention(layer, before):
            act.wait(*before)
            act.steps.append(lambda e: e.dma_start(v_tok[:, :, :], a["mem_2"][0].rearrange("(t p) n -> p t n", p=P))
                             .then_inc(mem_loaded[layer], 16))
            m_T = norm_to_features(v_tok, mem_T, vector("mem_norm_2", layer), ((mem_loaded[layer], 16),), at=2)
            n_T = norm_to_features(resid, normed, vector("xa_norm_2", layer), (*before, *m_T))
            wq, wkv = a["xa_wq_2"][layer], a["xa_wkv_2"][layer]
            for i in range(2):
                k_ready = features_out(columns(wkv, 512 * i), mem_T, m_T, dve_copy(pair_of(k_T, 4 * i)))
            for i in range(2):
                v_ready = tokens_out(columns(wkv, D + 512 * i), mem_T, m_T,
                                     act_copy(lambda t, i=i: v_tok[:, t, 512 * i:512 * (i + 1)]))
            for i in range(2):
                q_ready = features_out(columns(wq, 512 * i), normed, n_T, act_copy(pair_of(q_T, 4 * i)))
            for i in range(2):
                prob_free[i] = (pe.last, dve.last, act.last)
                probs_T_free[i] = (pe.last, dve.last, act.last)
            for h in range(XA_HEADS):
                bank = next_bank()
                pe.wait(q_ready, k_ready, *bank.free)
                for t in range(TT):
                    for j in range(2):
                        scored = pe(lambda e, t=t, j=j, h=h, b=bank: e.matmul(
                            b.ap[:, t * T:(t + 1) * T], q_T[:, 2 * h + j, t * P:(t + 1) * P], k_T[:, 2 * h + j, :],
                            start=(j == 0), stop=(j == 1)))
                p_ready = softmax_rows(bank, scored, h, XA_HD ** -0.5)
                p_T = turn_probs(p_ready, h)
                bank = next_bank()
                pe.wait(p_T, *v_ready, *bank.free)
                pt = tiles(probs_T[h % 2])
                for j in range(2):
                    for mt in range(TT):
                        done = pe(lambda e, j=j, mt=mt, h=h, pt=pt, b=bank: e.matmul(
                            b.ap[:, j * T:(j + 1) * T],
                            v_tok[:, mt, h * XA_HD + j * P:h * XA_HD + (j + 1) * P], pt[:, mt, :],
                            start=(mt == 0), stop=(mt == TT - 1)))
                probs_T_free[h % 2] = (done,)
                put = dve(lambda e, h=h, b=bank: e.tensor_copy(
                    mix_T[:, 2 * h:2 * h + 2, :].rearrange("p a b -> p (a b)"), b.ap[:, :]), done)
                bank.free = (put,)
            return add_projection(a["xa_wo_2"][layer], mix_T, (put,))

        done = (have_x,)
        steps = [lambda d: gla_and_attention(), experts,
                 lambda d: norm_tokens(row("final_norm_g"), (*d, lower_bounds()), resid)]
        for layer in range(LAYERS):
            steps += [lambda d, l=layer: ffn("ffn1", l, d), lambda d, l=layer: hgrn_and_pool(l, d),
                      lambda d, l=layer: cross_attention(l, d), lambda d, l=layer: ffn("ffn2", l, d)]
        if limit is not None:
            steps = steps[:limit]
        for step in steps:
            done = step(done)
        result = resid
        if limit is None:
            done = norm_tokens(row("final_norm_2"), done, work)
            result = work
        stream.plan(sp, *plan_ready)
        sp.wait(*done)
        sp.steps.append(lambda e: e.dma_start(out[0].rearrange("(t p) n -> p t n", p=P), result[:, :, :])
                        .then_inc(stored, 16))
        sp.wait((stored, 16))

        block = ctx.enter_context(nc.Block())
        block.sync(sp.emit)
        block.scalar(act.emit)
        block.tensor(pe.emit)
        block.vector(dve.emit)
        block.gpsimd(pool.emit)


DIRECT = ["x", "w_in", "gla_gate_w2", "w_out", "router_group_w", "router_expert_w", "expert_w1", "expert_w3",
          "expert_w2", "mem_2", "ffn1_w1_2", "ffn1_w3_2", "ffn1_w2_2", "w_in_2", "pool_w_2", "w_out_2", "xa_wq_2",
          "xa_wkv_2", "xa_wo_2", "ffn2_w1_2", "ffn2_w3_2", "ffn2_w2_2"]


def kernel(**inputs):
    import concourse.bacc as bacc
    from concourse.bass_utils import run_bass_kernel_spmd

    nc = bacc.Bacc("TRN2", target_bir_lowering=False, num_devices=1)
    arrays = {name: np.ascontiguousarray(inputs[name]) for name in DIRECT}
    arrays["vectors"] = np.ascontiguousarray(
        np.concatenate([np.asarray(inputs[name]).reshape(-1, P) for name, _ in VECTORS]).T)
    row = np.concatenate([np.asarray(inputs[name]).reshape(-1) for name, _ in ROWS])
    arrays["rows"] = np.ascontiguousarray(np.broadcast_to(row, (P, row.size)))
    start, arrays["constants"] = shape_constants()
    a = {name: nc.dram_tensor(f"in_{name}", v.shape, mybir.dt.from_np(v.dtype), kind="ExternalInput").ap()
         for name, v in arrays.items()}
    a["constants_at"] = start
    out = nc.dram_tensor("out_0", (1, T, D), F32, kind="ExternalOutput").ap()
    build(nc, a, out)
    result = run_bass_kernel_spmd(nc, [{f"in_{name}": v for name, v in arrays.items()}], core_ids=[0])
    return result.results[0]["out_0"]
```

```python
from contextlib import ExitStack
from itertools import chain

import numpy as np

import concourse.bass as bass
from concourse import mybir

F32 = mybir.dt.float32
F32R = mybir.dt.float32r
U32 = mybir.dt.uint32
I32 = mybir.dt.int32
ALU = mybir.AluOpType
ACT = mybir.ActivationFunctionType
AX = mybir.AxisListType

P = 128
T = 256
TT = T // P
D = 1024
DT = D // P
EPS = 1e-6

GLA_DK = 64
GLA_TAU = 16.0
LOWRANK = 16
ATT_HEADS = 8
ATT_HD = 64
DILATIONS = ((128, 1), (512, 4), (2048, 16))
N_GROUPS = 4
PER_GROUP = 8
N_EXPERTS = N_GROUPS * PER_GROUP
N_LOGITS = N_GROUPS + N_EXPERTS
D_EXPERT = 512
TOP_K = 2
SLOTS = 64
EXTRA = (TOP_K * T - 1) // (SLOTS + 1)
BLOCKS = N_EXPERTS + EXTRA

LAYERS = 2
LIN_HEADS = 4
LIN_DV = 128
HGRN_DK = 128
D_FF = 2816
N_MEM = 256
XA_HEADS = 4
XA_HD = 256
POOL_WINDOWS = (2, 4, 8, 16)

SEG = 64
LEVELS = 7
PAD = 16

UNIT = 2048
CHUNK = UNIT // 2
RING = 6
CHUNKS = 5
AHEAD = CHUNKS - 1

GLR_AT = 1536

VECTORS = [("norm1_g", 1), ("norm2_g", 1), ("gla_norm_g", 1), ("gla_gate_b", 1), ("ffn1_norm_2", 2),
           ("mix_norm_2", 2), ("xa_norm_2", 2), ("mem_norm_2", 2), ("ffn2_norm_2", 2), ("hgrn_norm_2", 2),
           ("pool_scale_2", 2), ("lb_logits_2", 2)]
VECTOR_SIZE = {"gla_norm_g": 128, "gla_gate_b": 256, "hgrn_norm_2": 512, "pool_scale_2": 512, "lb_logits_2": 512}


def vector_columns():
    at, start = 0, {}
    for name, layers in VECTORS:
        start[name] = at
        at += layers * VECTOR_SIZE.get(name, D) // P
    return start, at


def shape_constants():
    row, col = np.arange(P)[:, None], np.arange(P)[None, :]
    parts = {}
    levels = [(row == col)]
    for level in range(1, LEVELS + 1):
        block, half = 1 << level, 1 << (level - 1)
        levels.append((row // block == col // block) & (row % block < half) & (col % block >= half))
    parts["levels"] = np.concatenate([m.astype(np.float32) for m in levels], axis=1)
    i = (np.arange(TT)[:, None, None] * P + np.arange(P)[None, :, None])
    j = np.arange(T)[None, None, :]
    back = i - j
    count = np.zeros(back.shape, np.int64)
    for window, dilation in DILATIONS:
        count += (back >= 0) & (back % dilation == 0) & (back <= window)
    log_count = np.where(count > 0, np.log(np.maximum(count, 1)), -1e30).astype(np.float32)
    parts["log_count"] = log_count.transpose(1, 0, 2).reshape(P, TT * T)
    token = np.arange(T)
    parts["keep"] = np.broadcast_to((token % SEG != 0).astype(np.float32), (P, T))
    share = np.concatenate([1.0 / np.minimum(token[:PAD] + 1, w) for w in POOL_WINDOWS]).astype(np.float32)
    parts["share"] = np.broadcast_to(share, (P, len(POOL_WINDOWS) * PAD))
    parts["index"] = np.broadcast_to(np.arange(SLOTS), (P, SLOTS))
    parts["before"] = row < col
    parts["partition"] = row.astype(np.float32)
    at, start = 0, {}
    for name, a in parts.items():
        start[name] = (at, a.shape[1])
        at += a.shape[1]
    return start, np.concatenate(list(parts.values()), axis=1).astype(np.float32)


class Engine:

    def __init__(self, semaphore, one_by_one=True):
        self.semaphore = semaphore
        self.one_by_one = one_by_one
        self.count = 0
        self.steps = []
        self.waited = {}

    def wait(self, *done):
        for semaphore, value in done:
            if self.waited.get(semaphore.name, 0) < value:
                self.waited[semaphore.name] = value
                self.steps.append(lambda e, s=semaphore, v=value: e.wait_ge(s, v))

    def quiet(self, make, *done):
        self.wait(*done)
        self.steps.append(make)

    def __call__(self, make, *done):
        self.wait(*done)
        if self.one_by_one and self.count:
            self.wait(self.last)
        self.count += 1
        self.steps.append(lambda e: make(e).then_inc(self.semaphore, 1))
        return (self.semaphore, self.count)

    def begin_branch(self):
        self.outside = (self.steps, self.count, dict(self.waited))
        self.steps = []

    def end_branch(self, number):
        body, after = self.steps, self.count
        self.steps, before, self.waited = self.outside

        def step(e):
            value = e.value_load(number, min_val=0, max_val=EXTRA)
            with e.If(value > 0):
                for inner in body:
                    inner(e)
            if after > before:
                with e.Else():
                    e.wait_ge(self.semaphore, before)
                    e.sem_inc(self.semaphore, after - before)
        self.steps.append(step)

    @property
    def last(self):
        return (self.semaphore, self.count)

    def emit(self, e):
        for step in self.steps:
            step(e)


class Bank:

    def __init__(self, ap):
        self.ap = ap
        self.free = ()


class Split:

    def __init__(self, hi, lo):
        self.hi = hi
        self.lo = lo

    def __getitem__(self, at):
        return Split(self.hi[at], self.lo[at])


def expert_half(w, half):
    if w.shape[1] == D:
        return w[:, :, half * 256:(half + 1) * 256].rearrange("o (t p) n -> p o t n", p=P)
    return w[:, half * 256:(half + 1) * 256, :].rearrange("o (t p) n -> p o t n", p=P)


class Unit:

    def __init__(self, source, by_columns):
        self.source = source
        self.by_columns = by_columns
        self.n = None

    def chunk(self, slot, i):
        if self.by_columns:
            return slot.rearrange("p (t n) -> p t n", t=DT)[:, :, i * P:(i + 1) * P]
        return slot[:, i * CHUNK:(i + 1) * CHUNK]


def column_units(w, start, stop):
    return [Unit(w[:, at:min(stop, at + 256)].rearrange("(t p) n -> p t n", p=P), True)
            for at in range(start, stop, 256)]


def row_units(w, start, stop):
    return [Unit(w[at:at + 512, column:column + 512].rearrange("(t p) n -> p t n", p=P), False)
            for column in range(start, stop, 512) for at in range(0, D, 512)]


def output_units(w, halves):
    return [Unit(w[512 * rows:512 * (rows + 1), column:column + 512].rearrange("(t p) n -> p t n", p=P), False)
            for rows in halves for column in (0, 512)]


def both_chunks(units):
    return [(unit, i) for unit in units for i in range(2)]


def swiglu_chunks(w1, w3, w2):
    n = w1.shape[1] // P
    up = [column_units(w, 0, w.shape[1]) for w in (w1, w3)]
    down = [Unit(w2[at:at + 256, :].rearrange("(t p) n -> p t n", p=P), False) for at in range(0, w1.shape[1], 256)]
    order = []
    for f in range(n):
        order += [(up[0][f // 2], f % 2), (up[1][f // 2], f % 2)]
        if f:
            order.append((down[(f - 1) // 2], (f - 1) % 2))
    return order + [(down[(n - 1) // 2], (n - 1) % 2)]


def expert_chunks(w1, w3, w2):
    def down(pair):
        return [Unit(w2[e, at:at + 256, :].rearrange("(t p) n -> p t n", p=P), False)
                for e in (2 * pair, 2 * pair + 1) for at in range(0, D_EXPERT, 256)]

    order = []
    for pair in range(N_EXPERTS // 2):
        for e in (2 * pair, 2 * pair + 1):
            order += row_units(w1[e], 0, D_EXPERT) + row_units(w3[e], 0, D_EXPERT)
        if pair:
            order += down(pair - 1)
    return both_chunks(order + down(N_EXPERTS // 2 - 1))


class Splitter:

    SHARE = 4

    def __init__(self, stream, act, dve, pool, buffers, order):
        self.stream, self.act, self.dve, self.pool, self.buffers, self.order = stream, act, dve, pool, buffers, order
        self.ready = []
        self.used = []
        self.taken = 0

    def ahead(self):
        while len(self.ready) < min(self.taken + AHEAD, len(self.order)):
            n = len(self.ready)
            unit, i = self.order[n]
            if unit.n is None:
                unit.n, unit.slot, unit.arrived = self.stream.take(unit.source)
            hi, lo = self.buffers[n % CHUNKS].hi, self.buffers[n % CHUNKS].lo
            source = unit.chunk(unit.slot[:, :], i)
            if unit.by_columns:
                hi, lo = (x.rearrange("p (t n) -> p t n", t=DT) for x in (hi, lo))
            free = [self.used[n - CHUNKS]] if n >= CHUNKS else []
            rounded = self.act(lambda e, h=hi, s=source: e.activation(h, s, ACT.Copy), unit.arrived, *free)
            engine = self.pool if n % self.SHARE == self.SHARE - 1 else self.dve
            rest = engine(lambda e, h=hi, o=lo, s=source: e.tensor_tensor(o, s, h.bitcast(F32), ALU.subtract),
                          rounded)
            self.ready.append(rest)
            self.stream.released[unit.n] += (rest,)

    def take(self, by_columns):
        self.taken += 1
        self.ahead()
        n = self.taken - 1
        assert self.order[n][0].by_columns == by_columns and len(self.used) == n
        return self.buffers[n % CHUNKS], self.ready[n]

    def use(self, done):
        self.used.append(done)


class Stream:

    def __init__(self, slots, semaphores, branch_semaphores):
        self.slots = slots
        self.semaphores = {False: semaphores, True: branch_semaphores}
        self.sources = []
        self.in_branch = []
        self.released = []
        self.branch = False

    def arrival(self, n):
        earlier = sum(self.in_branch[m] == self.in_branch[n] for m in range(n % RING, n, RING))
        return self.semaphores[self.in_branch[n]][n % RING], 16 * (earlier + 1)

    def take(self, source):
        n = len(self.sources)
        self.sources.append(source)
        self.in_branch.append(self.branch)
        self.released.append(())
        return n, self.slots[n % RING], self.arrival(n)

    def load(self, dma, n, expert_number):
        source, slot = self.sources[n], self.slots[n % RING]
        semaphore = self.arrival(n)[0]
        if isinstance(source, tuple):
            w, j, half = source
            target = slot[:, :].rearrange("p (o a b) -> p o a b", o=1, a=DT if w.shape[1] == D else 2)
            dma.steps.append(lambda e: e.dma_start(
                target, expert_half(w[bass.ds(expert_number(e, j), 1)], half)).then_inc(semaphore, 16))
        else:
            target = slot[:, 0:source.shape[1] * source.shape[2]].rearrange("p (a b) -> p a b", a=source.shape[1])
            dma.steps.append(lambda e: e.dma_start(target, source).then_inc(semaphore, 16))

    def plan(self, dma, planned=None, extra_expert=None):
        picked = {}

        def expert_number(e, j):
            if j not in picked:
                picked[j] = e.value_load(extra_expert[0:1, j:j + 1], min_val=0, max_val=N_EXPERTS - 1)
            return picked[j]

        for n in range(len(self.sources)):
            if self.in_branch[n] and not self.in_branch[n - 1]:
                dma.wait(planned)
                dma.begin_branch()
            m = n - RING
            while not self.in_branch[n] and m >= 0 and self.in_branch[m]:
                m -= RING
            if m >= 0:
                dma.wait(*self.released[m])
            self.load(dma, n, expert_number)
            if self.in_branch[n] and not (n + 1 < len(self.sources) and self.in_branch[n + 1]):
                dma.wait(*(done for m in range(n - RING + 1, n + 1) for done in self.released[m]))
                dma.end_branch(extra_expert[0:1, EXTRA:EXTRA + 1])


def build(nc, a, out):
    with ExitStack() as ctx:
        def sb(name, *shape):
            return ctx.enter_context(nc.sbuf_tensor(name, list(shape), F32))

        def sem(name):
            return ctx.enter_context(nc.semaphore(name))

        const_at = a["constants_at"]
        vec_at, n_vec = vector_columns()

        ring = [sb(f"weights_{i}", P, UNIT) for i in range(RING)]
        constants = sb("constants", P, a["constants"].shape[1])
        vectors = sb("vectors", P, n_vec)
        logit_bias = sb("logit_bias", P, N_LOGITS)
        resid = sb("resid", P, TT, D)

        def split(name, *shape):
            return Split(*(ctx.enter_context(nc.sbuf_tensor(f"{name}_{part}", list(shape), F32R))
                           for part in ("hi", "lo")))

        chunks = [split(f"chunk_{i}", P, CHUNK)[:, :] for i in range(CHUNKS)]
        normed = split("normed_T", P, DT, T)
        mix_T = split("mix_T", P, DT, T)
        mem_T = normed
        q_T = sb("q_T", P, DT, T)
        k_T = sb("k_T", P, DT, T)
        v_tok = sb("v_tok", P, TT, D)
        work = k_T[:, :, :].rearrange("p a b -> p (a b)").rearrange("p (t n) -> p t n", t=TT)
        scratch = [sb(f"scratch_{i}", P, 4 * (PAD + T)) for i in range(4)]
        gate_tok = sb("gate_tok", P, TT, 512)
        attn = sb("attn", P, 3, 512)
        gain_row = gate_tok[:, :, :].rearrange("p a b -> p (a b)")
        norm_room = gain_row
        w_small = scratch[0][:, 0:DT * (N_LOGITS + LOWRANK)].rearrange("p (t n) -> p t n", t=DT)
        result_split = split("result", P, D)[:, :]
        back_split = [ctx.enter_context(nc.sbuf_tensor(f"back_{i}", [P, T], F32R))[:, :] for i in range(2)]
        small_split = split("w_small", P, DT, N_LOGITS + LOWRANK)
        hot_split = [x[:, :, :].rearrange("p a b -> p (a b)")[:, 0:TT * P].rearrange("p (t s) -> p t s", t=TT)
                     for x in (small_split.hi, small_split.lo)]
        w_router, w_lowrank = small_split[:, :, 0:N_LOGITS], small_split[:, :, N_LOGITS:]
        gate_w2 = sb("gate_w2", LOWRANK, 2 * P)
        pool_w = sb("pool_w", P, 4, P)
        lowrank_T = sb("lowrank_T", LOWRANK, T)
        gates = sb("gates", P, TT, N_EXPERTS)
        chosen = sb("chosen", P, TT, N_EXPERTS)
        ones = sb("ones", P, P)[:, :]
        plan = scratch[1][:, 256:416]
        slot_of = sb("slot_of", P, TT, BLOCKS)
        gate_of_block = sb("gate_of_block", P, TT, BLOCKS)
        extra_expert = ctx.enter_context(nc.sbuf_tensor("extra_expert", [1, EXTRA + 1], I32))
        work_T = scratch[0]
        stats = sb("stats", P, 64)
        route = scratch[1][:, 0:256]
        lb = sb("lb", P, 32)
        picks = ctx.enter_context(nc.sbuf_tensor("picks", [P, 16], U32))

        banks = [Bank(ctx.enter_context(nc.psum_tensor(f"bank_{i}", [P, 512], F32))) for i in range(8)]
        y_banks, loose = banks[0:4], banks[4:8]

        mem_tok = work
        hidden_split = mix_T[:, 0:2, :]
        work_split = Split(*(x[:, :, :].rearrange("p a b -> p (a b)").rearrange("p (t n) -> p t n", t=TT)
                             for x in (mix_T.hi, mix_T.lo)))

        act, dve, pool, sp = (Engine(sem(f"{n}_done")) for n in ("act", "dve", "pool", "sp"))
        pe = Engine(sem("pe_done"), one_by_one=False)
        slot_loaded = [sem(f"slot_loaded_{i}") for i in range(RING)]
        branch_loaded = [sem(f"branch_loaded_{i}") for i in range(RING)]
        first_loaded = sem("first_loaded")
        small_loaded = sem("small_loaded")
        x_loaded = sem("x_loaded")
        mem_loaded = [sem(f"mem_loaded_{i}") for i in range(LAYERS)]
        pool_w_loaded = [sem(f"pool_w_loaded_{i}") for i in range(LAYERS)]
        gain_loaded = sem("gain_loaded")
        stored = sem("stored")
        stream = Stream(ring, slot_loaded, branch_loaded)

        def const(name):
            at, size = const_at[name]
            return constants[:, at:at + size]

        ident = const("levels")[:, 0:P]

        def vector(name, layer=0):
            size = VECTOR_SIZE.get(name, D) // P
            at = vec_at[name] + layer * size
            return vectors[:, at:at + size]

        turn = [0]

        def next_bank():
            turn[0] += 1
            return loose[turn[0] % 4]

        def tiles(ap):
            return ap.rearrange("p (a b) -> p a b", b=T)

        first = [(constants[:, 0:P], a["constants"][:, 0:P]), (vectors[:, :], a["vectors"])]
        small = [(constants[:, P:], a["constants"][:, P:]), (logit_bias[:, :], a["logit_bias"]),
                 (w_small[:, :, 0:N_GROUPS], a["router_group_w"][0].rearrange("(t p) n -> p t n", p=P)),
                 (w_small[:, :, N_GROUPS:N_LOGITS], a["router_expert_w"][0].rearrange("(t p) n -> p t n", p=P)),
                 (w_small[:, :, N_LOGITS:],
                  a["w_in"][0, :, GLR_AT:GLR_AT + LOWRANK].rearrange("(t p) n -> p t n", p=P)),
                 (gate_w2[:, :], a["gla_gate_w2"][0])]
        act.steps.append(lambda e: e.dma_start(resid[:, :, :], a["x"][0].rearrange("(t p) n -> p t n", p=P))
                         .then_inc(x_loaded, 16))
        for target, source in first:
            act.steps.append(lambda e, t=target, s=source: e.dma_start(t, s).then_inc(first_loaded, 16))
        for target, source in small:
            act.steps.append(lambda e, t=target, s=source: e.dma_start(t, s).then_inc(small_loaded, 16))
        have_x = (x_loaded, 16)
        have_small = (first_loaded, 16 * len(first))
        have_rest = (small_loaded, 16 * len(small))


        def inverse_rms(src, at, ready, room, size=D):
            for t in range(TT):
                squares = act(lambda e, t=t: e.activation(room[:, 0:size], src[:, t, :], ACT.Square,
                                                          accum_out=stats[:, at + t:at + t + 1]),
                              *(ready if t else ready[:1]))
            s = stats[:, at:at + TT]
            mean = dve(lambda e: e.tensor_scalar(s, s, 1.0 / size, EPS, ALU.mult, ALU.add), squares)
            inverse = dve(lambda e: e.reciprocal(s, s), mean)
            return act(lambda e: e.activation(s, s, ACT.Sqrt), inverse)

        def put_split(made, *puts):
            for dst, source, scale in puts:
                hi = act(lambda e, d=dst, s=source, c=scale: e.activation(d.hi, s, ACT.Copy, scale=c), made)
            for dst, source, scale in puts:
                lo = dve(lambda e, d=dst, s=source, c=scale: e.scalar_tensor_tensor(
                    d.lo, s, c, d.hi.bitcast(F32), ALU.mult, ALU.subtract), hi)
            return lo

        def to_features(src, dst, gain, ready, n_tiles=DT, src_at=0, dst_at=0, scales=None):
            lasts = []
            for k in range(0, n_tiles, 2):
                bank = next_bank()
                pe.wait(*ready, have_small, *bank.free)
                for j in range(2):
                    for t in range(TT):
                        at = (src_at + k + j) * P
                        if scales is None:
                            turned = pe(lambda e, t=t, at=at, j=j, b=bank: e.transpose(
                                b.ap[:, j * T + t * P:j * T + (t + 1) * P], src[:, t, at:at + P], ident))
                        else:
                            turned = pe(lambda e, t=t, at=at, j=j, b=bank: e.matmul(
                                b.ap[:, j * T + t * P:j * T + (t + 1) * P], src[:, t, at:at + P], scales[t],
                                start=True, stop=True))
                last = put_split(turned, *((dst[:, dst_at + k + j, :], bank.ap[:, j * T:(j + 1) * T],
                                            gain[:, k + j:k + j + 1]) for j in range(2)))
                bank.free = (last,)
                lasts += [last, last]
            return lasts

        def diagonals(src, ready, at, room):
            rms = inverse_rms(src, at, ready, room)
            scales = [room[:, t * P:(t + 1) * P] for t in range(TT)]
            for t in range(TT):
                scaled = dve(lambda e, t=t: e.tensor_scalar(scales[t], ident, stats[:, at + t:at + t + 1],
                                                            None, ALU.mult), rms, have_small)
            return scales, scaled

        def norm_to_features(src, dst, gain, ready, at=0):
            scales, scaled = diagonals(src, ready, at, norm_room)
            return to_features(src, dst, gain, (scaled,), scales=scales)

        def three_passes(out_ap, lhs, rhs, first, last):
            passes = [(lhs.hi, rhs.hi), (lhs.hi, rhs.lo), (lhs.lo, rhs.hi)]
            for i, (left, right) in enumerate(passes):
                pe.quiet(lambda e, l=left, r=right, i=i: e.matmul(out_ap, l, r, start=(first and i == 0),
                                                                  stop=(last and i == len(passes) - 1)))

        def signalled():
            make = pe.steps.pop()
            return pe(make)

        def features_in_steps(n_tiles, src, ready, evacuate, banks, result):
            for pair in range(n_tiles // 2):
                bank = banks(pair)
                pe.wait(*bank.free)
                for j in range(2):
                    chunk, split_done = splitter.take(True)
                    w = Split(*(x.rearrange("p (t n) -> p t n", t=DT) for x in (chunk.hi, chunk.lo)))
                    pe.wait(split_done)
                    for k in range(DT):
                        pe.wait(ready[k])
                        three_passes(bank.ap[:, j * T:(j + 1) * T], w[:, k, :], src[:, k, :], k == 0, k == DT - 1)
                    done = signalled()
                    splitter.use(done)
                    if j == 0:
                        yield
                bank.free = (evacuate(pair, bank.ap, done),)
                if pair < n_tiles // 2 - 1:
                    yield
            result.append(bank.free[0])
            yield

        def features_out(n_tiles, src, ready, evacuate):
            result = []
            for _ in features_in_steps(n_tiles, src, ready, evacuate, lambda pair: next_bank(), result):
                pass
            return result[0]

        def tokens_in_steps(src, ready, evacuate, outs, result):
            pe.wait(*outs[0].free, *outs[1].free)
            for pair in range(DT // 2):
                chunk, split_done = splitter.take(False)
                pe.wait(split_done)
                for t in range(TT):
                    for j in range(2):
                        k = 2 * pair + j
                        pe.wait(ready[k])
                        three_passes(outs[t].ap[:, :], src[:, k, t * P:(t + 1) * P], chunk[:, j * 512:(j + 1) * 512],
                                     k == 0, k == DT - 1)
                done = signalled()
                splitter.use(done)
                if pair < DT // 2 - 1:
                    yield
            for t, bank in enumerate(outs):
                bank.free = (evacuate(t, bank.ap, done),)
            result += [bank.free[0] for bank in outs]
            yield

        def tokens_out(src, ready, evacuate):
            result = []
            for _ in tokens_in_steps(src, ready, evacuate, [next_bank() for _ in range(TT)], result):
                pass
            return result

        def act_copy(dst, scale=1.0, func=ACT.Copy, free=()):
            return lambda i, bank, done: act(lambda e: e.activation(dst(i), bank[:, :], func, scale=scale), done,
                                             *free)

        def dve_copy(dst, free=()):
            return lambda i, bank, done: dve(lambda e: e.tensor_copy(dst(i), bank[:, :]), done, *free)

        def pair_of(dst, at=0):
            return lambda pair: dst[:, at + 2 * pair:at + 2 * pair + 2, :].rearrange("p a b -> p (a b)")

        def add_projection(src, ready):
            steps, done = projection_in_steps(src, ready, (0, 1))
            for _ in steps:
                pass
            return done

        def projection_in_steps(src, ready, halves):
            done = []

            def steps():
                for n, rows in enumerate(halves):
                    for column in range(2):
                        outs = y_banks[2 * column:2 * column + 2]
                        if n == 0:
                            pe.wait(*outs[0].free, *outs[1].free)
                        for pair in range(DT // 4):
                            chunk, split_done = splitter.take(False)
                            pe.wait(split_done)
                            for t in range(TT):
                                for j in range(2):
                                    k = 4 * rows + 2 * pair + j
                                    pe.wait(ready[k])
                                    three_passes(outs[t].ap[:, :], src[:, k, t * P:(t + 1) * P],
                                                 chunk[:, j * 512:(j + 1) * 512], n == 0 and pair == j == 0,
                                                 n == 1 and pair == j == 1)
                            made = signalled()
                            splitter.use(made)
                            if n == 0 or pair == 0:
                                yield
                        if n == 1:
                            for t, bank in enumerate(outs):
                                r = resid[:, t, column * 512:(column + 1) * 512]
                                added = dve(lambda e, r=r, b=bank: e.tensor_tensor(r, b.ap[:, :], r, ALU.add), made)
                                bank.free = (added,)
                            done[:] = [added]
                            yield
            return steps(), done

        def swiglu(n_tiles, src, ready):
            silus, hidden = scratch[1], scratch[0]
            hidden_read = {}

            def up(f):
                bank = next_bank()
                pe.wait(*bank.free)
                for j in range(2):
                    chunk, split_done = splitter.take(True)
                    w = Split(*(x.rearrange("p (t n) -> p t n", t=DT) for x in (chunk.hi, chunk.lo)))
                    pe.wait(split_done)
                    for k in range(DT):
                        pe.wait(ready[k])
                        three_passes(bank.ap[:, j * T:(j + 1) * T], w[:, k, :], src[:, k, :], k == 0, k == DT - 1)
                    both = signalled()
                    splitter.use(both)
                s = silus[:, (f % 4) * T:(f % 4 + 1) * T]
                h = hidden[:, (f % 4) * T:(f % 4 + 1) * T]
                split_h = hidden_split[:, f % 2, :]
                silu = act(lambda e: e.activation(s, bank.ap[:, 0:T], ACT.Silu), both)
                product = dve(lambda e: e.tensor_tensor(h, s, bank.ap[:, T:2 * T], ALU.mult), silu)
                bank.free = (product,)
                free = [hidden_read[f - 2]] if f >= 2 else []
                hi = act(lambda e: e.activation(split_h.hi, h, ACT.Copy), product, *free)
                return dve(lambda e: e.tensor_tensor(split_h.lo, h, split_h.hi.bitcast(F32), ALU.subtract), hi)

            def down(f, hidden_ready):
                chunk, split_done = splitter.take(False)
                pe.wait(hidden_ready, split_done)
                if f == 0:
                    for bank in y_banks:
                        pe.wait(*bank.free)
                for t in range(TT):
                    for half in range(2):
                        three_passes(y_banks[2 * t + half].ap[:, :], hidden_split[:, f % 2, t * P:(t + 1) * P],
                                     chunk[:, half * 512:(half + 1) * 512], f == 0, f == n_tiles - 1)
                hidden_read[f] = signalled()
                splitter.use(hidden_read[f])

            for f in range(n_tiles):
                ready_now = up(f)
                if f:
                    down(f - 1, ready_before)
                ready_before = ready_now
            down(n_tiles - 1, ready_before)
            return hidden_read[n_tiles - 1]

        def add_y(done, scale):
            tile_done = []
            for t in range(TT):
                for half in range(2):
                    r = resid[:, t, half * 512:(half + 1) * 512]
                    b = y_banks[2 * t + half]
                    added = dve(lambda e, r=r, b=b: e.scalar_tensor_tensor(r, b.ap[:, :], scale, r, ALU.mult,
                                                                           ALU.add), done)
                    b.free = (added,)
                tile_done.append(added)
            return tile_done

        class Heads:

            def __init__(self, scores, values, scale, probs, probs_T, free, score_banks, turn_bank,
                         log_count=None):
                self.scores, self.values, self.scale, self.log_count = scores, values, scale, log_count
                self.probs, self.probs_T = probs, probs_T
                self.probs_free, self.probs_T_free = [free, free], [free, free]
                self.score_banks, self.turn_bank = score_banks, turn_bank
                self.scored, self.inverse, self.turned = {}, {}, {}

            def score(self, h):
                bank = self.score_banks[h % 2]
                pe.wait(*bank.free)
                self.scored[h] = self.scores(h, bank.ap)

            def exponentials(self, h):
                bank, done = self.score_banks[h % 2], self.scored[h]
                p, scale, free = self.probs[h % 2], self.scale, self.probs_free[h % 2]
                top = stats[:, 8 + 4 * (h % 2):10 + 4 * (h % 2)]
                den = stats[:, 10 + 4 * (h % 2):12 + 4 * (h % 2)]
                if self.log_count is not None:
                    done = dve(lambda e: e.scalar_tensor_tensor(p, bank.ap[:, :], self.scale, self.log_count,
                                                                ALU.mult, ALU.add), done, *free)
                    bank.free = (done,)
                    source, scale = p, 1.0
                else:
                    source = bank.ap[:, :]
                largest = dve(lambda e: e.tensor_reduce(top, tiles(source), AX.X, ALU.max, negate=True), done, *free)
                if scale != 1.0:
                    largest = dve(lambda e: e.tensor_scalar(top, top, scale, None, ALU.mult), largest)
                for t in range(TT):
                    ex = act(lambda e, t=t: e.activation(p[:, t * T:(t + 1) * T], source[:, t * T:(t + 1) * T],
                                                         ACT.Exp, bias=top[:, t:t + 1], scale=scale,
                                                         accum_out=den[:, t:t + 1]), largest)
                if self.log_count is None:
                    bank.free = (ex,)
                self.inverse[h] = (den, ex)

            def divide(self, h):
                p, (den, ex) = self.probs[h % 2], self.inverse[h]
                inv = dve(lambda e: e.reciprocal(den, den), ex)
                self.inverse[h] = dve(lambda e: e.tensor_tensor(
                    tiles(p), tiles(p), den.unsqueeze(2).broadcast_to([P, TT, T]), ALU.mult), inv)

            def turn(self, h):
                bank = self.turn_bank(h)
                pe.wait(self.inverse[h], *bank.free)
                for kt in range(TT):
                    for t in range(TT):
                        turned = pe(lambda e, kt=kt, t=t: e.transpose(
                            bank.ap[:, kt * T + t * P:kt * T + (t + 1) * P],
                            self.probs[h % 2][:, t * T + kt * P:t * T + (kt + 1) * P], ident))
                self.probs_free[h % 2] = (turned,)
                self.turned[h] = act(lambda e: e.activation(self.probs_T[h % 2], bank.ap[:, :], ACT.Copy), turned,
                                     *self.probs_T_free[h % 2])
                bank.free = (self.turned[h],)

            def value(self, h):
                pe.wait(self.turned[h])
                self.probs_T_free[h % 2] = (self.values(h, tiles(self.probs_T[h % 2])),)

        def in_turn(heads, n, last):
            heads.score(0)
            heads.exponentials(0)
            heads.score(1)
            for h in range(n):
                heads.divide(h)
                if h + 1 < n:
                    heads.exponentials(h + 1)
                if h + 2 < n:
                    heads.score(h + 2)
                if h + 1 == n:
                    last()
                heads.turn(h)
                if h > 0:
                    heads.value(h - 1)
                yield
            heads.value(n - 1)
            yield

        def linear_attention(dk, n_q, q_ready, v_ready, gate_ready, norm_gain, b, arg, factors, between, out_banks, q_at=0,
                             after=lambda: None):
            n = n_q * T
            q = q_T[:, q_at:q_at + n_q, :].rearrange("p a b -> p (a b)")
            k = k_T[:, q_at:q_at + n_q, :].rearrange("p a b -> p (a b)")
            got_by, arg_free = {}, ()

            def scores(xq, xk, ready, level):
                blocks = [(0, 0, 0), (1, 1, 1)] if level <= LEVELS else [(2, 0, 1)]
                filled = []
                for target, jt, it in blocks:
                    bank = next_bank()
                    pe.wait(*ready, *bank.free)
                    for n_h, h in enumerate(sorted(range(LIN_HEADS), key=lambda h: h * dk % P)):
                        tile, part = h * dk // P, h * dk % P
                        if part and n_h == LIN_HEADS // 2:
                            pe.wait(pe.last)
                        done = pe(lambda e, h=h, tile=tile, part=part, jt=jt, it=it, bk=bank: e.matmul(
                            bk.ap[:, h * P:(h + 1) * P],
                            xk[part:part + dk, tile * T + jt * P:tile * T + (jt + 1) * P],
                            xq[part:part + dk, tile * T + it * P:tile * T + (it + 1) * P],
                            start=True, stop=True))
                    filled.append((target, bank, done))

                def collect():
                    for target, bank, done in filled:
                        dst = attn[:, target, :].rearrange("p (h i) -> p h i", h=LIN_HEADS)
                        src = bank.ap[:, :].rearrange("p (h i) -> p h i", h=LIN_HEADS)
                        if level <= LEVELS:
                            mask = const("levels")[:, level * P:(level + 1) * P].unsqueeze(1)\
                                .broadcast_to([P, LIN_HEADS, P])
                        if level == 0:
                            got = dve(lambda e, d=dst, s=src, m=mask: e.tensor_tensor(d, s, m, ALU.mult), done)
                        elif level <= LEVELS:
                            got = dve(lambda e, d=dst, s=src, m=mask: e.copy_predicated(d, m.bitcast(U32), s),
                                      done, got_by[target])
                        else:
                            got = dve(lambda e, d=dst, s=src: e.tensor_copy(d, s), done)
                        got_by[target] = got
                        bank.free = (got,)
                return collect, done

            def exponents(level, arg_free):
                half = 1 << (level - 1)
                if level <= LEVELS - 1:
                    split = lambda x: x.rearrange("p (m s) -> p m s", s=2 * half)
                    first = lambda x: split(x)[:, :, 0:half]
                    later = lambda x: split(x)[:, :, half:2 * half]
                    mid = split(b)[:, :, half - 1:half].broadcast_to([P, n // (2 * half), half])
                    dve(lambda e: e.tensor_tensor(first(arg), mid, first(b), ALU.subtract), *q_ready, *arg_free)
                    last = dve(lambda e: e.tensor_tensor(later(arg), later(b), mid, ALU.subtract))
                elif level == LEVELS:
                    split = lambda x: x.rearrange("p (m s) -> p m s", s=2 * SEG)
                    first = lambda x: split(x)[:, :, 0:SEG]
                    later = lambda x: split(x)[:, :, SEG:2 * SEG]
                    end = first(b)[:, :, SEG - 1:SEG].broadcast_to([P, n // (2 * SEG), SEG])
                    dve(lambda e: e.tensor_tensor(first(arg), end, first(b), ALU.subtract), *arg_free)
                    last = dve(lambda e: e.tensor_copy(later(arg), later(b)))
                else:
                    seg = lambda x: x.rearrange("p (m c s) -> p m c s", c=4, s=SEG)
                    split = lambda x: x.rearrange("p (m s) -> p m s", s=T)
                    first = lambda x: split(x)[:, :, 0:P]
                    later = lambda x: split(x)[:, :, P:T]
                    total = lambda c: seg(b)[:, :, c, SEG - 1:SEG].broadcast_to([P, n_q, SEG])
                    t0 = dve(lambda e: e.tensor_tensor(seg(arg)[:, :, 0, :], total(0), seg(b)[:, :, 0, :],
                                                       ALU.subtract), *arg_free)
                    dve(lambda e: e.tensor_tensor(seg(arg)[:, :, 0, :], seg(arg)[:, :, 0, :], total(1), ALU.add),
                        t0)
                    dve(lambda e: e.tensor_tensor(seg(arg)[:, :, 1, :], total(1), seg(b)[:, :, 1, :],
                                                  ALU.subtract))
                    dve(lambda e: e.tensor_copy(seg(arg)[:, :, 2, :], seg(b)[:, :, 2, :]))
                    last = dve(lambda e: e.tensor_tensor(seg(arg)[:, :, 3, :], seg(b)[:, :, 3, :], total(2),
                                                         ALU.add))
                return first, later, last

            def factors_of(level, arg_free):
                xq, xk, free = factors[level % 2]
                first, later, last = exponents(level, arg_free)
                ex = act(lambda e: e.activation(arg, arg, ACT.Exp), last)
                if waiting:
                    waiting.pop(0)()
                free = scored[level - 2] if level > 2 else free
                r1 = dve(lambda e: e.tensor_tensor(later(xq), later(q), later(arg), ALU.mult), ex, *free)
                r2 = pool(lambda e: e.tensor_tensor(first(xk), first(k), first(arg), ALU.mult), ex, *free)
                return r1, r2

            waiting, scored = [], {}
            factors_ready = factors_of(1, ())
            collect, _ = scores(q, k, q_ready, 0)
            waiting.append(collect)
            between(0)
            for level in range(1, LEVELS + 2):
                if level <= LEVELS:
                    next_ready = factors_of(level + 1, factors_ready)
                collect, done = scores(*factors[level % 2][0:2], factors_ready, level)
                scored[level] = (done,)
                waiting.append(collect)
                factors_ready = next_ready
                between(level)
            for collect in waiting:
                collect()

            v = v_tok
            outs = []
            for t, bank in enumerate(out_banks):
                pe.wait(*got_by.values(), *v_ready, *bank.free)
                for h in range(LIN_HEADS):
                    pieces = [(0, 0)] if t == 0 else [(2, 0), (1, 1)]
                    for i, (block, jt) in enumerate(pieces):
                        done = pe(lambda e, h=h, block=block, jt=jt, i=i, last=len(pieces) - 1, bk=bank: e.matmul(
                            bk.ap[:, h * P:(h + 1) * P], attn[:, block, h * P:(h + 1) * P],
                            v[:, jt, h * LIN_DV:(h + 1) * LIN_DV], start=(i == 0),
                            stop=(i == last)))
                outs.append((bank, done))
            s = stats[:, 16:16 + TT * LIN_HEADS]
            squares, gated_o = (x[:, 0:TT * 512].rearrange("p (t n) -> p t n", t=TT)
                                for x in (scratch[2], scratch[3]))
            for t, (bank, done) in enumerate(outs):
                square = act(lambda e, t=t, bk=bank: e.activation(squares[:, t, :], bk.ap[:, :], ACT.Square), done)
                gated = dve(lambda e, t=t, bk=bank: e.tensor_tensor(gated_o[:, t, :], bk.ap[:, :],
                                                                    gate_tok[:, t, :], ALU.mult),
                            square, *gate_ready)
                bank.free = (gated,)
                summed = dve(lambda e, t=t: e.tensor_reduce(
                    s[:, t * LIN_HEADS:(t + 1) * LIN_HEADS],
                    squares[:, t, :].rearrange("p (h v) -> p h v", h=LIN_HEADS), AX.X, ALU.add), square)
            mean = dve(lambda e: e.tensor_scalar(s, s, 1.0 / LIN_DV, EPS, ALU.mult, ALU.add), summed)
            inverse = dve(lambda e: e.reciprocal(s, s), mean)
            rms = act(lambda e: e.activation(s, s, ACT.Sqrt), inverse)
            for t in range(TT):
                o = gated_o[:, t, :].rearrange("p (h v) -> p h v", h=LIN_HEADS)
                r = s[:, t * LIN_HEADS:(t + 1) * LIN_HEADS].unsqueeze(2).broadcast_to([P, LIN_HEADS, LIN_DV])
                scaled = dve(lambda e, o=o, r=r: e.tensor_tensor(o, o, r, ALU.mult), rms)
            after()
            return to_features(gated_o, mix_T, norm_gain, (scaled,), n_tiles=4)

        def log_sigmoid(z, tmp, ready):
            t1 = act(lambda e: e.activation(tmp, z, ACT.Abs), *ready)
            t2 = act(lambda e: e.activation(tmp, tmp, ACT.Exp, scale=-1.0), t1)
            t3 = act(lambda e: e.activation(tmp, tmp, ACT.Ln, bias=1.0), t2)
            return t3, lambda dst: dve(lambda e: e.scalar_tensor_tensor(dst, z, 0.0, tmp, ALU.min, ALU.subtract),
                                       t3)

        def running_sum(values, dst, n, ready):
            for at in range(0, n, T):
                done = dve(lambda e, at=at: e.tensor_tensor_scan(dst[:, at:at + T], const("keep"),
                                                                 values[:, at:at + T], 0.0, ALU.mult, ALU.add),
                           ready)
            return done

        dve(lambda e: e.memset(ones, 1.0))
        for x in (scratch[2][:, 0:2 * T], scratch[3][:, 0:2 * T], q_T[:, 6:8, :], k_T[:, 6:8, :]):
            factors_cleared = pool(lambda e, x=x: e.memset(x, 0.0))
        plan_ready = []
        memory_ready = {}

        w_in, at = a["w_in"][0], GLR_AT + LOWRANK
        order = both_chunks(column_units(w_in, 0, 512) + row_units(w_in, 512, 1536)
                            + column_units(w_in, at, at + 1024) + row_units(w_in, at + 1024, at + 1536)
                            + output_units(a["w_out"][0], (0, 1))) + expert_chunks(a["expert_w1"][0], a["expert_w3"][0],
                                                                              a["expert_w2"][0])
        for layer in range(LAYERS):
            w_in = a["w_in_2"][layer]
            order += swiglu_chunks(*(a[f"ffn1_{w}_2"][layer] for w in ("w1", "w3", "w2")))
            order += both_chunks(column_units(w_in, 512, 1024) + column_units(w_in, 2048, 2560)
                                 + column_units(w_in, 0, 512)
                                 + row_units(w_in, 1024, 2048)
                                 + output_units(a["w_out_2"][layer], (1, 0))
                                 + column_units(a["xa_wkv_2"][layer], 0, D)
                                 + row_units(a["xa_wkv_2"][layer], D, 2 * D)
                                 + column_units(a["xa_wq_2"][layer], 0, D)
                                 + output_units(a["xa_wo_2"][layer], (0, 1)))
            order += swiglu_chunks(*(a[f"ffn2_{w}_2"][layer] for w in ("w1", "w3", "w2")))
        splitter = Splitter(stream, act, dve, pool, chunks, order)

        def gla_and_attention():
            n_T = norm_to_features(resid, normed, vector("norm1_g"), (have_x, have_small))
            rounded = act(lambda e: e.activation(small_split.hi[:, :, :], w_small[:, :, :], ACT.Copy), have_rest)
            small_ready = dve(lambda e: e.tensor_tensor(small_split.lo[:, :, :], w_small[:, :, :],
                                                        small_split.hi[:, :, :].bitcast(F32), ALU.subtract), rounded)
            def q_and_k(pair, bank, done):
                dst = (q_T if pair == 0 else k_T)[:, 4:6, :].rearrange("p a b -> p (a b)")
                return act(lambda e: e.activation(dst, bank[:, :], ACT.Copy,
                                                  scale=GLA_DK ** -0.5 if pair == 0 else 1.0), done)
            qk_list = []
            qk_steps = features_in_steps(4, normed, n_T, q_and_k, lambda pair: y_banks[2 + pair], qk_list)
            bank = next_bank()
            pe.wait(*n_T, small_ready, *bank.free)
            for t in range(TT):
                for k in range(DT):
                    three_passes(bank.ap[:, t * LOWRANK:(t + 1) * LOWRANK], normed[:, k, t * P:(t + 1) * P],
                                 w_lowrank[:, k, :], k == 0, k == DT - 1)
            low = signalled()
            low_tok = scratch[3][:, 0:TT * LOWRANK]
            low = dve(lambda e, b=bank: e.tensor_copy(low_tok, b.ap[:, 0:TT * LOWRANK]), low, factors_cleared)
            bank.free = (low,)
            next(qk_steps)
            bank = next_bank()
            pe.wait(low, *bank.free)
            for t in range(TT):
                low = pe(lambda e, t=t, b=bank: e.transpose(b.ap[0:LOWRANK, t * P:(t + 1) * P],
                                                            low_tok[:, t * LOWRANK:(t + 1) * LOWRANK], ident))
            low = act(lambda e, b=bank: e.activation(lowrank_T[:, :], b.ap[0:LOWRANK, 0:T], ACT.Copy), low)
            bank.free = (low,)
            next(qk_steps)
            bank = next_bank()
            pe.wait(low, *bank.free)
            for j in range(2):
                made = pe(lambda e, j=j, b=bank: e.matmul(b.ap[:, j * T:(j + 1) * T],
                                                          gate_w2[:, j * P:(j + 1) * P], lowrank_T[:, :],
                                                          start=True, stop=True))
            z = scratch[1][:, 0:2 * T]
            for j in range(2):
                zed = dve(lambda e, j=j, b=bank: e.tensor_scalar(
                    z[:, j * T:(j + 1) * T], b.ap[:, j * T:(j + 1) * T], vector("gla_gate_b")[:, j:j + 1], None,
                    ALU.add), made)
            bank.free = (zed,)
            _, finish = log_sigmoid(z, scratch[2][:, 0:2 * T], (zed,))
            la = finish(scratch[1][:, 0:2 * T])
            la = dve(lambda e: e.tensor_scalar(z, z, 1.0 / GLA_TAU, None, ALU.mult), la)
            b_ready = running_sum(z, scratch[0][:, 0:2 * T], 2 * T, la)

            for _ in qk_steps:
                pass
            qk = qk_list[0]
            v, gate, aq, ak, av = [], [], [], [], []
            fill = chain(
                tokens_in_steps(normed, n_T, act_copy(lambda t: v_tok[:, t, 0:512]), y_banks[0:2], v),
                tokens_in_steps(normed, n_T, act_copy(lambda t: gate_tok[:, t, :], func=ACT.Silu), y_banks[2:4],
                                gate),
                features_in_steps(4, normed, n_T, act_copy(pair_of(q_T)), lambda pair: y_banks[pair], aq),
                features_in_steps(4, normed, n_T, dve_copy(pair_of(k_T)), lambda pair: y_banks[2 + pair], ak),
                tokens_in_steps(normed, n_T, act_copy(lambda t: v_tok[:, t, 512:D]), y_banks[0:2], av))

            for _ in range(4):
                next(fill)

            def between(level):
                for _ in range(2 if level <= LEVELS else len(order)):
                    if next(fill, "empty") == "empty":
                        break
            flat = lambda x: x.rearrange("p a b -> p (a b)")
            mix_ready = [None] * DT
            projection, done = projection_in_steps(mix_T, mix_ready, (0, 1))
            banks_of = {}

            def scores(h, bank):
                tile, part = h // 2, (h % 2) * ATT_HD
                pe.wait(aq[0], ak[0])
                for t in range(TT):
                    scored = pe(lambda e, t=t: e.matmul(
                        bank[:, t * T:(t + 1) * T], q_T[part:part + ATT_HD, tile, t * P:(t + 1) * P],
                        k_T[part:part + ATT_HD, tile, :], start=True, stop=True))
                return scored

            def values(h, pt):
                part = (h % 2) * ATT_HD
                if h % 2 == 0:
                    banks_of[h // 2] = y_banks[h // 2 % 2] if h // 2 < ATT_HEADS // 2 - 1 else loose[0]
                    pe.wait(*banks_of[h // 2].free)
                bank = banks_of[h // 2]
                pe.wait(*av)
                for jt in range(TT):
                    done = pe(lambda e, jt=jt: e.matmul(
                        bank.ap[part:part + ATT_HD, 0:T], v_tok[:, jt, 512 + h * ATT_HD:512 + (h + 1) * ATT_HD],
                        pt[:, jt, :], start=(jt == 0), stop=(jt == TT - 1)))
                if h % 2:
                    put = put_split(done, (mix_T[:, 4 + h // 2, :], bank.ap[:, 0:T], 1.0))
                    bank.free = (put,)
                    mix_ready[4 + h // 2] = put
                return done

            heads = []

            def after():
                attention = Heads(scores, values, ATT_HD ** -0.5, *([x[:, 512 * i:512 * (i + 1)] for i in range(2)]
                                                                    for x in scratch[0:2]),
                                  (pe.last, dve.last, pool.last), y_banks[2:4], lambda h: loose[2 + h % 2],
                                  const("log_count"))
                heads.append(in_turn(attention, ATT_HEADS, lambda: [next(projection) for _ in range(4)]))
                for _ in range(4):
                    next(heads[0])
            mix_ready[0:4] = linear_attention(
                GLA_DK, 2, (qk, b_ready), v, gate, vector("gla_norm_g").broadcast_to([P, 4]),
                scratch[0][:, 0:2 * T], scratch[1][:, 0:2 * T],
                [(scratch[2][:, 0:2 * T], scratch[3][:, 0:2 * T], (factors_cleared, b_ready)),
                 (flat(q_T[:, 6:8, :]), flat(k_T[:, 6:8, :]), (factors_cleared,))],
                between, loose[0:2], q_at=4, after=after)
            for _ in heads[0]:
                pass
            for _ in projection:
                pass
            return done

        def route_tokens(n_T):
            for t in range(TT):
                bank = next_bank()
                pe.wait(*n_T, *bank.free)
                for k in range(DT):
                    three_passes(bank.ap[:, 0:N_LOGITS], normed[:, k, t * P:(t + 1) * P], w_router[:, k, :],
                                 k == 0, k == DT - 1)
                done = signalled()
                r = route[:, t * 128:(t + 1) * 128]
                logits, group8, top8, hot = r[:, 0:36], r[:, 36:44], r[:, 44:52], r[:, 52:56]
                spread, top2, pick1, pick2, one = r[:, 56:88], r[:, 88:96], r[:, 96:104], r[:, 104:112], r[:, 112:128]
                bias = logit_bias[:, :]
                g = gates[:, t, :].rearrange("p (g e) -> p g e", g=N_GROUPS)
                experts = logits[:, N_GROUPS:].rearrange("p (g e) -> p g e", g=N_GROUPS)
                sp3 = spread.rearrange("p (g e) -> p g e", g=N_GROUPS)
                index = const("index")[:, 0:PER_GROUP]
                pk = picks[:, t * 8:(t + 1) * 8]

                def step(make, *more):
                    return dve(make, dve.last, *more)

                read = dve(lambda e, b=bank, l=logits, bi=bias: e.tensor_tensor(l, b.ap[:, 0:N_LOGITS], bi,
                                                                               ALU.add), done)
                bank.free = (read,)
                step(lambda e, x=group8: e.memset(x, -3.0e38))
                step(lambda e, x=group8, l=logits: e.tensor_copy(x[:, 0:N_GROUPS], l[:, 0:N_GROUPS]))
                step(lambda e, o=top8, x=group8: e.max(o, x))
                step(lambda e, o=pk, m=top8, x=group8: e.max_index(o, m, x))
                step(lambda e, o=one, x=pk: e.tensor_copy(o[:, 0:8], x))
                step(lambda e, o=hot, x=one, i=index: e.tensor_scalar(o, i[:, 0:N_GROUPS], x[:, 0:1], None,
                                                                      ALU.is_equal))
                neg = step(lambda e, o=one, m=top8: e.tensor_scalar(o[:, 8:9], m[:, 0:1], -1.0, None, ALU.mult))
                ex = act(lambda e, o=one, l=logits, s=spread: e.activation(
                    s[:, 0:N_GROUPS], l[:, 0:N_GROUPS], ACT.Exp, bias=o[:, 8:9], accum_out=o[:, 9:10]), neg)
                step(lambda e, o=one: e.reciprocal(o[:, 10:11], o[:, 9:10]), ex)
                step(lambda e, o=sp3, x=experts, hh=hot: e.tensor_tensor(
                    o, x, hh.unsqueeze(2).broadcast_to([P, N_GROUPS, PER_GROUP]), ALU.mult))
                step(lambda e, o=group8, s=sp3: e.tensor_reduce(o, s.rearrange("p g e -> p e g"), AX.X, ALU.add))
                step(lambda e, o=top2, x=group8: e.max(o, x))
                step(lambda e, o=pk, m=top2, x=group8: e.max_index(o, m, x))
                step(lambda e, o=one, x=pk: e.tensor_copy(o[:, 0:8], x))
                diff = step(lambda e, o=one, m=top2: e.tensor_tensor(o[:, 11:12], m[:, 1:2], m[:, 0:1],
                                                                     ALU.subtract))
                ex = act(lambda e, o=one: e.activation(o[:, 12:13], o[:, 11:12], ACT.Exp), diff)
                step(lambda e, o=one: e.tensor_scalar(o[:, 13:14], o[:, 12:13], 1.0, None, ALU.add), ex)
                step(lambda e, o=one: e.reciprocal(o[:, 14:15], o[:, 13:14]))
                step(lambda e, o=one: e.tensor_tensor(o[:, 14:15], o[:, 14:15], o[:, 10:11], ALU.mult))
                step(lambda e, o=one: e.tensor_tensor(o[:, 15:16], o[:, 14:15], o[:, 12:13], ALU.mult))
                step(lambda e, o=pick1, x=one, i=index: e.tensor_scalar(o, i, x[:, 0:1], x[:, 14:15],
                                                                        ALU.is_equal, ALU.mult))
                step(lambda e, o=pick2, x=one, i=index: e.tensor_scalar(o, i, x[:, 1:2], x[:, 15:16],
                                                                        ALU.is_equal, ALU.mult))
                step(lambda e, o=pick1, x=pick2: e.tensor_tensor(o, o, x, ALU.add))
                step(lambda e, o=pick2, x=one, i=index: e.tensor_scalar(o, i, x[:, 0:1], None, ALU.is_equal))
                step(lambda e, o=top2, x=one, i=index: e.tensor_scalar(o, i, x[:, 1:2], None, ALU.is_equal))
                step(lambda e, o=pick2, x=top2: e.tensor_tensor(o, o, x, ALU.add))
                step(lambda e, o=chosen[:, t, :].rearrange("p (g e) -> p g e", g=N_GROUPS), x=pick2, hh=hot:
                     e.tensor_tensor(o, x.unsqueeze(1).broadcast_to([P, N_GROUPS, PER_GROUP]),
                                     hh.unsqueeze(2).broadcast_to([P, N_GROUPS, PER_GROUP]), ALU.mult))
                last = step(lambda e, o=g, x=pick1, hh=hot: e.tensor_tensor(
                    o, x.unsqueeze(1).broadcast_to([P, N_GROUPS, PER_GROUP]),
                    hh.unsqueeze(2).broadcast_to([P, N_GROUPS, PER_GROUP]), ALU.mult))
            return last

        def plan_blocks(routed):
            before_me, index, number = const("before"), const("index"), const("partition")
            rank = next_bank()
            pe.wait(routed, *rank.free)
            for t in range(TT):
                pieces = [(before_me, 0)] if t == 0 else [(ones, 0), (before_me, 1)]
                for i, (which, jt) in enumerate(pieces):
                    ranked = pe(lambda e, t=t, i=i, w=which, jt=jt, n=len(pieces): e.matmul(
                        rank.ap[:, t * N_EXPERTS:(t + 1) * N_EXPERTS], w, chosen[:, jt, :],
                        start=(i == 0), stop=(i == n - 1)))
            for t in range(TT):
                counted = pe(lambda e, t=t: e.matmul(rank.ap[0:N_EXPERTS, 2 * N_EXPERTS:2 * N_EXPERTS + 1],
                                                     chosen[:, t, :], ones[:, 0:1], start=(t == 0),
                                                     stop=(t == TT - 1)))
            place = plan[:, 0:2 * N_EXPERTS].rearrange("p (t e) -> p t e", t=TT)
            by_expert = plan[0:N_EXPERTS, 64:128]
            count, more, tmp, start = (by_expert[:, i:i + 1] for i in range(4))
            placed = dve(lambda e: e.scalar_tensor_tensor(
                place, rank.ap[:, 0:2 * N_EXPERTS].rearrange("p (t e) -> p t e", t=TT), 1.0, chosen[:, :, :],
                ALU.add, ALU.mult), counted)
            dve(lambda e: e.tensor_scalar(slot_of[:, :, 0:N_EXPERTS], place, -1.0, None, ALU.add))
            dve(lambda e: e.tensor_copy(gate_of_block[:, :, 0:N_EXPERTS], gates[:, :, :]))
            read = dve(lambda e: e.tensor_copy(count, rank.ap[0:N_EXPERTS, 2 * N_EXPERTS:2 * N_EXPERTS + 1]))
            rank.free = (read,)
            dve(lambda e: e.tensor_scalar(more, count, float(SLOTS), None, ALU.is_gt))
            for k in range(2, T // SLOTS):
                dve(lambda e, k=k: e.tensor_scalar(tmp, count, float(k * SLOTS), None, ALU.is_gt))
                got = dve(lambda e: e.tensor_tensor(more, more, tmp, ALU.add))
            bank = next_bank()
            begun = pe(lambda e, b=bank: e.matmul(b.ap[0:N_EXPERTS, 0:1], before_me[0:N_EXPERTS, 0:N_EXPERTS], more,
                                                  start=True, stop=True), got, *bank.free)
            owns, shift, tmp7 = (plan[0:N_EXPERTS, 128 + 8 * i:128 + 8 * i + EXTRA] for i in range(3))
            back = dve(lambda e, b=bank: e.tensor_copy(start, b.ap[0:N_EXPERTS, 0:1]), begun)
            bank.free = (back,)
            dve(lambda e: e.tensor_scalar(shift, index[0:N_EXPERTS, 0:EXTRA], start, None, ALU.subtract))
            dve(lambda e: e.tensor_scalar(owns, shift, 0.0, None, ALU.is_ge))
            dve(lambda e: e.tensor_scalar(tmp7, shift, more, None, ALU.is_lt))
            dve(lambda e: e.tensor_tensor(owns, owns, tmp7, ALU.mult))
            dve(lambda e: e.tensor_scalar(shift, shift, 1.0, float(SLOTS), ALU.add, ALU.mult))
            owned = dve(lambda e: e.tensor_tensor(shift, shift, owns, ALU.mult))
            bank = next_bank()
            pe.wait(owned, *bank.free)
            for t in range(TT):
                turned = pe(lambda e, t=t, b=bank: e.transpose(b.ap[0:N_EXPERTS, t * P:(t + 1) * P], place[:, t, :],
                                                               ident))
            for t in range(TT):
                turned = pe(lambda e, t=t, b=bank: e.transpose(b.ap[0:N_EXPERTS, T + t * P:T + (t + 1) * P],
                                                               gates[:, t, :], ident))
            both_T = work_T[0:N_EXPERTS, 0:2 * T]
            got = dve(lambda e, b=bank: e.tensor_copy(both_T, b.ap[0:N_EXPERTS, 0:2 * T]), turned)
            bank.free = (got,)
            bank = next_bank()
            pe.wait(got, *bank.free)
            for i in range(2 * TT):
                pe(lambda e, i=i, b=bank: e.matmul(b.ap[:, i * 8:i * 8 + EXTRA], both_T[:, i * P:(i + 1) * P], owns,
                                                   start=True, stop=True))
            pe(lambda e, b=bank: e.matmul(b.ap[:, 32:32 + EXTRA], ones[0:N_EXPERTS, :], shift, start=True,
                                          stop=True))
            pe(lambda e, b=bank: e.matmul(b.ap[0:1, 40:40 + EXTRA], number[0:N_EXPERTS, :], owns,
                                          start=True, stop=True))
            made = pe(lambda e, b=bank: e.matmul(b.ap[0:1, 40 + EXTRA:41 + EXTRA], ones[0:N_EXPERTS, 0:1], more,
                                                 start=True, stop=True))
            b = bank
            shifts = plan[:, 152:152 + EXTRA]
            dve(lambda e: e.tensor_scalar(shifts, b.ap[:, 32:32 + EXTRA], 1.0, None, ALU.add), made)
            for t in range(TT):
                dve(lambda e, t=t: e.tensor_tensor(slot_of[:, t, N_EXPERTS:], b.ap[:, t * 8:t * 8 + EXTRA], shifts,
                                                   ALU.subtract))
                dve(lambda e, t=t: e.tensor_copy(gate_of_block[:, t, N_EXPERTS:],
                                                 b.ap[:, (TT + t) * 8:(TT + t) * 8 + EXTRA]))
            done = dve(lambda e: e.tensor_copy(extra_expert[:, :], b.ap[0:1, 40:41 + EXTRA]))
            bank.free = (done,)
            return done

        def experts(before):
            n_T = norm_to_features(resid, normed, vector("norm2_g"), before)
            for t in range(TT):
                scaled = act(lambda e, t=t: e.activation(work[:, t, :], resid[:, t, :], ACT.Copy,
                                                         scale=stats[:, t:t + 1]))
                rounded = act(lambda e, t=t: e.activation(work_split.hi[:, t, :], work[:, t, :], ACT.Copy), scaled)
                work_ready = pool(lambda e, t=t: e.tensor_tensor(
                    work_split.lo[:, t, :], work[:, t, :], work_split.hi[:, t, :].bitcast(F32), ALU.subtract),
                    rounded)
            routed = route_tokens(n_T)
            planned = plan_blocks(routed)
            plan_ready.extend((planned, extra_expert))
            lower_bounds()
            gain = vector("norm2_g").unsqueeze(2).broadcast_to([P, DT, SLOTS])
            index = const("index")
            gather_bank, hidden_bank, out_banks = loose[0], loose[1], loose[2:4]
            w1, w3, w2 = a["expert_w1"][0], a["expert_w3"][0], a["expert_w2"][0]
            tokens_of = [q_T[:, 0:2, :], q_T[:, 2:4, :]]
            silu_of = [q_T[:, 4, :], q_T[:, 5, :]]
            hidden_of = [q_T[:, 6, :], q_T[:, 7, :]]
            hot_of = [scratch[2][:, 512 * i:512 * i + 256].rearrange("p (t s) -> p t s", t=TT) for i in range(2)]
            gated_of = [scratch[2][:, 512 * i + 256:512 * i + 512].rearrange("p (t s) -> p t s", t=TT)
                        for i in range(2)]
            back_of = [scratch[3][:, 256 * i:256 * i + 256] for i in range(2)]
            result_of = [v_tok[:, 0, :], v_tok[:, 1, :]]
            start_of = pe.last
            gathered, hot_ready, hidden_ready = {}, {}, {}
            hot_read, back_ready, back_read, result_ready = {}, {}, {}, {}

            def expert_weight(w, b, half):
                if b >= N_EXPERTS:
                    return w, b - N_EXPERTS, half
                return expert_half(w[b:b + 1], half)[:, 0]

            def size_of(pair):
                return 2 if 2 * pair + 1 < BLOCKS else 1

            def one_hot(pair):
                waits = [planned, start_of] + ([hot_read[pair - 2]] if pair >= 2 else [])
                hot = hot_split[pair % 2] if 2 * pair < N_EXPERTS else hot_of[pair % 2]
                for i in range(size_of(pair)):
                    b = 2 * pair + i
                    for t in range(TT):
                        s = slice(i * SLOTS, (i + 1) * SLOTS)
                        pool(lambda e, t=t, s=s, b=b: e.tensor_scalar(
                            hot[:, t, s], index[:, :], slot_of[:, t, b:b + 1], None, ALU.is_equal), *waits)
                        hot_ready[pair] = pool(lambda e, t=t, s=s, b=b: e.tensor_scalar(
                            gated_of[pair % 2][:, t, s], hot[:, t, s].bitcast(F32), gate_of_block[:, t, b:b + 1],
                            None, ALU.mult))

            def gather(b):
                pair, s = b // 2, slice(b % 2 * SLOTS, (b % 2 + 1) * SLOTS)
                pe.wait(hot_ready[pair], *gather_bank.free)
                for k in range(DT):
                    for t in range(TT):
                        done = pe(lambda e, k=k, t=t: e.matmul(
                            gather_bank.ap[:, k * SLOTS:(k + 1) * SLOTS], work[:, t, k * P:(k + 1) * P],
                            hot_of[pair % 2][:, t, s], start=(t == 0), stop=(t == TT - 1)))
                dst = tokens_of[b % 2].rearrange("p a b -> p (a b)").rearrange("p (k s) -> p k s", s=SLOTS)
                gathered[b] = dve(lambda e: e.tensor_tensor(
                    dst, gather_bank.ap[:, :].rearrange("p (k s) -> p k s", s=SLOTS), gain, ALU.mult), done)
                gather_bank.free = (gathered[b],)

            def up(b):
                x = tokens_of[b % 2].rearrange("p a b -> p (a b)").rearrange("p (k s) -> p k s", s=SLOTS)
                pe.wait(gathered[b], *hidden_bank.free)
                for i, w in enumerate((w1, w3)):
                    for f in range(D_EXPERT // P):
                        if f % 2 == 0:
                            unit, slot, arrived = stream.take(expert_weight(w, b, f // 2))
                            columns = slot[:, :].rearrange("p (t n) -> p t n", t=DT)
                            pe.wait(arrived)
                        for k in range(DT):
                            make = lambda e, i=i, f=f, k=k, w=columns: e.matmul(
                                hidden_bank.ap[:, i * 256 + f * SLOTS:i * 256 + (f + 1) * SLOTS],
                                w[:, k, f % 2 * P:(f % 2 + 1) * P], x[:, k, :], start=(k == 0), stop=(k == DT - 1))
                            if k == DT - 1:
                                done = pe(make)
                            else:
                                pe.quiet(make)
                        stream.released[unit] = (done,)
                s, h = silu_of[b % 2], hidden_of[b % 2]
                silu = act(lambda e: e.activation(s, hidden_bank.ap[:, 0:256], ACT.Silu), done)
                hidden_ready[b] = dve(lambda e: e.tensor_tensor(h, s, hidden_bank.ap[:, 256:512], ALU.mult), silu)
                hidden_bank.free = (hidden_ready[b],)

            def turn(pair, bank):
                n = size_of(pair) * SLOTS
                pe.wait(hot_ready[pair], *bank.free)
                for t in range(TT):
                    done = pe(lambda e, t=t: e.transpose(bank.ap[0:n, t * P:(t + 1) * P],
                                                         gated_of[pair % 2][:, t, 0:n], ident))
                hot_read[pair] = done
                waits = [back_read[pair - 2]] if pair >= 2 else []
                back_ready[pair] = act(lambda e: e.activation(back_of[pair % 2][0:n, :], bank.ap[0:n, 0:T],
                                                              ACT.Copy), done, *waits)
                bank.free = (back_ready[pair],)

            def empty_results(pair, out, n, done):
                waits = [back_read[pair - 2]] if pair >= 2 else []
                r = result_of[pair % 2]
                c0 = act(lambda e: e.activation(r[0:n, 0:512], out[0].ap[0:n, :], ACT.Copy), done, *waits)
                c1 = dve(lambda e: e.tensor_copy(r[0:n, 512:D], out[1].ap[0:n, :]), done, *waits)
                out[0].free, out[1].free = (c0,), (c1,)
                result_ready[pair] = (c0, c1)

            def down(b):
                pair, at = b // 2, b % 2 * SLOTS
                pe.wait(hidden_ready[b])
                if b % 2 == 0:
                    pe.wait(*out_banks[0].free, *out_banks[1].free)
                for f in range(D_EXPERT // P):
                    if f % 2 == 0:
                        unit, slot, arrived = stream.take(expert_weight(w2, b, f // 2))
                        pe.wait(arrived)
                    for half in range(2):
                        at_w = f % 2 * D + half * 512
                        done = pe(lambda e, f=f, half=half, w=slot[:, at_w:at_w + 512]: e.matmul(
                            out_banks[half].ap[at:at + SLOTS, :], hidden_of[b % 2][:, f * SLOTS:(f + 1) * SLOTS],
                            w, start=(f == 0), stop=(f == D_EXPERT // P - 1)))
                    stream.released[unit] = (done,)
                if b % 2 == 1 or b == BLOCKS - 1:
                    empty_results(pair, out_banks, at + SLOTS, done)

            def scatter(pair):
                n = size_of(pair) * SLOTS
                pe.wait(back_ready[pair], *result_ready[pair])
                if pair == 0:
                    for b in y_banks:
                        pe.wait(*b.free)
                for t in range(TT):
                    for half in range(2):
                        done = pe(lambda e, t=t, half=half: e.matmul(
                            y_banks[2 * t + half].ap[:, :], back_of[pair % 2][0:n, t * P:(t + 1) * P],
                            result_of[pair % 2][0:n, half * 512:(half + 1) * 512],
                            start=(pair == 0), stop=(2 * pair + 2 == N_EXPERTS or 2 * pair + 2 > BLOCKS),
                            skip_group_check=True))
                back_read[pair] = done
                return done

            x_pair = Split(*(x[:, 0:4, :].rearrange("p a b -> p (a b)").rearrange("p (k s) -> p k s", s=P)
                             for x in (normed.hi, normed.lo)))
            turned_hidden = [Split(*(x[:, 4 + 2 * i:6 + 2 * i, :].rearrange("p a b -> p (a b)")
                                     .rearrange("p (f s) -> p f s", s=P) for x in (normed.hi, normed.lo)))
                             for i in range(2)]
            slot_gate = [stats[:, 40 + i:41 + i] for i in range(2)]
            slot_gate_ready = {}
            x_plain, silu_pair, hidden_pair = scratch[1][:, 0:512], scratch[0][:, 0:512], scratch[0][:, 512:1024]
            for i in range(2):
                for x in (turned_hidden[i].hi, turned_hidden[i].lo):
                    other = x[:, :, (1 - i) * SLOTS:(2 - i) * SLOTS]
                    zeroed = dve(lambda e, o=other: e.memset(o.bitcast(F32), 0.0), start_of)
            pair_gathered, hidden_done, pair_hidden = {}, {}, {}
            wide_gain = vector("norm2_g").unsqueeze(2).broadcast_to([P, DT, P])

            def gather_pair(pair):
                for part in range(2):
                    bank = next_bank()
                    pe.wait(hot_ready[pair], work_ready, *bank.free)
                    for k in range(4 * part, 4 * part + 4):
                        for t in range(TT):
                            for i, w in enumerate((work_split.hi, work_split.lo)):
                                pe.quiet(lambda e, k=k, t=t, b=bank, i=i, w=w: e.matmul(
                                    b.ap[:, k % 4 * P:(k % 4 + 1) * P], w[:, t, k * P:(k + 1) * P],
                                    hot_split[pair % 2][:, t, :], start=(t == 0 and i == 0),
                                    stop=(t == TT - 1 and i == 1)))
                    done = signalled()
                    scaled = dve(lambda e, b=bank, part=part: e.tensor_tensor(
                        x_plain.rearrange("p (k s) -> p k s", s=P), b.ap[:, :].rearrange("p (k s) -> p k s", s=P),
                        wide_gain[:, 4 * part:4 * part + 4, :], ALU.mult), done)
                    bank.free = (scaled,)
                    x = x_pair[:, 4 * part:4 * part + 4, :]
                    plain = x_plain.rearrange("p (k s) -> p k s", s=P)
                    hi = act(lambda e, x=x: e.activation(x.hi, plain, ACT.Copy), scaled)
                    pair_gathered[pair] = dve(lambda e, x=x: e.tensor_tensor(
                        x.lo, plain, x.hi.bitcast(F32), ALU.subtract), hi)

            def up_split(b):
                rows = slice(b % 2 * SLOTS, (b % 2 + 1) * SLOTS)
                out = [next_bank(), next_bank()]
                pe.wait(pair_gathered[b // 2], zeroed)
                for bank in out:
                    pe.wait(*bank.free)
                    for part in range(DT // 2):
                        chunk, split_done = splitter.take(False)
                        pe.wait(split_done)
                        for j in range(2):
                            k = 2 * part + j
                            three_passes(bank.ap[:, :], x_pair[:, k, :], chunk[:, j * 512:(j + 1) * 512], k == 0,
                                         k == DT - 1)
                        done = signalled()
                        splitter.use(done)
                turned = [pair_hidden[b // 2 - 1]] if b >= 2 else []
                silu = act(lambda e: e.activation(silu_pair[rows, :], out[0].ap[rows, :], ACT.Silu), done, *turned)
                out[0].free = (silu,)
                hidden_done[b] = dve(lambda e: e.tensor_tensor(hidden_pair[rows, :], silu_pair[rows, :],
                                                               out[1].ap[rows, :], ALU.mult), silu)
                out[1].free = (hidden_done[b],)

            def turn_hidden(pair):
                bank = next_bank()
                pe.wait(hidden_done[2 * pair], hidden_done[2 * pair + 1], *bank.free)
                for f in range(D_EXPERT // P):
                    done = pe(lambda e, f=f: e.transpose(bank.ap[:, f * P:(f + 1) * P],
                                                         hidden_pair[:, f * P:(f + 1) * P], ident))
                source = bank.ap[:, :].rearrange("p (f s) -> p f s", s=P)
                pair_hidden[pair] = put_split(done, *(
                    (turned_hidden[i][:, :, i * SLOTS:(i + 1) * SLOTS], source[:, :, i * SLOTS:(i + 1) * SLOTS], 1.0)
                    for i in range(2)))
                bank.free = (pair_hidden[pair],)

            def down_pair(pair):
                out = [next_bank(), next_bank()]
                pe.wait(pair_hidden[pair], *out[0].free, *out[1].free)
                for i in range(2):
                    for f in range(D_EXPERT // P):
                        chunk, split_done = splitter.take(False)
                        pe.wait(split_done)
                        for half in range(2):
                            three_passes(out[half].ap[:, :], turned_hidden[i][:, f, :],
                                         chunk[:, half * 512:(half + 1) * 512], i == 0 and f == 0,
                                         i == 1 and f == D_EXPERT // P - 1)
                        done = signalled()
                        splitter.use(done)
                waits = [slot_gate_ready[pair]] + ([back_read[pair - 1]] if pair else [])
                gate = slot_gate[pair % 2]
                for half in range(2):
                    r = result_split[:, half * 512:(half + 1) * 512]
                    hi = act(lambda e, r=r, b=out[half]: e.activation(r.hi, b.ap[:, :], ACT.Copy, scale=gate), done,
                             *waits)
                    lo = dve(lambda e, r=r, b=out[half]: e.scalar_tensor_tensor(
                        r.lo, b.ap[:, :], gate, r.hi.bitcast(F32), ALU.mult, ALU.subtract), hi)
                    out[half].free = (lo,)
                result_ready[pair] = (lo,)

            def turn_hot(pair):
                bank = next_bank()
                pe.wait(hot_ready[pair], *bank.free)
                for t in range(TT):
                    pe(lambda e, t=t: e.transpose(bank.ap[:, t * P:(t + 1) * P],
                                                   hot_split[pair % 2][:, t, :].bitcast(F32), ident))
                for t in range(TT):
                    done = pe(lambda e, t=t: e.matmul(bank.ap[:, T:T + 1], gated_of[pair % 2][:, t, :], ones[:, 0:1],
                                                      start=(t == 0), stop=(t == TT - 1)))
                hot_read[pair] = done
                waits = [back_read[pair - 2]] if pair >= 2 else []
                back_ready[pair] = act(lambda e: e.activation(back_split[pair % 2], bank.ap[:, 0:T], ACT.Copy), done,
                                       *waits)
                slot_gate_ready[pair] = act(lambda e: e.activation(slot_gate[pair % 2], bank.ap[:, T:T + 1],
                                                                   ACT.Copy), done)
                bank.free = (slot_gate_ready[pair],)

            def scatter_pair(pair):
                pe.wait(back_ready[pair], *result_ready[pair])
                if pair == 0:
                    for b in y_banks:
                        pe.wait(*b.free)
                for t in range(TT):
                    for half in range(2):
                        for i, r in enumerate((result_split.hi, result_split.lo)):
                            pe.quiet(lambda e, t=t, half=half, i=i, r=r: e.matmul(
                                y_banks[2 * t + half].ap[:, :], back_split[pair % 2][:, t * P:(t + 1) * P],
                                r[:, half * 512:(half + 1) * 512], start=(pair == 0 and i == 0),
                                stop=(2 * pair + 2 == N_EXPERTS and i == 1), skip_group_check=True))
                back_read[pair] = signalled()

            def run_split(pairs):
                one_hot(0)
                gather_pair(0)
                for pair in range(pairs):
                    if pair + 1 < pairs:
                        one_hot(pair + 1)
                    up_split(2 * pair)
                    if pair > 1:
                        scatter_pair(pair - 2)
                    up_split(2 * pair + 1)
                    if pair + 1 < pairs:
                        gather_pair(pair + 1)
                    turn_hot(pair)
                    if pair:
                        down_pair(pair - 1)
                    turn_hidden(pair)
                scatter_pair(pairs - 2)
                down_pair(pairs - 1)
                scatter_pair(pairs - 1)

            def run(first, last):
                one_hot(first // 2)
                gather(first)
                for b in range(first, last):
                    if b % 2 == 0 and b + 2 < last:
                        one_hot(b // 2 + 1)
                    if b + 1 < last:
                        gather(b + 1)
                    up(b)
                    if b % 2 == 1:
                        turn(b // 2, gather_bank)
                        if b > first + 2:
                            scatter(b // 2 - 1)
                    if b > first:
                        down(b - 1)
                down(last - 1)
                if last % 2:
                    turn(last // 2, gather_bank)
                    scatter(last // 2 - 1)
                return scatter((last - 1) // 2)

            run_split(N_EXPERTS // 2)
            engines = (pe, act, dve, pool)
            for engine in engines:
                engine.wait(planned)
                engine.begin_branch()
            stream.branch = True
            y = run(N_EXPERTS, BLOCKS)
            stream.branch = False
            for engine in engines:
                engine.end_branch(extra_expert[0:1, EXTRA:EXTRA + 1])
            splitter.ahead()
            return add_y(y, 1.0)

        def load_gain(n, ready):
            act.wait(*ready)
            act.steps.append(lambda e: e.dma_start(gain_row, a["gain_rows"][n]).then_inc(gain_loaded, 16))
            return (gain_loaded, 16 * (n + 1))

        def norm_tokens(n, before, dst):
            loaded = load_gain(n, before)
            rms = inverse_rms(resid, 0, before, scratch[3])
            gain = gain_row
            dve.wait(loaded)
            return [dve(lambda e, t=t: e.scalar_tensor_tensor(dst[:, t, :], resid[:, t, :], stats[:, t:t + 1],
                                                              gain, ALU.mult, ALU.mult), rms) for t in range(TT)]

        def ffn(which, layer, before):
            n_T = norm_to_features(resid, normed, vector(f"{which}_norm_2", layer), before)
            y = swiglu(D_FF // P, normed, n_T)
            return add_y(y, 0.5)

        def lower_bounds():
            l0, l1 = vector("lb_logits_2", 0), vector("lb_logits_2", 1)
            top, e0, e1, d0, d1 = (lb[:, 4 * i:4 * i + 4] for i in range(2, 7))
            m = dve(lambda e: e.tensor_tensor(top, l0, l1, ALU.max), have_small)
            dve(lambda e: e.tensor_tensor(d0, l0, top, ALU.subtract), m)
            d = dve(lambda e: e.tensor_tensor(d1, l1, top, ALU.subtract))
            act(lambda e: e.activation(e0, d0, ACT.Exp), d)
            x = act(lambda e: e.activation(e1, d1, ACT.Exp))
            s = dve(lambda e: e.tensor_tensor(e0, e0, e1, ALU.add), x)
            ln = act(lambda e: e.activation(e0, e0, ACT.Ln), s)
            dve(lambda e: e.tensor_tensor(lb[:, 0:4], d1, e0, ALU.subtract), ln)
            return dve(lambda e: e.tensor_tensor(lb[:, 4:8], d0, e0, ALU.subtract))

        def hgrn_and_pool(layer, before):
            n_T = norm_to_features(resid, normed, vector("mix_norm_2", layer), before)
            loaded = (pool_w_loaded[layer], 16)
            act.wait(pe.last)
            act.steps.append(lambda e: e.dma_start(pool_w[:, :, :], a["pool_w_2"][layer].rearrange("g c d -> c g d"))
                             .then_inc(pool_w_loaded[layer], 16))
            z4, b = scratch[1][:, 0:4 * T], scratch[1][:, 0:4 * T]
            tmp, logf, km_of = gain_row, v_tok[:, 0, :], v_tok[:, 1, :]
            zed = features_out(4, normed, n_T, dve_copy(lambda pair: z4[:, pair * 512:(pair + 1) * 512]))
            _, finish = log_sigmoid(z4, tmp, (zed,))
            u, wa, wb = (x[:, :].rearrange("p (g t) -> p g t", g=4) for x in (scratch[0], scratch[2], scratch[3]))
            for x in (u, wa, wb):
                dve(lambda e, x=x: e.memset(x[:, :, 0:PAD], 0.0))
            up = features_out(4, normed, n_T, lambda pair, bank, done: dve(
                lambda e: e.tensor_copy(u[:, 2 * pair:2 * pair + 2, PAD:], bank[:, :].rearrange(
                    "p (a b) -> p a b", b=T)), done))
            lsz = finish(logf)
            km = dve(lambda e: e.tensor_tensor(km_of, logf, z4, ALU.subtract), lsz)
            k4 = k_T[:, 0:4, :].rearrange("p a b -> p (a b)")
            if layer == 0:
                keys = act(lambda e: e.activation(k4, km_of, ACT.Exp), km)
                b_ready = running_sum(logf, b, 4 * T, lsz)
            else:
                for j in range(4):
                    keys = act(lambda e, j=j: e.activation(k4[:, j * T:(j + 1) * T], km_of[:, j * T:(j + 1) * T],
                                                           ACT.Exp, bias=lb[:, 4 + j:5 + j]), km)
                larger = tmp
                for j in range(4):
                    c = slice(j * T, (j + 1) * T)
                    x1 = dve(lambda e, j=j, c=c: e.tensor_scalar(logf[:, c], logf[:, c], lb[:, 4 + j:5 + j], None,
                                                                 ALU.add), km)
                    dve(lambda e, j=j, c=c: e.tensor_scalar(larger[:, c], logf[:, c], lb[:, j:j + 1], None,
                                                            ALU.max), x1)
                    x2 = dve(lambda e, j=j, c=c: e.tensor_scalar(logf[:, c], logf[:, c], lb[:, j:j + 1], None,
                                                                 ALU.subtract))
                act(lambda e: e.activation(logf, logf, ACT.Abs), x2)
                act(lambda e: e.activation(logf, logf, ACT.Exp, scale=-1.0), act.last)
                ln = act(lambda e: e.activation(logf, logf, ACT.Ln, bias=1.0), act.last)

            def shifted(dst, src, g0, by, ready):
                return dve(lambda e: e.tensor_tensor(dst[:, g0:, PAD:], src[:, g0:, PAD:],
                                                     src[:, g0:, PAD - by:PAD + T - by], ALU.add), ready)
            last = shifted(wa, u, 0, 1, up)
            last = shifted(wb, wa, 1, 2, last)
            last = shifted(wa, wb, 2, 4, last)
            last = shifted(wb, wa, 3, 8, last)
            share = const("share").rearrange("p (g t) -> p g t", g=4)
            pooled = k_T[:, 4:8, :]
            for g in range(4):
                s = (wa, wb, wa, wb)[g]
                dve(lambda e, g=g, s=s: e.tensor_tensor(pooled[:, g, 0:PAD], s[:, g, PAD:2 * PAD], share[:, g, :],
                                                        ALU.mult), last)
                mean = dve(lambda e, g=g, s=s: e.tensor_scalar(pooled[:, g, PAD:], s[:, g, 2 * PAD:],
                                                               1.0 / POOL_WINDOWS[g], None, ALU.mult))
            less = dve(lambda e: e.tensor_tensor(pooled, pooled, u[:, :, PAD:], ALU.subtract), mean)
            if layer:
                whole = dve(lambda e: e.tensor_tensor(logf, logf, larger, ALU.add), ln)
                b_ready = running_sum(logf, b, 4 * T, whole)
            q = features_out(4, normed, n_T, act_copy(pair_of(q_T)))
            for pair in range(2):
                bank = next_bank()
                pe.wait(less, loaded, *bank.free)
                for j in range(2):
                    g = 2 * pair + j
                    made = pe(lambda e, g=g, j=j, b=bank: e.matmul(b.ap[:, j * T:(j + 1) * T], pool_w[:, g, :],
                                                                   pooled[:, g, :], start=True, stop=True))
                put = put_split(made, *((mix_T[:, 4 + g, :], bank.ap[:, g % 2 * T:(g % 2 + 1) * T],
                                         vector("pool_scale_2", layer)[:, g:g + 1])
                                        for g in (2 * pair, 2 * pair + 1)))
                bank.free = (put,)
            v, gate = [], []
            fill = chain(
                tokens_in_steps(normed, n_T, act_copy(lambda t: v_tok[:, t, 0:512], free=(b_ready,)), y_banks[0:2], v),
                tokens_in_steps(normed, n_T, act_copy(lambda t: gate_tok[:, t, :], func=ACT.Silu, free=(b_ready,)),
                                y_banks[2:4], gate))
            mix_ready = [None] * 4 + [put] * 4
            projection, done = projection_in_steps(mix_T, mix_ready, (1, 0))

            memory_scales = []

            def after():
                for _ in fill:
                    pass
                load_memory(layer)
                memory_scales.append(diagonals(mem_tok, ((mem_loaded[layer], 16),), 2,
                                               q_T[:, 0:4, :].rearrange("p a b -> p (a b)")))
                for _ in range(4):
                    next(projection)
            mix_ready[0:4] = linear_attention(
                HGRN_DK, 4, (q, keys, b_ready), v, gate, vector("hgrn_norm_2", layer), b, scratch[0][:, 0:4 * T],
                [(scratch[2][:, 0:4 * T], scratch[3][:, 0:4 * T], (less,)),
                 (q_T[:, 4:8, :].rearrange("p a b -> p (a b)"), k_T[:, 4:8, :].rearrange("p a b -> p (a b)"), (made,))],
                lambda level: next(fill, None), loose[0:2], after=after)
            scales, scaled = memory_scales[0]
            memory_ready[layer] = to_features(mem_tok, mem_T, vector("mem_norm_2", layer), (scaled,), scales=scales)
            for _ in projection:
                pass
            return done

        def load_memory(layer):
            act.wait(pe.last, dve.last, pool.last)
            act.steps.append(lambda e: e.dma_start(mem_tok, a["mem_2"][0].rearrange("(t p) n -> p t n", p=P))
                             .then_inc(mem_loaded[layer], 16))

        def cross_attention(layer, before):
            m_T = memory_ready[layer]
            k_ready = features_out(DT, mem_T, m_T, dve_copy(pair_of(k_T)))
            v_ready = []
            for i in range(2):
                fill = tokens_in_steps(mem_T, m_T, act_copy(lambda t, i=i: v_tok[:, t, 512 * i:512 * (i + 1)]),
                                       y_banks[2 * i:2 * i + 2], v_ready)
                if i == 0:
                    n_T = norm_to_features(resid, mix_T, vector("xa_norm_2", layer), before)
                for _ in fill:
                    pass
            q_ready = features_out(DT, mix_T, n_T, act_copy(pair_of(q_T)))
            mix_ready = [None] * DT
            projection, done = projection_in_steps(mix_T, mix_ready, (0, 1))

            def scores(h, bank):
                pe.wait(q_ready, k_ready)
                for t in range(TT):
                    for j in range(2):
                        scored = pe(lambda e, t=t, j=j: e.matmul(
                            bank[:, t * T:(t + 1) * T], q_T[:, 2 * h + j, t * P:(t + 1) * P], k_T[:, 2 * h + j, :],
                            start=(j == 0), stop=(j == 1)))
                return scored

            def values(h, pt):
                bank = next_bank()
                pe.wait(*v_ready, *bank.free)
                for j in range(2):
                    for mt in range(TT):
                        made = pe(lambda e, j=j, mt=mt: e.matmul(
                            bank.ap[:, j * T:(j + 1) * T],
                            v_tok[:, mt, h * XA_HD + j * P:h * XA_HD + (j + 1) * P], pt[:, mt, :],
                            start=(mt == 0), stop=(mt == TT - 1)))
                head = mix_T[:, 2 * h:2 * h + 2, :]
                put = put_split(made, (Split(*(x.rearrange("p a b -> p (a b)") for x in (head.hi, head.lo))),
                                       bank.ap[:, :], 1.0))
                bank.free = (put,)
                mix_ready[2 * h:2 * h + 2] = [put, put]
                return made

            attention = Heads(scores, values, XA_HD ** -0.5, *([x[:, 512 * i:512 * (i + 1)] for i in range(2)]
                                                               for x in (scratch[0], scratch[1])), (),
                              y_banks[0:2], lambda h: next_bank())
            for _ in in_turn(attention, XA_HEADS, lambda: [next(projection) for _ in range(4)]):
                pass
            for _ in projection:
                pass
            return done

        done = (have_x,)
        steps = [lambda d: gla_and_attention(), experts,
                 lambda d: norm_tokens(0, d, resid)[-1:]]
        for layer in range(LAYERS):
            steps += [lambda d, l=layer: ffn("ffn1", l, d), lambda d, l=layer: hgrn_and_pool(l, d),
                      lambda d, l=layer: cross_attention(l, d), lambda d, l=layer: ffn("ffn2", l, d)]
        for step in steps:
            done = step(done)
        done = norm_tokens(1, done, work)
        sp.wait(have_x)
        stream.plan(sp, *plan_ready)
        for t in range(TT):
            sp.wait(done[min(t, len(done) - 1)])
            sp.steps.append(lambda e, t=t: e.dma_start(out[0, t * P:(t + 1) * P, :], work[:, t, :])
                            .then_inc(stored, 16))
        sp.wait((stored, 16 * TT))

        block = ctx.enter_context(nc.Block())
        block.sync(sp.emit)
        block.scalar(act.emit)
        block.tensor(pe.emit)
        block.vector(dve.emit)
        block.gpsimd(pool.emit)


DIRECT = ["x", "w_in", "gla_gate_w2", "w_out", "router_group_w", "router_expert_w", "expert_w1", "expert_w3",
          "expert_w2", "mem_2", "ffn1_w1_2", "ffn1_w3_2", "ffn1_w2_2", "w_in_2", "pool_w_2", "w_out_2", "xa_wq_2",
          "xa_wkv_2", "xa_wo_2", "ffn2_w1_2", "ffn2_w3_2", "ffn2_w2_2"]


def kernel(**inputs):
    import concourse.bacc as bacc
    from concourse.bass_utils import run_bass_kernel_spmd

    nc = bacc.Bacc("TRN2", target_bir_lowering=False, num_devices=1)
    arrays = {name: np.ascontiguousarray(inputs[name]) for name in DIRECT}
    arrays["vectors"] = np.ascontiguousarray(
        np.concatenate([np.asarray(inputs[name]).reshape(-1, P) for name, _ in VECTORS]).T)
    bias = np.concatenate([np.asarray(inputs[name]).reshape(-1) for name in ("router_group_b", "router_expert_b")])
    arrays["logit_bias"] = np.ascontiguousarray(np.broadcast_to(bias, (P, bias.size)))
    gains = np.stack([np.asarray(inputs[name]) for name in ("final_norm_g", "final_norm_2")])
    arrays["gain_rows"] = np.ascontiguousarray(np.broadcast_to(gains[:, None, :], (2, P, D)))
    start, arrays["constants"] = shape_constants()
    a = {name: nc.dram_tensor(f"in_{name}", v.shape, mybir.dt.from_np(v.dtype), kind="ExternalInput").ap()
         for name, v in arrays.items()}
    a["constants_at"] = start
    out = nc.dram_tensor("out_0", (1, T, D), F32, kind="ExternalOutput").ap()
    build(nc, a, out)
    result = run_bass_kernel_spmd(nc, [{f"in_{name}": v for name, v in arrays.items()}], core_ids=[0])
    return result.results[0]["out_0"]
```
